# Optimizing a Trainium2 kernel written in Bass

```python
import jax, jax.numpy as jnp
from jax import lax
import numpy as np

D_MODEL = 1024
BATCH = 1
SEQ = 512
DEPTH = 1

SSM_WIDTH = D_MODEL // 2
SSM_GROUP = 16
SSM_GROUPS = SSM_WIDTH // SSM_GROUP
SSM_STATE = 64
NSA_HEADS = 8
NSA_KV_GROUPS = 2
HEADS_PER_GROUP = NSA_HEADS // NSA_KV_GROUPS
HEAD_DIM = 64
NSA_WIDTH = NSA_HEADS * HEAD_DIM
CMP_STRIDE = 16
CMP_BLOCK = 2 * CMP_STRIDE
CMP_HIDDEN = 2 * HEAD_DIM
SEL_BLOCK = 64
SEL_TOP_K = 16
WINDOW = 512
Q_BLOCK = 128
D_FF = 4 * D_MODEL
N_MIXERS = 2
KV_WIDTH = 3 * 2 * NSA_KV_GROUPS * HEAD_DIM
IN_WIDTH = SSM_WIDTH + NSA_WIDTH + KV_WIDTH + 3 * NSA_HEADS + N_MIXERS * D_MODEL
EPS = 1e-6
NEG_INF = -1e30
FORCE_BONUS = 1e4


def rmsnorm(x, g):
    xf = x.astype(jnp.float32)
    y = xf * lax.rsqrt(jnp.mean(xf * xf, axis=-1, keepdims=True) + EPS)
    return (y * g.astype(jnp.float32)).astype(x.dtype)

def masked_softmax(s, mask):
    s = jnp.where(mask, s.astype(jnp.float32), NEG_INF)
    p = jax.nn.softmax(s, axis=-1)
    return jnp.where(mask, p, 0.0)

def alibi_slopes():
    h = jnp.arange(1, NSA_HEADS + 1, dtype=jnp.float32)
    return jnp.exp2(-8.0 * h / NSA_HEADS).reshape(NSA_KV_GROUPS, HEADS_PER_GROUP, 1, 1)

def s5_mixer(u, a_re, a_im, log_dt, b_re, b_im, c_re, c_im, d_skip, w_glu, b_glu):
    bsz, s, _ = u.shape
    f32 = jnp.float32
    ug = u.astype(f32).reshape(bsz, s, SSM_GROUPS, SSM_GROUP)
    ar = a_re.astype(f32)
    ai = a_im.astype(f32)
    dt = jnp.exp(log_dt.astype(f32))[:, None]
    mag = jnp.exp(ar * dt)
    abar_re = mag * jnp.cos(ai * dt)
    abar_im = mag * jnp.sin(ai * dt)
    den = ar * ar + ai * ai
    nr = abar_re - 1.0
    fr = (nr * ar + abar_im * ai) / den
    fi = (abar_im * ar - nr * ai) / den
    br = b_re.astype(f32)
    bi = b_im.astype(f32)
    bbar_re = fr[..., None] * br - fi[..., None] * bi
    bbar_im = fr[..., None] * bi + fi[..., None] * br
    bu_re = jnp.einsum('bsgc,gpc->bsgp', ug, bbar_re)
    bu_im = jnp.einsum('bsgc,gpc->bsgp', ug, bbar_im)
    a_seq_re = jnp.broadcast_to(abar_re, (1, s, SSM_GROUPS, SSM_STATE))
    a_seq_im = jnp.broadcast_to(abar_im, (1, s, SSM_GROUPS, SSM_STATE))

    def combine(left, right):
        a1r, a1i, b1r, b1i = left
        a2r, a2i, b2r, b2i = right
        return (a2r * a1r - a2i * a1i, a2r * a1i + a2i * a1r,
                a2r * b1r - a2i * b1i + b2r, a2r * b1i + a2i * b1r + b2i)

    _, _, xr, xi = lax.associative_scan(combine, (a_seq_re, a_seq_im, bu_re, bu_im), axis=1)
    y = (jnp.einsum('bsgp,gcp->bsgc', xr, c_re.astype(f32))
         - jnp.einsum('bsgp,gcp->bsgc', xi, c_im.astype(f32))
         + d_skip.astype(f32).reshape(SSM_GROUPS, SSM_GROUP) * ug).reshape(bsz, s, SSM_WIDTH)
    yg = jax.nn.gelu(y)
    out = yg * jax.nn.sigmoid(yg @ w_glu.astype(f32) + b_glu.astype(f32))
    return out.astype(u.dtype)

def compress_blocks(tok, pe, w1, w2):
    bsz, g, s, d = tok.shape
    chunks = tok.reshape(bsz, g, s // CMP_STRIDE, CMP_STRIDE, d)
    blocks = jnp.concatenate([chunks[:, :, :-1], chunks[:, :, 1:]], axis=3) + pe
    flat = blocks.reshape(bsz, g, s // CMP_STRIDE - 1, CMP_BLOCK * d)
    return jax.nn.gelu(flat @ w1) @ w2

def nsa_mixer(q, kv, gate_logits, cmp_pe_k, cmp_pe_v, cmp_wk1, cmp_wk2, cmp_wv1, cmp_wv2,
              q_norm_g, k_norm_g):
    bsz, s, _ = q.shape
    G, HG, d = NSA_KV_GROUPS, HEADS_PER_GROUP, HEAD_DIM
    f32 = jnp.float32
    q = rmsnorm(q.reshape(bsz, s, G, HG, d), q_norm_g).transpose(0, 2, 3, 1, 4)
    kv = kv.reshape(bsz, s, 3, 2, G, d).transpose(2, 3, 0, 4, 1, 5)
    kc = rmsnorm(compress_blocks(kv[0, 0], cmp_pe_k, cmp_wk1, cmp_wk2), k_norm_g[0])
    vc = compress_blocks(kv[0, 1], cmp_pe_v, cmp_wv1, cmp_wv2)
    n_cmp = kc.shape[2]
    n_sel = s // SEL_BLOCK
    k_top = min(SEL_TOP_K, n_sel)
    ks = rmsnorm(kv[1, 0], k_norm_g[1]).reshape(bsz, G, n_sel, SEL_BLOCK, d)
    vs = kv[1, 1].reshape(bsz, G, n_sel, SEL_BLOCK, d)
    pad = ((0, 0), (0, 0), (WINDOW, 0), (0, 0))
    kw = jnp.pad(rmsnorm(kv[2, 0], k_norm_g[2]), pad)
    vw = jnp.pad(kv[2, 1], pad)
    gates = jax.nn.sigmoid(gate_logits.reshape(bsz, s, 3, G, HG).astype(f32))
    gates = gates.astype(q.dtype).transpose(0, 3, 4, 1, 2)
    slopes = alibi_slopes()
    scale = HEAD_DIM ** -0.5
    c_end = (jnp.arange(n_cmp) * CMP_STRIDE + CMP_BLOCK - 1).astype(f32)
    blk_ids = jnp.arange(n_sel)
    bi = jnp.arange(bsz)[:, None, None, None]
    gi = jnp.arange(G)[None, :, None, None]
    sel_off = jnp.arange(SEL_BLOCK)
    win_off = jnp.arange(Q_BLOCK + WINDOW)

    def query_block(i):
        qs = i * Q_BLOCK
        qb = lax.dynamic_slice_in_dim(q, qs, Q_BLOCK, axis=3)
        gb = lax.dynamic_slice_in_dim(gates, qs, Q_BLOCK, axis=3)
        t = qs + jnp.arange(Q_BLOCK)
        tf = t.astype(f32)
        dist_c = tf[:, None] - c_end[None, :]
        sc = jnp.einsum('bghqd,bgcd->bghqc', qb, kc).astype(f32) * scale - slopes * dist_c
        pc = masked_softmax(sc, dist_c >= 0)
        o_cmp = jnp.einsum('bghqc,bgcd->bghqd', pc.astype(vc.dtype), vc)
        imp = jnp.pad(pc.sum(axis=2), ((0, 0), (0, 0), (0, 0), (0, 1)))
        chunks = imp.reshape(bsz, G, Q_BLOCK, n_sel, SEL_BLOCK // CMP_STRIDE)
        prev = jnp.pad(chunks[..., :-1, -1], ((0, 0), (0, 0), (0, 0), (1, 0)))
        imp_sel = chunks.sum(axis=-1) + prev
        cur = t // SEL_BLOCK
        valid = blk_ids[None, :] <= cur[:, None]
        forced = ((blk_ids[None, :] == 0) | (blk_ids[None, :] == cur[:, None])
                  | (blk_ids[None, :] == cur[:, None] - 1))
        imp_sel = jnp.where(valid, imp_sel + jnp.where(forced, FORCE_BONUS, 0.0), NEG_INF)
        _, idx = lax.top_k(imp_sel, k_top)
        k_g = ks[bi, gi, idx].reshape(bsz, G, Q_BLOCK, k_top * SEL_BLOCK, d)
        v_g = vs[bi, gi, idx].reshape(bsz, G, Q_BLOCK, k_top * SEL_BLOCK, d)
        pos = (idx[..., None] * SEL_BLOCK + sel_off).reshape(bsz, G, Q_BLOCK, k_top * SEL_BLOCK)
        dist_s = (t[None, None, :, None] - pos).astype(f32)[:, :, None]
        ss = jnp.einsum('bghqd,bgqkd->bghqk', qb, k_g).astype(f32) * scale - slopes * dist_s
        ps = masked_softmax(ss, dist_s >= 0)
        o_slc = jnp.einsum('bghqk,bgqkd->bghqd', ps.astype(v_g.dtype), v_g)
        kwb = lax.dynamic_slice_in_dim(kw, qs, Q_BLOCK + WINDOW, axis=2)
        vwb = lax.dynamic_slice_in_dim(vw, qs, Q_BLOCK + WINDOW, axis=2)
        s_pos = qs - WINDOW + win_off
        dist_w = t[:, None] - s_pos[None, :]
        mask_w = (dist_w >= 0) & (dist_w < WINDOW) & (s_pos[None, :] >= 0)
        sw = jnp.einsum('bghqd,bgkd->bghqk', qb, kwb).astype(f32) * scale - slopes * dist_w.astype(f32)
        pw = masked_softmax(sw, mask_w)
        o_win = jnp.einsum('bghqk,bgkd->bghqd', pw.astype(vwb.dtype), vwb)
        return gb[..., 0:1] * o_cmp + gb[..., 1:2] * o_slc + gb[..., 2:3] * o_win

    out = lax.map(query_block, jnp.arange(s // Q_BLOCK))
    return out.transpose(1, 0, 4, 2, 3, 5).reshape(bsz, s, NSA_WIDTH)

def first_inputs(seed: int = 0) -> dict:
    key = jax.random.key(seed)
    ks = jax.random.split(key, 32)
    L = DEPTH
    f32 = jnp.float32

    def nrm(k, shape, scale):
        return jax.random.normal(k, shape, f32) * scale

    return {
        'x': nrm(ks[0], (BATCH, SEQ, D_MODEL), 1.0),
        'norm1_g': 1.0 + nrm(ks[1], (L, D_MODEL), 0.02),
        'w_in': nrm(ks[2], (L, D_MODEL, IN_WIDTH), D_MODEL ** -0.5),
        'ssm_a_re': -0.5 + nrm(ks[3], (L, SSM_GROUPS, SSM_STATE), 0.01),
        'ssm_a_im': np.pi * jnp.arange(SSM_STATE, dtype=f32) + nrm(ks[4], (L, SSM_GROUPS, SSM_STATE), 0.01),
        'ssm_log_dt': jax.random.uniform(ks[5], (L, SSM_GROUPS), f32, np.log(1e-3), np.log(1e-1)),
        'ssm_b_re': nrm(ks[6], (L, SSM_GROUPS, SSM_STATE, SSM_GROUP), (2 * SSM_GROUP) ** -0.5),
        'ssm_b_im': nrm(ks[7], (L, SSM_GROUPS, SSM_STATE, SSM_GROUP), (2 * SSM_GROUP) ** -0.5),
        'ssm_c_re': nrm(ks[8], (L, SSM_GROUPS, SSM_GROUP, SSM_STATE), SSM_STATE ** -0.5),
        'ssm_c_im': nrm(ks[9], (L, SSM_GROUPS, SSM_GROUP, SSM_STATE), SSM_STATE ** -0.5),
        'ssm_d': nrm(ks[10], (L, SSM_WIDTH), 1.0),
        'ssm_w_glu': nrm(ks[11], (L, SSM_WIDTH, SSM_WIDTH), SSM_WIDTH ** -0.5),
        'ssm_b_glu': nrm(ks[12], (L, SSM_WIDTH), 0.01),
        'cmp_pe_k': nrm(ks[13], (L, CMP_BLOCK, HEAD_DIM), 0.1),
        'cmp_pe_v': nrm(ks[14], (L, CMP_BLOCK, HEAD_DIM), 0.1),
        'cmp_wk1': nrm(ks[15], (L, CMP_BLOCK * HEAD_DIM, CMP_HIDDEN), (CMP_BLOCK * HEAD_DIM) ** -0.5),
        'cmp_wk2': nrm(ks[16], (L, CMP_HIDDEN, HEAD_DIM), CMP_HIDDEN ** -0.5),
        'cmp_wv1': nrm(ks[17], (L, CMP_BLOCK * HEAD_DIM, CMP_HIDDEN), (CMP_BLOCK * HEAD_DIM) ** -0.5),
        'cmp_wv2': nrm(ks[18], (L, CMP_HIDDEN, HEAD_DIM), CMP_HIDDEN ** -0.5),
        'q_norm_g': 1.0 + nrm(ks[19], (L, HEAD_DIM), 0.02),
        'k_norm_g': 1.0 + nrm(ks[20], (L, 3, HEAD_DIM), 0.02),
        'w_proj_ssm': nrm(ks[21], (L, SSM_WIDTH, D_MODEL), SSM_WIDTH ** -0.5),
        'w_proj_nsa': nrm(ks[22], (L, NSA_WIDTH, D_MODEL), NSA_WIDTH ** -0.5),
        'w_out': nrm(ks[23], (L, D_MODEL, D_MODEL), D_MODEL ** -0.5),
        'norm2_g': 1.0 + nrm(ks[24], (L, D_MODEL), 0.02),
        'w_up': nrm(ks[25], (L, D_MODEL, D_FF), D_MODEL ** -0.5),
        'w_down': nrm(ks[26], (L, D_FF, D_MODEL), D_FF ** -0.5),
    }

def first_block(x, norm1_g, w_in, ssm_a_re, ssm_a_im, ssm_log_dt, ssm_b_re, ssm_b_im, ssm_c_re, ssm_c_im,
              ssm_d, ssm_w_glu, ssm_b_glu, cmp_pe_k, cmp_pe_v, cmp_wk1, cmp_wk2, cmp_wv1, cmp_wv2,
              q_norm_g, k_norm_g, w_proj_ssm, w_proj_nsa, w_out, norm2_g, w_up, w_down):
    bsz, s, _ = x.shape
    o1 = SSM_WIDTH
    o2 = o1 + NSA_WIDTH
    o3 = o2 + KV_WIDTH
    o4 = o3 + 3 * NSA_HEADS
    for l in range(DEPTH):
        h = rmsnorm(x, norm1_g[l])
        hp = h @ w_in[l]
        y_ssm = s5_mixer(hp[..., :o1], ssm_a_re[l], ssm_a_im[l], ssm_log_dt[l], ssm_b_re[l], ssm_b_im[l],
                         ssm_c_re[l], ssm_c_im[l], ssm_d[l], ssm_w_glu[l], ssm_b_glu[l])
        y_nsa = nsa_mixer(hp[..., o1:o2], hp[..., o2:o3], hp[..., o3:o4], cmp_pe_k[l], cmp_pe_v[l],
                          cmp_wk1[l], cmp_wk2[l], cmp_wv1[l], cmp_wv2[l], q_norm_g[l], k_norm_g[l])
        gate = jax.nn.sigmoid(hp[..., o4:].reshape(bsz, s, N_MIXERS, D_MODEL))
        merged = gate[..., 0, :] * (y_ssm @ w_proj_ssm[l]) + gate[..., 1, :] * (y_nsa @ w_proj_nsa[l])
        x = x + merged @ w_out[l]
        h2 = rmsnorm(x, norm2_g[l])
        x = x + jnp.square(jax.nn.relu(h2 @ w_up[l])) @ w_down[l]
    return x


GRID_W = 64
CTX_LEN = 256
D_MIX = D_MODEL
ML_HEADS = 4
ML_HEAD_DIM = 128
ML_WIDTH = ML_HEADS * ML_HEAD_DIM
HG_HEADS = 4
HG_HEAD_DIM = 128
HG_WIDTH = HG_HEADS * HG_HEAD_DIM
ML_COLS = 4 * ML_WIDTH + 4 * ML_HEADS
HG_COLS = 5 * HG_WIDTH
IN_COLS = ML_COLS + HG_COLS
CONV_W = 3
D_FF_2 = 2816
ML_CHUNK = 64
HG_CHUNK = 32
N_MOD = 6


F32 = jnp.float32

def _rmsnorm(x, w):
    xf = x.astype(F32)
    y = xf * lax.rsqrt(jnp.mean(xf * xf, axis=-1, keepdims=True) + EPS)
    return (y * w.astype(F32)).astype(x.dtype)

def _modulate(h, shift, scale):
    return h * (1 + scale) + shift

def _head_rmsnorm(h, w):
    B, H, T, d = h.shape
    y = h * lax.rsqrt(jnp.mean(h * h, axis=-1, keepdims=True) + EPS)
    y = jnp.transpose(y, (0, 2, 1, 3)).reshape(B, T, H * d)
    return y * w.astype(F32)

def _to_heads(a, n_heads):
    B, T, C = a.shape
    return jnp.transpose(a.reshape(B, T, n_heads, C // n_heads), (0, 2, 1, 3)).astype(F32)

def _dwconv2d(x, w, rows, cols):
    B, T, C = x.shape
    img = x.reshape(B, rows, cols, C)
    out = lax.conv_general_dilated(img, w[:, :, None, :].astype(x.dtype), (1, 1), 'SAME',
                                   dimension_numbers=('NHWC', 'HWIO', 'NHWC'), feature_group_count=C)
    return out.reshape(B, T, C)

def _chunks(a, L):
    B, H, T = a.shape[:3]
    a = a.reshape(B, H, T // L, L, *a.shape[3:])
    return jnp.moveaxis(a, 2, 0)

def _unchunks(a):
    nc, B, H, L, d = a.shape
    return jnp.moveaxis(a, 0, 2).reshape(B, H, nc * L, d)

def _mlstm_scan(q, k, v, ig, lf, state):
    L = ML_CHUNK
    causal = jnp.tril(jnp.ones((L, L), bool))

    def step(carry, inp):
        C, n, m = carry
        qc, kc, vc, ic, fc = inp
        b = jnp.cumsum(fc, axis=-1)
        dlog = jnp.where(causal, b[..., :, None] - b[..., None, :] + ic[..., None, :], -jnp.inf)
        inter = b + m[..., None]
        mt = jnp.maximum(inter, jnp.max(dlog, axis=-1))
        w_intra = jnp.exp(dlog - mt[..., None])
        w_inter = jnp.exp(inter - mt)
        s = jnp.einsum('bhtd,bhsd->bhts', qc, kc) * w_intra
        num = jnp.einsum('bhts,bhsv->bhtv', s, vc) + w_inter[..., None] * jnp.einsum('bhtd,bhdv->bhtv', qc, C)
        den = jnp.sum(s, axis=-1) + w_inter * jnp.einsum('bhtd,bhd->bht', qc, n)
        h = num / jnp.maximum(jnp.abs(den), jnp.exp(-mt))[..., None]
        bL = b[..., -1]
        wlog = bL[..., None] - b + ic
        m_new = jnp.maximum(bL + m, jnp.max(wlog, axis=-1))
        decay = jnp.exp(bL + m - m_new)
        ws = jnp.exp(wlog - m_new[..., None])
        C_new = decay[..., None, None] * C + jnp.einsum('bhs,bhsd,bhsv->bhdv', ws, kc, vc)
        n_new = decay[..., None] * n + jnp.einsum('bhs,bhsd->bhd', ws, kc)
        return (C_new, n_new, m_new), h

    state, hs = lax.scan(step, state, tuple(_chunks(a, L) for a in (q, k, v, ig, lf)))
    return _unchunks(hs), state

def _hgrn_scan(q, k, v, lf, S):
    L = HG_CHUNK
    causal = jnp.tril(jnp.ones((L, L), bool))[:, :, None]

    def step(S, inp):
        qc, kc, vc, fc = inp
        b = jnp.cumsum(fc, axis=2)
        rel = jnp.where(causal, b[:, :, :, None, :] - b[:, :, None, :, :], -jnp.inf)
        a = jnp.einsum('bhtk,bhtsk,bhsk->bhts', qc, jnp.exp(rel), kc)
        o = jnp.einsum('bhts,bhsv->bhtv', a, vc) + jnp.einsum('bhtk,bhkv->bhtv', qc * jnp.exp(b), S)
        bL = b[:, :, -1]
        S_new = jnp.exp(bL)[..., None] * S + jnp.einsum('bhsk,bhsv->bhkv', kc * jnp.exp(bL[:, :, None] - b), vc)
        return S_new, o

    S, os_ = lax.scan(step, S, tuple(_chunks(a, L) for a in (q, k, v, lf)))
    return _unchunks(os_), S

def _bidir(scan_fn, ctx_f, ctx_b, lat_f, lat_b, init):
    flip = lambda a: jnp.flip(a, axis=2)
    hc_f, st_f = scan_fn(*ctx_f, init)
    hl_f, _ = scan_fn(*lat_f, st_f)
    hc_b, st_b = scan_fn(*(flip(a) for a in ctx_b), init)
    hl_b, _ = scan_fn(*(flip(a) for a in lat_b), st_b)
    return hl_f + flip(hl_b), hc_f + flip(hc_b)

def _mlstm_prep(p, conv_w, gate_b, rows, cols):
    W, H = ML_WIDTH, ML_HEADS
    qk = jax.nn.silu(_dwconv2d(p[..., :2 * W], conv_w, rows, cols))
    q = _to_heads(qk[..., :W], H) * (ML_HEAD_DIM ** -0.5)
    k = _to_heads(qk[..., W:], H)
    v = _to_heads(p[..., 2 * W:3 * W], H)
    o = p[..., 3 * W:4 * W]
    g = jnp.transpose(p[..., 4 * W:].astype(F32) + gate_b.astype(F32), (0, 2, 1))
    i_f, f_f, i_b, f_b = jnp.split(g, 4, axis=1)
    return q, k, v, o, (i_f, jax.nn.log_sigmoid(f_f)), (i_b, jax.nn.log_sigmoid(f_b))

def _mlstm_mixer(pl, pc, conv_w, gate_b, norm_w, rows, need_ctx):
    ql, kl, vl, ol, gfl, gbl = _mlstm_prep(pl, conv_w, gate_b, rows, GRID_W)
    qc, kc, vc, oc, gfc, gbc = _mlstm_prep(pc, conv_w, gate_b, 1, pc.shape[1])
    B = pl.shape[0]
    init = (jnp.zeros((B, ML_HEADS, ML_HEAD_DIM, ML_HEAD_DIM), F32),
            jnp.zeros((B, ML_HEADS, ML_HEAD_DIM), F32),
            jnp.zeros((B, ML_HEADS), F32))
    hl, hc = _bidir(_mlstm_scan, (qc, kc, vc) + gfc, (qc, kc, vc) + gbc,
                    (ql, kl, vl) + gfl, (ql, kl, vl) + gbl, init)
    out = lambda h, o: (_head_rmsnorm(h, norm_w) * jax.nn.sigmoid(o.astype(F32))).astype(pl.dtype)
    return out(hl, ol), (out(hc, oc) if need_ctx else None)

def _hgrn_prep(p, lb):
    W, H = HG_WIDTH, HG_HEADS
    pf = p.astype(F32)
    q = _to_heads(jax.nn.silu(pf[..., :W]), H) * (HG_HEAD_DIM ** -0.5)
    v = _to_heads(pf[..., 3 * W:4 * W], H)
    g = p[..., 4 * W:5 * W]
    dirs = []
    for j in range(2):
        z = pf[..., (1 + j) * W:(2 + j) * W]
        lbj = lb[j]
        lf = jnp.logaddexp(jnp.log(lbj), jnp.log1p(-lbj) + jax.nn.log_sigmoid(z))
        k = (1 - lbj) * jax.nn.sigmoid(-z)
        dirs.append((q, _to_heads(k, H), v, _to_heads(lf, H)))
    return dirs[0], dirs[1], g

def _hgrn_mixer(pl, pc, lb, norm_w, need_ctx):
    lat_f, lat_b, gl = _hgrn_prep(pl, lb)
    ctx_f, ctx_b, gc = _hgrn_prep(pc, lb)
    B = pl.shape[0]
    init = jnp.zeros((B, HG_HEADS, HG_HEAD_DIM, HG_HEAD_DIM), F32)
    hl, hc = _bidir(_hgrn_scan, ctx_f, ctx_b, lat_f, lat_b, init)
    out = lambda h, g: (_head_rmsnorm(h, norm_w) * jax.nn.silu(g.astype(F32))).astype(pl.dtype)
    return out(hl, gl), (out(hc, gc) if need_ctx else None)

def _conv_ffn(h, w_up, conv_w, w_down, rows, cols):
    u = _dwconv2d(h @ w_up, conv_w, rows, cols)
    a, b = jnp.split(u, 2, axis=-1)
    return (jax.nn.silu(a) * b) @ w_down

def second_inputs(seed: int = 0) -> dict:
    key = jax.random.key(seed)
    ks = jax.random.split(key, 24)
    nrm = lambda k, shape, s: jax.random.normal(k, shape, F32) * s
    L, D = DEPTH, D_MODEL
    gate_b = jnp.concatenate([
        nrm(ks[8], (L, ML_HEADS), 0.1),
        jnp.linspace(3.0, 6.0, ML_HEADS, dtype=F32)[None] + nrm(ks[9], (L, ML_HEADS), 0.1),
        nrm(ks[10], (L, ML_HEADS), 0.1),
        jnp.linspace(3.0, 6.0, ML_HEADS, dtype=F32)[None] + nrm(ks[11], (L, ML_HEADS), 0.1)], axis=-1)
    return {
        "x": nrm(ks[0], (BATCH, SEQ, D), 1.0),
        "c": nrm(ks[1], (BATCH, D), 1.0),
        "ctx": nrm(ks[2], (BATCH, CTX_LEN, D), 1.0),
        "c_ctx": nrm(ks[3], (D,), 1.0),
        "w_mod": nrm(ks[4], (L, D, N_MOD * D), D ** -0.5),
        "b_mod": nrm(ks[5], (L, N_MOD * D), 0.02),
        "norm1_w": 1.0 + nrm(ks[6], (L, D), 0.05),
        "w_in": nrm(ks[7], (L, D, IN_COLS), D ** -0.5),
        "mlstm_gate_b": gate_b,
        "mlstm_conv_w": nrm(ks[12], (L, CONV_W, CONV_W, 2 * ML_WIDTH), 1.0 / CONV_W),
        "mlstm_norm_w": 1.0 + nrm(ks[13], (L, ML_WIDTH), 0.05),
        "hgrn_lb_logits": nrm(ks[14], (2, L + 1, HG_WIDTH), 0.1),
        "hgrn_norm_w": 1.0 + nrm(ks[15], (L, HG_WIDTH), 0.05),
        "w_out": nrm(ks[16], (L, D_MIX, D), D_MIX ** -0.5),
        "norm2_w": 1.0 + nrm(ks[17], (L, D), 0.05),
        "w_up": nrm(ks[18], (L, D, 2 * D_FF_2), D ** -0.5),
        "ffn_conv_w": nrm(ks[19], (L, CONV_W, CONV_W, 2 * D_FF_2), 1.0 / CONV_W),
        "w_down": nrm(ks[20], (L, D_FF_2, D), D_FF_2 ** -0.5),
        "final_norm_w": 1.0 + nrm(ks[21], (D,), 0.05),
    }

def second_block(x, c, ctx, c_ctx, w_mod, b_mod, norm1_w, w_in, mlstm_gate_b, mlstm_conv_w, mlstm_norm_w,
              hgrn_lb_logits, hgrn_norm_w, w_out, norm2_w, w_up, ffn_conv_w, w_down, final_norm_w):
    rows = x.shape[1] // GRID_W
    ctx_len = ctx.shape[1]
    lower_bounds = jnp.cumsum(jax.nn.softmax(hgrn_lb_logits.astype(F32), axis=1), axis=1)
    xl, xc = x, ctx
    for l in range(DEPTH):
        last = l == DEPTH - 1
        mod_l = (jax.nn.silu(c) @ w_mod[l] + b_mod[l])[:, None, :]
        mod_c = (jax.nn.silu(c_ctx) @ w_mod[l] + b_mod[l])[None, None, :]
        sh1, sc1, g1, sh2, sc2, g2 = jnp.split(mod_l, N_MOD, axis=-1)
        sh1c, sc1c, g1c, sh2c, sc2c, g2c = jnp.split(mod_c, N_MOD, axis=-1)
        pl = _modulate(_rmsnorm(xl, norm1_w[l]), sh1, sc1) @ w_in[l]
        pc = _modulate(_rmsnorm(xc, norm1_w[l]), sh1c, sc1c) @ w_in[l]
        ml_l, ml_c = _mlstm_mixer(pl[..., :ML_COLS], pc[..., :ML_COLS], mlstm_conv_w[l], mlstm_gate_b[l],
                                  mlstm_norm_w[l], rows, not last)
        hg_l, hg_c = _hgrn_mixer(pl[..., ML_COLS:], pc[..., ML_COLS:], lower_bounds[:, l], hgrn_norm_w[l], not last)
        xl = xl + g1 * (jnp.concatenate([ml_l, hg_l], axis=-1) @ w_out[l])
        xl = xl + g2 * _conv_ffn(_modulate(_rmsnorm(xl, norm2_w[l]), sh2, sc2), w_up[l], ffn_conv_w[l],
                                 w_down[l], rows, GRID_W)
        if not last:
            xc = xc + g1c * (jnp.concatenate([ml_c, hg_c], axis=-1) @ w_out[l])
            xc = xc + g2c * _conv_ffn(_modulate(_rmsnorm(xc, norm2_w[l]), sh2c, sc2c), w_up[l], ffn_conv_w[l],
                                      w_down[l], 1, ctx_len)
    return _rmsnorm(xl, final_norm_w)


def setup_inputs(seed=0):
    out = dict(first_inputs(seed))
    for name, value in second_inputs(seed + 1).items():
        if name != "x":
            out[name + "_2"] = value
    return out


def reference(
    x, norm1_g, w_in, ssm_a_re, ssm_a_im, ssm_log_dt, ssm_b_re, ssm_b_im, ssm_c_re, ssm_c_im,
    ssm_d, ssm_w_glu, ssm_b_glu, cmp_pe_k, cmp_pe_v, cmp_wk1, cmp_wk2, cmp_wv1, cmp_wv2,
    q_norm_g, k_norm_g, w_proj_ssm, w_proj_nsa, w_out, norm2_g, w_up, w_down, c_2, ctx_2,
    c_ctx_2, w_mod_2, b_mod_2, norm1_w_2, w_in_2, mlstm_gate_b_2, mlstm_conv_w_2,
    mlstm_norm_w_2, hgrn_lb_logits_2, hgrn_norm_w_2, w_out_2, norm2_w_2, w_up_2, ffn_conv_w_2,
    w_down_2, final_norm_w_2,
):
    x = first_block(
        x, norm1_g, w_in, ssm_a_re, ssm_a_im, ssm_log_dt, ssm_b_re, ssm_b_im, ssm_c_re,
        ssm_c_im, ssm_d, ssm_w_glu, ssm_b_glu, cmp_pe_k, cmp_pe_v, cmp_wk1, cmp_wk2, cmp_wv1,
        cmp_wv2, q_norm_g, k_norm_g, w_proj_ssm, w_proj_nsa, w_out, norm2_g, w_up, w_down,
    )
    return second_block(
        x, c_2, ctx_2, c_ctx_2, w_mod_2, b_mod_2, norm1_w_2, w_in_2, mlstm_gate_b_2,
        mlstm_conv_w_2, mlstm_norm_w_2, hgrn_lb_logits_2, hgrn_norm_w_2, w_out_2, norm2_w_2,
        w_up_2, ffn_conv_w_2, w_down_2, final_norm_w_2,
    )


_drawn_inputs = setup_inputs


def setup_inputs(seed=0):
    import zlib

    import numpy as np

    out = dict(_drawn_inputs(seed))
    spreads = {}
    factors = {'norm1_g': 6.871,
     'ssm_a_re': 200.0,
     'ssm_a_im': 67.976,
     'ssm_log_dt': 71.592,
     'ssm_b_re': 139.16,
     'ssm_b_im': 132.656,
     'ssm_c_re': 136.72,
     'ssm_c_im': 132.408,
     'ssm_b_glu': 62.05,
     'cmp_pe_k': 8.0,
     'cmp_pe_v': 2.999,
     'q_norm_g': 8.0,
     'k_norm_g': 8.0,
     'norm2_g': 3.147,
     'ctx_2': 5.391,
     'b_mod_2': 2.895,
     'norm1_w_2': 4.337,
     'mlstm_norm_w_2': 56.096,
     'hgrn_lb_logits_2': 24.356,
     'hgrn_norm_w_2': 4.666,
     'c_ctx_2': 4.317,
     'mlstm_conv_w_2': 5.318,
     'norm2_w_2': 8.0}
    for name, (base, spread) in spreads.items():
        noise = np.random.default_rng([zlib.crc32(name.encode()), seed]).standard_normal(out[name].shape)
        drawn = base * np.exp(spread * noise) if base else spread * noise
        out[name] = __import__('jax').numpy.asarray(drawn.astype(out[name].dtype))
    for name, factor in factors.items():
        out[name] = (out[name] * factor).astype(out[name].dtype)
    return out
```

```python
import concourse.bass as bass
from concourse import mybir
from contextlib import ExitStack

F32 = mybir.dt.float32
U8 = mybir.dt.uint8
ACT = mybir.ActivationFunctionType
ALU = mybir.AluOpType
AX = mybir.AxisListType
ds = bass.ds

P = 128
T, C, D = 512, 256, 1024
S = C + T
TT, CT, DT = T // P, C // P, D // P
ST = CT + TT
EPS = 1e-6

GROUPS, GROUP, STATE = 32, 16, 64
STEP = P // GROUP
CHUNKS = T // STEP
UT = GROUPS * GROUP // P
HEADS, HD = 8, 64
KVG = 2
HPG = HEADS // KVG
CMP_STRIDE, CMP_BLOCK = 16, 32
NCMP = T // CMP_STRIDE - 1
FF = 4 * D
FT = FF // P
FAR = 2.56e32

MH = 4
FF2 = 2816
F2T = FF2 // P
TAPS = 9
GRID_W, ROWS = 64, 8
NMOD = 6

VEC = {}
_at = 0
for _name, _rows in (("norm1_g", DT), ("ssm_d", UT), ("ssm_b_glu", UT), ("norm2_g", DT), ("c_2", DT),
                     ("c_ctx_2", DT), ("norm1_w_2", DT), ("norm2_w_2", DT), ("final_norm_w_2", DT),
                     ("hgrn_lb_logits_2", 4 * MH), ("b_mod_2", NMOD * DT),
                     ("mlstm_conv_w_2", TAPS * DT), ("q_norm_g", 1), ("k_norm_g", 3),
                     ("mlstm_norm_w_2", MH), ("hgrn_norm_w_2", MH), ("pe", CMP_BLOCK),
                     ("a_re", GROUPS), ("a_im", GROUPS)):
    VEC[_name] = _at
    _at += _rows
VEC_COLS = _at
VEC0 = VEC["mlstm_conv_w_2"]
VEC1 = VEC["pe"]

TILES = (("params", 4), ("x", DT), ("u", UT), ("q", 4), ("kv", 6), ("gates", 1),
         ("kernel", 8), ("bt", 8), ("state", 4), ("qk_norm", 6), ("v_tok", 2), ("y", 4), ("glu", UT),
         ("o_nsa", 4), ("merge", 32), ("out1", DT), ("up1", FT), ("down1", DT),
         ("ctx", 4), ("gate_rows", 2), ("v2", 12), ("gate_cols", 1), ("hg_in", 16), ("hg", 64), ("ml", 32),
         ("out2", DT), ("up2", 2 * F2T), ("down2", DT), ("final", 8))
CHUNK_OF = (("u", 2), ("q", 2), ("kv", 3), ("cmp", 4), ("mod", 24), ("glu", 1), ("merge", 16), ("out1", 4),
            ("up1", 16), ("down1", 16), ("v2", 4), ("hg_in", 8), ("ml_in", 8),
            ("ml_o", 8), ("out2", 4), ("up2", F2T), ("down2", 16))


def offsets(plan):
    at, out = 0, {}
    for name, n in plan:
        out[name] = at
        at += n
    return out


T0, C0 = offsets(TILES), offsets(CHUNK_OF)
BANKS, SLOTS = 4, 2

ARENA = 34 * 1024 - 160

(LOG_DT, DT_, AR_DT, ANGLE, TURNS, SIN_H, SIN, COS, MAG, MAG_STEP, DEN, NR, FR, FI, TMP, _1, _2, _3, _4) = range(19)
PR, PI = 20, 20 + STEP + 1
E1C, E1S, E8C, E8S = 38, 39, 40, 41
S5_TERMS = 44
TWO_PI = 6.283185307179586
TURN_A = 6.28125
TURN_B = 0.0019350051879882812
TURN_C = TWO_PI - TURN_A - TURN_B
ROUND = 12582912.0
ATT_STEPS = 136


SEGS = (P + 1) * ST
SUMS = 2 * SEGS + 16
PRE_F, SUF_B, PRE_B, CTX_F = (2 * SEGS + k for k in (0, 4, 8, 10))
LEVELS = (64, 32, 16, 8, 4, 2, 1)
UNITS = 11
DIAG, PAIRS, HALVES, CONTEXT = 7, 8, 9, 10
TINY = 1e-37


class Steps:

    def __init__(self, eng, sem):
        self.eng, self.sem, self.base, self.n = eng, sem, 0, 0

    def mark(self, ins):
        ins.then_inc(self.sem, 1)
        self.n += 1
        return self.base + self.n

    def wait(self, value):
        self.eng.wait_ge(self.sem, value)

    def __call__(self, ins):
        self.wait(self.mark(ins))

    def enter(self, i, steps):
        self.start, self.steps = self.base + self.n, steps
        self.base, self.n = self.start + i * steps, 0

    def leave(self, rounds):
        assert self.n == self.steps, f"{self.n} steps, not {self.steps}"
        self.base, self.n = self.start + rounds * self.steps, 0


def two_block_program(nc, a, out):
    ctx = ExitStack()
    with ctx:
        def sb(name, shape, dt=F32):
            return ctx.enter_context(nc.sbuf_tensor(name, shape, dt))

        def sem(name):
            return ctx.enter_context(nc.semaphore(name))

        ident = sb("ident", [P, P])
        mean_d = sb("mean_d", [P, P])
        mean_hd = sb("mean_hd", [P, P])
        dist = sb("dist", [P, T])
        cdist = sb("cdist", [P, TT, NCMP])
        cmask = sb("cmask", [P, TT, NCMP])
        negslope = sb("negslope", [P, HEADS])
        sign = sb("sign", [P, 1])
        nsign = sb("nsign", [P, 1])
        g_q = sb("g_q", [P, 1])
        eps = sb("eps", [P, 1])
        vec = sb("vec", [P, VEC_COLS])
        ffn_taps = sb("ffn_taps", [P, TAPS * 2 * F2T])
        w_gate = sb("w_gate", [P, DT, 3 * HEADS])
        w_mgate = sb("w_mgate", [P, DT, 4 * MH])
        mgate_b = sb("mgate_b", [4 * MH, 1])
        wk2 = sb("wk2", [P, 2, HD])
        wv2 = sb("wv2", [P, HD])
        mod = sb("mod", [P, NMOD * DT, 2])
        silu_c = sb("silu_c", [P, DT, 2])
        xT = sb("xT", [P, DT, T])
        hT = sb("hT", [P, DT, T])
        ring = sb("ring", [P, SLOTS, DT * 2 * P])
        sq = sb("sq", [P, 2, T])
        rstd = sb("rstd", [P, T])
        root = sb("root", [P, 2, T])
        tick = sb("tick", [P, 10])
        zero = sb("zero", [P, 1])
        same = sb("same", [P, len(LEVELS), P], U8)
        arena = sb("arena", [P, ARENA])

        def area(at, *shape):
            n = 1
            for k in shape:
                n *= k
            v = arena[:, at:at + n]
            names = "abcd"[:len(shape)]
            if len(shape) > 1:
                v = v.rearrange(f"p ({' '.join(names)}) -> p {' '.join(names)}",
                                **{k: s for k, s in zip(names[1:], shape[1:])})
            return v

        K = 1024
        pows = area(0, GROUPS, STEP, GROUP)
        e1 = area(0, GROUPS, CHUNKS)
        e2 = area(2 * K, GROUPS, CHUNKS)
        z2 = area(0, GROUPS, CHUNKS)
        xprev = area(2 * K, GROUPS, CHUNKS)
        ubar = area(4 * K, GROUPS, GROUP)
        vbar = area(4 * K + 512, GROUPS, GROUP)
        cu = area(4 * K + 1024, GROUPS, GROUP)
        cv = area(4 * K + 1536, GROUPS, GROUP)
        bt = area(4 * K, GROUPS, P)
        z1 = area(4 * K, GROUPS, CHUNKS)
        zs = area(6 * K, GROUPS, CHUNKS)
        ych = area(4 * K, GROUPS, CHUNKS)
        yT = area(6 * K, UT, STEP, CHUNKS)
        vrows = area(8 * K, 5, P)
        frows = area(9 * K, 4, P)
        ca = area(8 * K, GROUPS, STEP + 1, GROUP)
        AT = 8 * K + GROUPS * (STEP + 1) * GROUP
        bu = area(AT, GROUPS, GROUP)
        bv = area(AT + 512, GROUPS, GROUP)
        cn = area(AT + 1024, 2, UT, P)
        kern = area(AT, GROUPS, P)
        uch = area(AT + 2 * K, GROUPS, CHUNKS)
        rot_c = area(AT + 4 * K, GROUPS, CHUNKS)
        rot_s = area(AT + 6 * K, GROUPS, CHUNKS)
        us = area(AT + 4 * K, UT, STEP, CHUNKS)
        x_tok = area(AT + 8 * K, TT, D)
        u_st = area(AT + 8 * K, UT, STEP, CHUNKS)
        toep = area(AT + 8 * K, GROUPS, P)
        s5 = area(AT + 12 * K, S5_TERMS, GROUPS)
        ptmp = area(AT + 12 * K + S5_TERMS * GROUPS, 2, 512)
        AT2 = AT + 12 * K + S5_TERMS * GROUPS + K
        gelu_y = area(0, UT, T)
        y_ssm = area(8 * K, UT, T)
        qT = area(AT2, 4, T)
        kvT = area(AT2 + 2 * K, 6, T)
        v_tok = area(AT2 + 5 * K, 2, TT, P)
        kc = area(AT2 + 6 * K, KVG * NCMP)
        vc = area(AT2 + 6 * K + 64, KVG, HD)
        gsig = area(AT2 + 6 * K + 192, TT, 3 * HEADS)
        hid = area(AT2 + 6 * K + 288, 2, 64)
        hbias = area(AT2 + 6 * K + 416, 2)
        knorm = area(AT2 + 6 * K + 420, 64)
        assert AT2 + 6 * K + 484 <= ARENA
        kk = area(AT, 2, KVG, T)
        N = AT + 2 * K
        qn = area(N, 2, T)
        score = area(N + K, 2, 2, T)
        prob = area(N + 3 * K, 2, 2, T)
        probT = area(N + 5 * K, 2, 2, T)
        bias = area(N + 7 * K, 2, T)
        cscore = area(N + 8 * K, 2, NCMP)
        cprob = area(N + 8 * K + 64, 2, NCMP)
        cprobT = area(N + 8 * K + 128, 2, P)
        cbias = area(N + 8 * K + 384, 2, TT, NCMP)
        stats = area(N + 8 * K + 640, 2, 16)
        kcg = area(N + 8 * K + 672, NCMP)
        kkg = area(N + 9 * K, 2, T)
        o_tok = area(4 * K, TT, HEADS * HD)
        y_nsa = area(6 * K, 4, T)
        merged = area(N, DT, T)
        sig = area(N + 4 * K, 2, T)
        prod = area(N + 5 * K, 2, 2, T)
        act = area(0, FT, T)
        relu = area(AT2, 4, T)

        ml_q = area(0, MH, T)
        hg_g = area(2 * K, MH, T)
        y_all = area(0, 2 * MH, T)
        ml_k = area(4 * K, MH, S)
        hg_q = area(7 * K, MH, T)
        hg_k = area(9 * K, MH, 2, S)
        sums = area(15 * K, MH, SUMS)
        at = 15 * K + MH * SUMS
        hg_v = area(at, ST, MH * P)
        ml_v = area(at + ST * MH * P, ST, MH, P + 1)
        at += ST * MH * P + ST * MH * (P + 1)
        hcT = area(at, DT, C)
        W2 = at + DT * C
        ctx_tok = area(W2, CT, D)
        xcT = area(W2 + 2 * K, DT, C)
        block_of = area(W2 + 4 * K, P)
        row_g = area(W2, 2, S)
        row_f = area(W2 + 2 * S, 2, S)
        row_b = area(W2 + 4 * S, 2, S)
        logf = area(W2, 2, ST, P + 1)
        sums1 = area(W2 + 2 * SEGS, SUMS)
        a_ctx = area(W2, CT, T)
        a_half = area(W2 + CT * T, TT, T // 2)
        a_pair = area(W2 + CT * T + TT * T // 2, TT, P)
        a_own = area(W2 + CT * T + TT * T // 2 + TT * P, TT, P)
        at = W2 + CT * T + TT * T // 2 + 2 * TT * P
        y_tok = area(at, TT, P)
        squared = area(at + TT * P, TT, P)
        at = W2 + 6 * S
        assert W2 + 2 * SEGS + SUMS <= at and W2 + 4 * K + P <= at
        gcol = area(at, 2, ST, MH)
        floor = area(at + 2 * ST * MH, 2, TT, MH)
        amod = area(at + 2 * ST * MH + 2 * TT * MH, 3, DT)
        lb = area(at + 2 * ST * MH + 2 * TT * MH + 3 * DT, 3, 2, MH)
        at += 2 * ST * MH + 2 * TT * MH + 3 * DT + 6 * MH
        stat2 = area(at, 4, 2 * TT)
        assert at + 8 * TT <= ARENA
        W3 = 7 * K
        qc = area(W3, T)
        kc2 = area(W3 + T, S)
        cummax = area(W3 + T + S, 2, T)
        o_sig = area(W3 + 3 * T + S, T)
        h_tok = area(W3 + 4 * T + S, TT, P)
        weight = area(W3 + 5 * T + S, 2, ST, T)
        assert W3 + 5 * T + S + 2 * ST * T <= 15 * K + MH * SUMS
        causal = area(W2, 2, P)
        act2 = area(0, F2T, T)
        raw = area(11 * K, 4, T)
        conv = area(13 * K, 4, T)
        out_tok = area(0, TT, D)
        sums_v = sums[:, :, 0:2 * SEGS].rearrange("p h (d a n) -> p h d a n", d=2, a=ST)
        ek, eq, eq_b = sq, root, rstd

        def unit_tiles(u):
            t = T0["hg"] + 3
            return [t + u] if u < HALVES else [t + HALVES + 2 * (u - HALVES) + k for k in range(2)]

        m_scr = nc.dram_tensor("m_scr", (2, MH, T), F32, kind="Internal").ap()

        def targets(w, d, s):
            b = s - CT
            if b < 0:
                return w[:, d, s, :]
            return w[:, d, s, b * P:] if d == 0 else w[:, d, s, 0:(b + 1) * P]
        banks = [ctx.enter_context(nc.psum_tensor(f"bank{i}", [P, T], F32)) for i in range(8)]
        acc = banks[:BANKS]
        stat, modp = banks[4], banks[5]

        u_scr = nc.dram_tensor("u_scr", (UT * P, STEP, CHUNKS), F32, kind="Internal").ap()
        y_scr = nc.dram_tensor("y_scr", (UT * P, STEP, CHUNKS), F32, kind="Internal").ap()

        loaded = [sem(f"chunk_loaded{i}") for i in range(SLOTS)]
        chunk_used = sem("chunk_used")
        acc_full = sem("acc_full")
        acc_out = [sem(f"acc_out{i}") for i in range(BANKS)]
        dve_step, act_step, pool_step = sem("dve_step"), sem("act_step"), sem("pool_step")
        consts = sem("consts")
        params, x_in, w_small = sem("params"), sem("x_in"), sem("w_small")
        sq_ready, sq_used = sem("sq_ready"), sem("sq_used")
        rstd_ready, h_ready = sem("rstd_ready"), sem("h_ready")
        s5_exp, s5_angle, s5_sin, s5_small, s5_bbar = (sem(n) for n in ("s5_exp", "s5_angle", "s5_sin", "s5_small", "s5_bbar"))
        ca_ready, rot_ready, decay_ready = (sem(n) for n in ("ca_ready", "rot_ready", "decay_ready"))
        u_out, u_in, toep_zero, toep_in = (sem(n) for n in ("u_out", "u_in", "toep_zero", "toep_in"))
        e_swapped, z_scanned, z_swapped, xprev_ready = (sem(n) for n in ("e_swapped", "z_scanned", "z_swapped", "xprev_ready"))
        y_out, y_in, y_sum, gelu_done, yssm_ready = (sem(n) for n in ("y_out", "y_in", "y_sum", "gelu_done", "yssm_ready"))
        silu_ready, mod_full, mod_ready = sem("silu_ready"), sem("mod_full"), sem("mod_ready")
        hid_full, hid_ready, kc_full, kc_sq, kc_mean, kc_ready, vc_full, vc_ready = (
            sem(n) for n in ("hid_full", "hid_ready", "kc_full", "kc_sq", "kc_mean", "kc_ready", "vc_full", "vc_ready"))
        qk_sq, qk_rstd, k_normed, k_dup = (sem(n) for n in ("qk_sq", "qk_rstd", "k_normed", "k_dup"))
        qn_ready, score_full, cscore_full, score_ready, prob_ready, cprob_ready = (
            sem(n) for n in ("qn_ready", "score_full", "cscore_full", "score_ready", "prob_ready", "cprob_ready"))
        pt_full, pt_out, cpt_out, o_full, o_ready = (sem(n) for n in ("pt_full", "pt_out", "cpt_out", "o_full", "o_ready"))
        merged_ready, x1_ready, relu_ready, act_ready = (
            sem(n) for n in ("merged_ready", "x1_ready", "relu_ready", "act_ready"))
        stored = sem("stored")
        ctx_in, h_scaled = sem("ctx_in"), sem("h_scaled")
        g16_ready, rows_in, neg_ready, ln_ready, rows_ready, max_out, cols_ready = (
            sem(n) for n in ("g16_ready", "rows_in", "neg_ready", "ln_ready", "rows_ready", "max_out", "cols_ready"))
        lb_logit, lb_sig, lb_ready, same_ready, ones_ready = (
            sem(n) for n in ("lb_logit", "lb_sig", "lb_ready", "same_ready", "ones_ready"))
        z_ctx, z_ready, f_ready, logf_ready, sums_ready, sums_kept = (
            sem(n) for n in ("z_ctx", "z_ready", "f_ready", "logf_ready", "sums_ready", "sums_kept"))
        diff_ready, exp_ready, kq_ready, hg_o, hg_rstd, hg_y, hg_flipped, hg_done = (
            sem(n) for n in ("diff_ready", "exp_ready", "kq_ready", "hg_o", "hg_rstd", "hg_y", "hg_flipped", "hg_done"))
        max_in, qk_conv, qk_ready, gap_ready, w_ready, p_ready, p_masked, ml_o, ml_h, ml_rstd, ml_y = (
            sem(n) for n in ("max_in", "qk_conv", "qk_ready", "gap_ready", "w_ready", "p_ready", "p_masked", "ml_o",
                             "ml_h", "ml_rstd", "ml_y"))
        conv_ready, silu2_ready, act2_ready = (sem(n) for n in ("conv_ready", "silu2_ready", "act2_ready"))
        out_ready = sem("out_ready")

        def rows(at, name, src, tile=0):
            n = src.shape[0]
            return vrows[VEC[name] - at:VEC[name] - at + n, tile, 0:src.shape[1]], src

        def of128(ap):
            return ap.rearrange("(r c) -> r c", c=P)

        param_loads = [rows(0, n, of128(a[n][0])) for n in ("norm1_g", "ssm_d", "ssm_b_glu", "norm2_g", "c_2",
                                                            "norm1_w_2", "norm2_w_2", "b_mod_2")]
        param_loads += [rows(0, n, of128(a[n])) for n in ("c_ctx_2", "final_norm_w_2")]
        param_loads += [rows(0, "hgrn_lb_logits_2", a["hgrn_lb_logits_2"].rearrange("d l (r c) -> (d l r) c", c=P)),
                        rows(VEC0, "mlstm_conv_w_2", a["mlstm_conv_w_2"][0].rearrange("y x (r c) -> (y x r) c", c=P), 1),
                        rows(VEC0, "mlstm_norm_w_2", of128(a["mlstm_norm_w_2"][0]), 1),
                        rows(VEC0, "hgrn_norm_w_2", of128(a["hgrn_norm_w_2"][0]), 1)]
        for h in range(2):
            half = slice(h * HD, (h + 1) * HD)
            for n, src in (("q_norm_g", a["q_norm_g"]), ("k_norm_g", a["k_norm_g"][0])):
                r = VEC[n] - VEC0
                param_loads.append((vrows[r:r + src.shape[0], 1, half], src))
            param_loads.append((vrows[0:CMP_BLOCK, 2, half], a[("cmp_pe_k", "cmp_pe_v")[h]][0]))
            for k, n in enumerate(("ssm_a_re", "ssm_a_im")):
                param_loads.append((vrows[0:GROUPS, 3 + k, half], a[n][0]))
            for k in range(2):
                n = ("re", "im")[(h + k) % 2]
                param_loads.append((cn[:, k, :, half],
                                    a["ssm_c_" + n][0].rearrange("g c p -> (g c) p").rearrange("(m q) p -> q m p", q=P)))
                param_loads.append(((bu, bv)[k][half], a["ssm_b_" + n][0].rearrange("g p c -> p g c")))
        param_loads.append((frows[0:99], a["ffn_conv_w_2"][0].rearrange("y x (r c) -> (y x r) c", c=P)
                            .rearrange("(m r) c -> r m c", r=99)))
        param_loads.append((s5[:, LOG_DT], a["ssm_log_dt"].to_broadcast([P, GROUPS])))
        gate_at = GROUPS * GROUP + HEADS * HD + 6 * KVG * HD
        mgate_at = 4 * MH * P
        small_loads = [(w_gate[:], a["w_in"][0][:, gate_at:gate_at + 3 * HEADS].rearrange("(k p) n -> p k n", p=P)),
                       (w_mgate[:], a["w_in_2"][0][:, mgate_at:mgate_at + 4 * MH].rearrange("(k p) n -> p k n", p=P)),
                       (mgate_b[:], a["mlstm_gate_b_2"].rearrange("a n -> n a")),
                       (wk2[:, 0], a["cmp_wk2"][0]), (wk2[:, 1], a["cmp_wk2"][0]), (wv2[:], a["cmp_wv2"][0])]
        CONSTS = 10 + HEADS

        block = ctx.enter_context(nc.Block())

        def full(eng, t, more=0):
            eng.wait_ge(acc_full, t + 1 + more)

        def copied(eng, t, more=0):
            eng.wait_ge(acc_out[t % BANKS], t // BANKS + 1 + more)

        def out_of(t, ins):
            ins.then_inc(acc_out[t % BANKS], 1)

        cells = iter(range(2, 10))

        def free(eng, place, n=1):
            cell = tick[:, next(cells)].unsqueeze(1)
            (eng.copy(cell, zero[:]) if eng is nc.scalar else eng.memset(cell, 0.0)).then_inc(place, n)

        def vcol(name, k=0):
            return vec[:, VEC[name] + k:VEC[name] + k + 1]

        @block.sync
        def _(sp):
            def load(n, *pairs, i=0, per=0):
                if n >= SLOTS or per:
                    sp.wait_ge(chunk_used, n - SLOTS + 1 + i * per)
                for dst, src in pairs:
                    sp.dma_start(dst, src).then_inc(loaded[n % SLOTS], 16)

            def columns(n, w, at, width, **kw):
                dst = ring[:, n % SLOTS, 0:DT * width].rearrange("p (k n) -> p k n", n=width)
                src = w[:, at:at + width] if isinstance(at, int) else w[:, ds(at, width)]
                src = src.rearrange("(k p) n -> p k n", p=P)
                half = DT // 2
                load(n, (dst[:, :half], src[:, :half]), (dst[:, half:], src[:, half:]), **kw)

            x_v = a["x"][0].rearrange("(t p) c -> p t c", p=P)
            for t in range(TT):
                sp.dma_start(x_tok[:, t], x_v[:, t]).then_inc(x_in, 16)
            w_in = a["w_in"][0]
            width = 2 * P
            for n in range(7):
                columns(n, w_in, n * width, width)
            for n in range(4):
                w1 = (a["cmp_wk1"], a["cmp_wv1"])[n // 2][0].rearrange("(r d) n -> d r n", d=HD)
                c, r = C0["cmp"] + n, CMP_BLOCK // 2
                dst = ring[:, c % SLOTS, :].rearrange("p (r n) -> p r n", n=P)
                load(c, *[(dst[h * HD:(h + 1) * HD], w1[:, n % 2 * r:(n % 2 + 1) * r]) for h in range(2)])
            with sp.Fori(0, 12) as i:
                for k in range(2):
                    columns(C0["mod"] + k, a["w_mod_2"][0], i * (2 * width) + k * width, width, i=i, per=2)
            g = C0["glu"]
            w_glu = a["ssm_w_glu"][0].rearrange("(k p) n -> p k n", p=P)
            dst = ring[:, g % SLOTS, :].rearrange("p (k n) -> p k n", k=UT)
            load(g, (dst[:, 0:2], w_glu[:, 0:2]), (dst[:, 2:4], w_glu[:, 2:4]))
            gates_at = gate_at + 3 * HEADS
            with sp.Fori(0, DT) as i:
                for m, w in enumerate((a["w_proj_ssm"], a["w_proj_nsa"])):
                    n = C0["merge"] + m
                    dst = ring[:, n % SLOTS, 0:12 * P].rearrange("p (k n) -> p k n", n=P)
                    load(n, (dst[:, 0:DT], w_in[:, ds(i * P + gates_at + m * D, P)].rearrange("(k p) n -> p k n", p=P)),
                         (dst[:, DT:], w[0][:, ds(i * P, P)].rearrange("(k p) n -> p k n", p=P)), i=i, per=2)

            def whole(name, w, chunks):
                with sp.Fori(0, chunks // 2) as i:
                    for k in range(2):
                        columns(C0[name] + k, w, i * (2 * width) + k * width, width, i=i, per=2)

            whole("out1", a["w_out"][0], 4)
            whole("up1", a["w_up"][0], 16)
            with sp.Fori(0, 4) as i:
                for k in range(4):
                    columns(C0["down1"] + k, a["w_down"][0][k * D:(k + 1) * D, :], i * width, width, i=i, per=4)
            w_in2 = a["w_in_2"][0]
            hg_at = mgate_at + 4 * MH
            for m, at in enumerate((hg_at + 3 * MH * P, 2 * MH * P)):
                for k in range(2):
                    n = C0["v2"] + 2 * m + k
                    dst = ring[:, n % SLOTS, :].rearrange("p (k n) -> p k n", k=DT // 2)
                    src = w_in2[k * D // 2:(k + 1) * D // 2, at:at + MH * P].rearrange("(k p) n -> p k n", p=P)
                    load(n, (dst[:, 0:2], src[:, 0:2]), (dst[:, 2:4], src[:, 2:4]))

            def pairs(n, w, ats, i, per):
                dst = ring[:, n % SLOTS, :].rearrange("p (m k n) -> p m k n", m=2, k=DT)
                load(n, *[(dst[:, m], w[:, ds(at, P)].rearrange("(k p) n -> p k n", p=P)) for m, at in enumerate(ats)],
                     i=i, per=per)

            with sp.Fori(0, MH) as i:
                for k, (m0, m1) in enumerate(((0, 1), (2, 4))):
                    pairs(C0["hg_in"] + k, w_in2, [i * P + hg_at + m * MH * P for m in (m0, m1)], i, 2)
            with sp.Fori(0, MH) as i:
                for k in range(2):
                    columns(C0["ml_in"] + k, w_in2, i * P + k * MH * P, P, i=i, per=2)
            with sp.Fori(0, MH) as i:
                for k in range(2):
                    n = C0["ml_o"] + k
                    dst = ring[:, n % SLOTS, 0:DT // 2 * P].rearrange("p (k n) -> p k n", n=P)
                    src = w_in2[k * D // 2:(k + 1) * D // 2, ds(i * P + 3 * MH * P, P)].rearrange("(k p) n -> p k n", p=P)
                    load(n, (dst[:, 0:2], src[:, 0:2]), (dst[:, 2:4], src[:, 2:4]), i=i, per=2)
            whole("out2", a["w_out_2"][0], 4)
            with sp.Fori(0, F2T // 2) as i:
                for k in range(2):
                    pairs(C0["up2"] + k, a["w_up_2"][0], [i * (2 * P) + k * P + m * FF2 for m in range(2)], i, 2)
            with sp.Fori(0, 2) as i:
                for k in range(8):
                    n, kt = C0["down2"] + k, F2T // 2
                    dst = ring[:, n % SLOTS, 0:kt * P].rearrange("p (k n) -> p k n", n=P)
                    src = a["w_down_2"][0][k % 2 * kt * P:(k % 2 + 1) * kt * P, ds(i * (4 * P) + k // 2 * P, P)]
                    src = src.rearrange("(k p) n -> p k n", p=P)
                    load(n, (dst[:, 0:6], src[:, 0:6]), (dst[:, 6:kt], src[:, 6:kt]), i=i, per=8)
            out_v = out[0].rearrange("(t p) c -> p t c", p=P)
            for t in range(TT):
                for k in range(2):
                    copied(sp, T0["final"] + 2 * t + k)
                sp.dma_start(out_v[:, t], out_tok[:, t]).then_inc(stored, 16)
            sp.wait_ge(stored, 16 * TT)

        @block.gpsimd
        def _(pool):
            step = Steps(pool, pool_step)

            def select(out, op, fill, base, pattern, mult):
                return pool.affine_select(out=out, in_=out, compare_op=op, fill=fill, base=base,
                                          pattern=pattern, channel_multiplier=mult)

            pool.memset(mean_d[:], 1.0 / D).then_inc(consts, 1)
            pool.memset(eps[:], EPS).then_inc(consts, 1)
            step(pool.memset(ident[:], 0.0))
            select(ident[:], ALU.not_equal, 1.0, 0, [[-1, P]], 1).then_inc(consts, 1)
            step.mark(pool.iota(dist[:], pattern=[[-1, T]], base=T - P, channel_multiplier=1,
                                allow_small_or_imprecise_dtypes=True))
            step(pool.iota(cdist[:], pattern=[[P, TT], [-CMP_STRIDE, NCMP]], base=1 - CMP_BLOCK, channel_multiplier=1,
                           allow_small_or_imprecise_dtypes=True))
            select(dist[:], ALU.is_ge, FAR, T - P, [[-1, T]], 1).then_inc(consts, 1)
            select(cdist[:], ALU.is_ge, FAR, 1 - CMP_BLOCK, [[P, TT], [-CMP_STRIDE, NCMP]], 1).then_inc(consts, 1)
            for h in range(HEADS):
                pool.memset(negslope[:, h:h + 1], -2.0 ** -(8.0 * (h + 1) / HEADS)).then_inc(consts, 1)

            def cols(k):
                return s5[:, k].unsqueeze(2).to_broadcast([P, GROUPS, GROUP])

            def twist(out, re, im, x, y):
                t0, t1 = (ptmp[:, k].rearrange("p (g c) -> p g c", c=GROUP) for k in range(2))
                step.mark(pool.tensor_tensor(t0, cols(re), x, ALU.mult))
                step(pool.tensor_tensor(t1, cols(im), y, ALU.mult))
                return pool.tensor_tensor(out, t0, t1, ALU.add)

            pool.wait_ge(s5_bbar, 2)
            for k in range(STEP):
                step(twist(pows[:, :, STEP - 1 - k, :], PR + k, PI + k, ubar, vbar))
            copied(pool, T0["params"] + 3)
            copied(pool, T0["params"] + 2)
            for k in range(STEP):
                step(twist(ca[:, :, k, :], PR + k, PI + k, cu, cv))
            twist(ca[:, :, STEP, :], PR + STEP, PI + STEP, cu, cv).then_inc(ca_ready, 1)
            pool.wait_ge(ca_ready, 1)
            step.mark(pool.memset(rot_c[:, :, 0:1], 1.0))
            step.mark(pool.memset(rot_s[:, :, 0:1], 0.0))
            step.mark(pool.tensor_copy(rot_c[:, :, 1:2], s5[:, E8C].unsqueeze(2)))
            step(pool.tensor_copy(rot_s[:, :, 1:2], s5[:, E8S].unsqueeze(2)))
            m = 2
            while m < CHUNKS:
                half_c, half_s = rot_c[:, :, m // 2:m // 2 + 1], rot_s[:, :, m // 2:m // 2 + 1]
                wc, ws, t0, t1 = (s5[:, TMP + k].unsqueeze(2) for k in range(4))
                step.mark(pool.tensor_tensor(t0, half_c, half_c, ALU.mult))
                step.mark(pool.tensor_tensor(t1, half_s, half_s, ALU.mult))
                step(pool.tensor_tensor(ws, half_c, half_s, ALU.mult))
                step.mark(pool.tensor_tensor(wc, t0, t1, ALU.subtract))
                step(pool.tensor_tensor(ws, ws, ws, ALU.add))
                t0, t1 = (ptmp[:, k, 0:GROUPS * min(m, 16)].rearrange("p (g j) -> p g j", g=GROUPS) for k in range(2))
                for b in range(0, m, 16):
                    w = min(16, m)
                    shape = [P, GROUPS, w]
                    oc, os, ic, is_ = rot_c[:, :, m + b:m + b + w], rot_s[:, :, m + b:m + b + w], rot_c[:, :, b:b + w], rot_s[:, :, b:b + w]
                    step.mark(pool.tensor_tensor(t0, ic, wc.to_broadcast(shape), ALU.mult))
                    step(pool.tensor_tensor(t1, is_, ws.to_broadcast(shape), ALU.mult))
                    step(pool.tensor_tensor(oc, t0, t1, ALU.subtract))
                    step.mark(pool.tensor_tensor(t0, ic, ws.to_broadcast(shape), ALU.mult))
                    step(pool.tensor_tensor(t1, is_, wc.to_broadcast(shape), ALU.mult))
                    step(pool.tensor_tensor(os, t0, t1, ALU.add))
                m *= 2
            pool.tensor_scalar(rot_s, rot_s, sign[:], None, ALU.mult).then_inc(rot_ready, 1)

            for m in range(UT):
                copied(pool, T0["u"] + m)
            pool.dma_start(u_scr.rearrange("(m p) s j -> p m s j", p=P), u_st).then_inc(u_out, 16)
            pool.wait_ge(u_out, 16)
            pool.memset(toep, 0.0).then_inc(toep_zero, 1)
            copied(pool, T0["kernel"] + 7)
            copied(pool, T0["kernel"] + 6)
            copied(pool, T0["kernel"] + 5)
            copied(pool, T0["kernel"] + 4)
            pool.wait_ge(toep_zero, 1)
            for s in range(STEP):
                pool.dma_start(toep[s * GROUP:(s + 1) * GROUP, :, s * GROUP:P],
                               kern[0:GROUP, :, 0:P - s * GROUP]).then_inc(toep_in, 16)
            pool.wait_ge(toep_in, 16 * STEP)
            for s in range(STEP):
                pool.dma_start(uch[s * GROUP:(s + 1) * GROUP],
                               u_scr[:, s, :].rearrange("(g c) j -> c g j", c=GROUP)).then_inc(u_in, 16)
            for t in range(4):
                copied(pool, T0["state"] + t)
            pool.dma_start(e2[0:HD], e1[HD:P]).then_inc(e_swapped, 16)
            pool.dma_start(e2[HD:P], e1[0:HD]).then_inc(e_swapped, 16)
            pool.wait_ge(z_scanned, 1)
            pool.dma_start(z2[0:HD], zs[HD:P]).then_inc(z_swapped, 16)
            pool.dma_start(z2[HD:P], zs[0:HD]).then_inc(z_swapped, 16)
            pool.wait_ge(xprev_ready, 1)
            pool.dma_start(us, u_scr.rearrange("(m p) s j -> p m s j", p=P)).then_inc(y_in, 16)
            for m in range(2):
                pool.wait_ge(k_normed, 2 * m + 2)
                pool.dma_start(kk[HD:P, m, 0], kk[0:HD, m, 0]).then_inc(k_dup, 16)
                pool.dma_start(kk[0:HD, m, 1], kk[HD:P, m, 1]).then_inc(k_dup, 16)
            for t in range(4):
                copied(pool, T0["y"] + t)
            for s in range(STEP):
                pool.dma_start(y_scr[:, s, :].rearrange("(g c) j -> c g j", c=GROUP),
                               ych[s * GROUP:(s + 1) * GROUP]).then_inc(y_out, 16)
            pool.wait_ge(y_out, 16 * STEP)
            pool.dma_start(yT, y_scr.rearrange("(m p) s j -> p m s j", p=P)).then_inc(y_in, 16)
            pool.wait_ge(merged_ready, 2)
            pool.dma_start(ctx_tok, a["ctx_2"][0].rearrange("(t p) c -> p t c", p=P)).then_inc(ctx_in, 16)
            for k, b in enumerate(LEVELS):
                step(pool.memset(block_of, 1.0))
                grid = block_of.rearrange("p (g j) -> p g j", j=b)
                step(select(grid, ALU.is_ge, 0.0, 0, [[-b, P // b], [0, b]], 1))
                step(select(grid, ALU.is_ge, 0.0, b - 1, [[b, P // b], [0, b]], -1))
                pool.tensor_copy(same[:, k, :], block_of).then_inc(same_ready, 1)
                pool.wait_ge(same_ready, k + 1)
            pool.wait_ge(x1_ready, 2)
            pool.memset(ml_v[:, :, :, P:P + 1], 1.0).then_inc(ones_ready, 1)
            pool.wait_ge(g16_ready, 1)
            for k in range(4):
                row = (row_g, row_f)[k % 2]
                pool.dma_start(row[0:MH, k // 2, :], sq[k * MH:(k + 1) * MH].rearrange("p a n -> p (a n)")[:, 0:S])\
                  .then_inc(rows_in, 16)
            pool.wait_ge(rows_ready, 1)
            for d in range(2):
                pool.dma_start(m_scr[d], row_f[0:MH, d, C:S]).then_inc(max_out, 16)
            pool.wait_ge(max_out, 32)
            with pool.Fori(0, MH) as i:
                pool.wait_ge(sums_kept, i + 2)
                for u, m in enumerate(LEVELS):
                    full(pool, unit_tiles(u - 2)[0] if u >= 2 else unit_tiles(CONTEXT - u)[1] - 16, 16 * i)

                    def split(x):
                        return x.rearrange("p (a b t m) -> p a b t m", a=TT, t=2, m=m)

                    def upto(d, inclusive):
                        v = sums_v[:, ds(i, 1), d, CT:ST, inclusive:inclusive + P]
                        return v.rearrange("p o a (b t m) -> p (o a) b t m", t=2, m=m)

                    k_, q_ = split(ek[:, u % 2]), split(eq[:, u % 2])
                    half = [P, TT, P // (2 * m), m]
                    mid_f, mid_b = (upto(d, 0)[:, :, :, 1, 0:1].to_broadcast(half) for d in range(2))
                    pool.tensor_tensor(k_[:, :, :, 1], upto(1, 0)[:, :, :, 1], mid_b, ALU.subtract)
                    pool.tensor_tensor(k_[:, :, :, 0], mid_f, upto(0, 1)[:, :, :, 0], ALU.subtract)
                    pool.tensor_tensor(q_[:, :, :, 0], mid_b, upto(1, 0)[:, :, :, 0], ALU.subtract)
                    pool.tensor_tensor(q_[:, :, :, 1], upto(0, 1)[:, :, :, 1], mid_f, ALU.subtract)\
                        .then_inc(diff_ready, 1)
            pool.wait_ge(hg_done, MH)
            for d, sign_ in enumerate((1, -1)):
                step(pool.memset(causal[:, d], 1.0))
                step(select(causal[:, d], ALU.is_ge, 0.0, 0, [[sign_, P]], -sign_))
            with pool.Fori(0, MH) as i:
                pool.wait_ge(gap_ready, 2 * ST * (i + 1))
                for d in range(2):
                    pool.dma_start(cummax[:, d, :], m_scr[d, ds(i, 1), :].partition_broadcast(P)).then_inc(max_in, 16)
                for n in range(2 * TT):
                    b, d = divmod(n, 2)
                    if d == 0:
                        pool.wait_ge(p_ready, ST * i + CT + b + 1)
                    else:
                        copied(pool, T0["ml"] + 1 + CT + b, 2 * i)
                    w = weight[:, d, CT + b, b * P:(b + 1) * P]
                    pool.tensor_tensor(w, w, causal[:, d], ALU.mult).then_inc(p_masked, 1)
            free(pool, act2_ready, 2)
            with pool.Fori(0, F2T // 2) as i:
                for j in range(2):
                    pool.wait_ge(silu2_ready, 2 * i + j + 1)
                    pool.tensor_tensor(act2[:, ds(2 * i + j, 1), :], conv[:, 2 * j].unsqueeze(1),
                                       conv[:, 2 * j + 1].unsqueeze(1), ALU.mult).then_inc(act2_ready, 1)

        @block.tensor
        def _(pe):
            def claim(t, more=0):
                if t >= BANKS:
                    pe.wait_ge(acc_out[t % BANKS], t // BANKS + more)

            def arrived(n, more=0):
                pe.wait_ge(loaded[n % SLOTS], 32 * (n // SLOTS + 1) + 32 * more)

            def slot(n, k=DT):
                return ring[:, n % SLOTS, :].rearrange("p (k n) -> p k n", k=k)

            def flip(out, in_, rows=P):
                return pe.matmul(out, in_, ident[0:rows, 0:rows], is_transpose=True)

            def mean_square(ready, used, n):
                for k in range(DT):
                    pe.wait_ge(sq_ready, ready + k + 1)
                    pe.matmul(stat[:, 0:n], mean_d[:], sq[:, k % 2, 0:n], start=k == 0, stop=k == DT - 1)\
                      .then_inc(sq_used, 1)

            def linear(t, n, src, tiles=2, kt=DT, i=0, tile_rounds=0, slot_rounds=0, wait=None):
                arrived(n, i * slot_rounds)
                w = slot(n, kt)
                for m in range(tiles):
                    claim(t + m, i * tile_rounds)
                    for k in range(kt):
                        if wait is not None and m == 0:
                            pe.wait_ge(h_ready, wait + k + 1)
                        ins = pe.matmul(acc[(t + m) % BANKS][:], w[:, k, m * P:(m + 1) * P], src[:, k, :],
                                        start=k == 0, stop=k == kt - 1)
                        if m == 0 and k == 0 and n:
                            ins.then_inc(chunk_used, 1)
                    ins.then_inc(acc_full, 1)

            pe.wait_ge(consts, CONSTS)
            pe.wait_ge(params, 16 * len(param_loads))
            v = acc[0]
            flip(v[:, 0:P], vrows[:, 0, :])
            flip(v[:, VEC0:VEC1], vrows[0:VEC1 - VEC0, 1, :], VEC1 - VEC0)
            for k in range(3):
                ins = flip(v[:, VEC1 + 32 * k:VEC1 + 32 * (k + 1)], vrows[0:32, 2 + k, :], 32)
            ins.then_inc(acc_full, 1)
            for m in range(4):
                ins = flip(acc[1][:, 99 * m:99 * (m + 1)], frows[0:99, m, :], 99)
            ins.then_inc(acc_full, 1)
            for k in range(2):
                for m in range(UT):
                    ins = flip(acc[2 + k][:, m * P:(m + 1) * P], cn[:, k, m, :])
                ins.then_inc(acc_full, 1)
            pe.wait_ge(x_in, 16 * TT)
            for c in range(DT):
                t = T0["x"] + c
                claim(t)
                for m in range(TT):
                    ins = flip(acc[t % BANKS][:, m * P:(m + 1) * P], x_tok[:, m, c * P:(c + 1) * P])
                ins.then_inc(acc_full, 1)
            mean_square(0, 0, T)
            for n in range(7):
                linear(T0["u"] + 2 * n, n, hT, wait=0 if n == 0 else None)
            t = T0["gates"]
            claim(t)
            pe.wait_ge(w_small, 16 * len(small_loads))
            for m in range(TT):
                for k in range(DT):
                    ins = pe.matmul(acc[t % BANKS][:, 24 * m:24 * (m + 1)], hT[:, k, m * P:(m + 1) * P],
                                    w_gate[:, k, :], start=k == 0, stop=k == DT - 1)
            ins.then_inc(acc_full, 1)
            pe.wait_ge(ca_ready, 1)
            for m in range(8):
                t = T0["kernel"] + m
                claim(t)
                for g in range(4):
                    ins = pe.matmul(acc[t % BANKS][0:GROUP, g * P:(g + 1) * P], ubar[:, 4 * m + g, :],
                                    ca[:, 4 * m + g, 0:STEP, :], start=True, stop=True)
                ins.then_inc(acc_full, 1)
            for m in range(8):
                t = T0["bt"] + m
                claim(t)
                for g in range(4):
                    ins = flip(acc[t % BANKS][:, g * P:(g + 1) * P],
                               pows[:, 4 * m + g].rearrange("p s c -> p (s c)"))
                ins.then_inc(acc_full, 1)
            for m in range(2):
                copied(pe, T0["bt"] + 6 + m)
            pe.wait_ge(u_in, 16 * STEP)
            for m in range(4):
                t = T0["state"] + m
                claim(t)
                for g in range(8):
                    if g % 4 == 0:
                        copied(pe, T0["bt"] + 2 * m + g // 4)
                    ins = pe.matmul(acc[t % BANKS][:, g * CHUNKS:(g + 1) * CHUNKS], bt[:, 8 * m + g, :],
                                    uch[:, 8 * m + g, :], start=True, stop=True)
                ins.then_inc(acc_full, 1)
            for m in range(6):
                t = T0["qk_norm"] + m
                claim(t)
                pe.wait_ge(sq_ready, DT + m + 1)
                pe.matmul(acc[t % BANKS][:], mean_hd[:], sq[:, m % 2, :], start=True, stop=True).then_inc(acc_full, 1)
            for m in range(2):
                t = T0["v_tok"] + m
                claim(t)
                copied(pe, T0["kv"] + 3 + 2 * m)
                for b in range(TT):
                    ins = flip(acc[t % BANKS][:, b * P:(b + 1) * P], kvT[:, 3 + 2 * m, b * P:(b + 1) * P])
                ins.then_inc(acc_full, 1)
            r_half = CMP_BLOCK // 2
            for kind in range(2):
                copied(pe, T0["kv"] + kind)
                if kind:
                    pe.wait_ge(hid_ready, 2)
                own = slice(kind * HD, (kind + 1) * HD)
                for r in range(CMP_BLOCK):
                    n = C0["cmp"] + 2 * kind + r // r_half
                    if r % r_half == 0:
                        arrived(n)
                    w = ring[:, n % SLOTS, :].rearrange("p (r n) -> p r n", n=P)[:, r % r_half, :]
                    for g in range(KVG):
                        half = slice(g * HD, (g + 1) * HD)
                        ins = pe.matmul(banks[6 + g][:, 64 * kind:64 * kind + NCMP], w[half],
                                        kvT[half, kind, r:r + CMP_STRIDE * (NCMP - 1) + 1:CMP_STRIDE],
                                        start=r == 0, stop=r == CMP_BLOCK - 1)
                        if r % r_half == 0 and g == 0:
                            ins.then_inc(chunk_used, 1)
                    ins = pe.matmul(stat[:, kind:kind + 1], w[own], vec[own, VEC["pe"] + r:VEC["pe"] + r + 1],
                                    start=r == 0, stop=r == CMP_BLOCK - 1)
                ins.then_inc(hid_full, 1)
            pe.wait_ge(hid_ready, 4)
            pe.matmul(stat[:, 64:64 + KVG * NCMP], wk2[:].rearrange("p a n -> p (a n)"), hid[:, 0, 0:KVG * NCMP],
                      start=True, stop=True).then_inc(kc_full, 1)
            for g in range(KVG):
                ins = pe.matmul(banks[6][0:NCMP, g * HD:(g + 1) * HD], hid[:, 1, g * NCMP:(g + 1) * NCMP],
                                wv2[:], start=True, stop=True)
            ins.then_inc(vc_full, 1)
            pe.wait_ge(kc_sq, 1)
            pe.matmul(banks[7][:, 0:KVG * NCMP], mean_hd[:], knorm[:, 0:KVG * NCMP],
                      start=True, stop=True).then_inc(kc_mean, 1)
            pe.wait_ge(silu_ready, 2)
            with pe.Fori(0, 12) as i:
                for k in range(2):
                    n = C0["mod"] + k
                    arrived(n, i)
                    w = slot(n)
                    for m in range(2):
                        for kt in range(DT):
                            ins = pe.matmul(modp[:, ds(8 * i + 4 * k + 2 * m, 2)], w[:, kt, m * P:(m + 1) * P],
                                            silu_c[:, kt, :], start=kt == 0, stop=kt == DT - 1)
                            if m == 0 and kt == 0:
                                ins.then_inc(chunk_used, 1)
                    ins.then_inc(mod_full, 1)
            pe.wait_ge(toep_in, 16 * STEP)
            pe.wait_ge(xprev_ready, 1)
            for m in range(4):
                t = T0["y"] + m
                claim(t)
                for g in range(8):
                    o = acc[t % BANKS][:, g * CHUNKS:(g + 1) * CHUNKS]
                    pe.matmul(o, toep[:, 8 * m + g, :], uch[:, 8 * m + g, :], start=True, stop=False)
                    ins = pe.matmul(o, ca[:, 8 * m + g, 1:, :].rearrange("p s c -> p (s c)"), xprev[:, 8 * m + g, :],
                                    start=False, stop=True)
                ins.then_inc(acc_full, 1)
            pe.wait_ge(gelu_done, UT)
            linear(T0["glu"], C0["glu"], gelu_y, tiles=UT, kt=UT)

            pe.wait_ge(vc_ready, 1)
            for t in range(T0["y"] + 4, T0["glu"] + UT):
                copied(pe, t)
            copied(pe, T0["v_tok"])
            copied(pe, T0["v_tok"] + 1)
            QUERIES = HPG * TT
            with pe.Fori(0, KVG) as gi:
                def scores(n):
                    hg, tt = divmod(n, TT)
                    half = slice(hg % 2 * HD, (hg % 2 + 1) * HD)
                    q = qn[half, hg // 2, tt * P:(tt + 1) * P]
                    if tt == 0 and hg % 2 == 0:
                        pe.wait_ge(qn_ready, 5 * gi + hg // 2 + 4)
                    if n:
                        pe.wait_ge(score_ready, gi * QUERIES + n)
                    pe.matmul(stat[:, 0:NCMP], q, kcg[half],
                              start=True, stop=True)
                    for m in range(2):
                        ins = pe.matmul(banks[m][:, 0:(tt + 1) * P], q,
                                        kkg[half, m, 0:(tt + 1) * P],
                                        start=True, stop=True)
                    ins.then_inc(score_full, 1)

                scores(0)
                for n in range(QUERIES):
                    tt = n % TT
                    if n + 1 < QUERIES:
                        scores(n + 1)
                    pe.wait_ge(prob_ready, gi * QUERIES + n + 1)
                    for m in range(2):
                        for b in range(tt + 1):
                            flip(banks[5 + m][:, b * P:(b + 1) * P], prob[:, n % 2, m, b * P:(b + 1) * P])
                    pe.wait_ge(cprob_ready, gi * QUERIES + n + 1)
                    flip(banks[3][0:NCMP, 0:P], cprob[:, n % 2, :]).then_inc(pt_full, 1)
                    pe.wait_ge(pt_out, gi * QUERIES + n + 1)
                    pe.wait_ge(cpt_out, gi * QUERIES + n + 1)
                    if n >= 2:
                        pe.wait_ge(o_ready, gi * QUERIES + n - 1)
                    o = banks[(2, 7)[n % 2]][:, 0:3 * HD]
                    for m in range(2):
                        for b in range(tt + 1):
                            pe.matmul(o[:, (m + 1) * HD:(m + 2) * HD], probT[:, n % 2, m, b * P:(b + 1) * P],
                                      v_tok[:, m, b, ds(gi * HD, HD)], start=b == 0, stop=b == tt)
                    pe.matmul(o[:, 0:HD], cprobT[0:NCMP, n % 2, :], vc[0:NCMP, ds(gi, 1), :].rearrange("p a n -> p (a n)"),
                              start=True, stop=True).then_inc(o_full, 1)
                pe.wait_ge(o_ready, gi * QUERIES + QUERIES)
            for c in range(4):
                t = T0["o_nsa"] + c
                claim(t)
                for m in range(TT):
                    ins = flip(acc[t % BANKS][:, m * P:(m + 1) * P], o_tok[:, m, c * P:(c + 1) * P])
                ins.then_inc(acc_full, 1)
            pe.wait_ge(yssm_ready, UT)
            for c in range(4):
                copied(pe, T0["o_nsa"] + c)
            with pe.Fori(0, DT) as i:
                for m in range(2):
                    n = C0["merge"] + m
                    arrived(n, i)
                    w = ring[:, n % SLOTS, 0:12 * P].rearrange("p (k n) -> p k n", n=P)
                    for j, (at, kt, src) in enumerate(((0, DT, hT), (DT, 4, (y_ssm, y_nsa)[m]))):
                        t = T0["merge"] + 2 * m + j
                        claim(t, i)
                        for k in range(kt):
                            ins = pe.matmul(acc[t % BANKS][:], w[:, at + k, :], src[:, k, :], start=k == 0, stop=k == kt - 1)
                            if j == 0 and k == 0:
                                ins.then_inc(chunk_used, 1)
                        ins.then_inc(acc_full, 1)

            def looped(name, src, rounds):
                with pe.Fori(0, rounds) as i:
                    for k in range(2):
                        linear(T0[name] + 2 * k, C0[name] + k, src, i=i, tile_rounds=1, slot_rounds=1)

            pe.wait_ge(merged_ready, DT + 1)
            looped("out1", merged, 2)
            mean_square(DT + 6, DT, T)
            pe.wait_ge(h_ready, 2 * DT)
            looped("up1", hT, 8)
            pe.wait_ge(act_ready, FT + 4)

            with pe.Fori(0, 2) as i:
                for mp in range(2):
                    for c in range(4):
                        n = C0["down1"] + 4 * mp + c
                        arrived(n, 4 * i)
                        w = slot(n)
                        for m in range(2):
                            t = T0["down1"] + 2 * mp + m
                            if c == 0:
                                claim(t, i)
                            for k in range(DT):
                                ins = pe.matmul(acc[t % BANKS][:], w[:, k, m * P:(m + 1) * P], act[:, c * DT + k, :],
                                                start=c == 0 and k == 0, stop=c == 3 and k == DT - 1)
                                if m == 0 and k == 0:
                                    ins.then_inc(chunk_used, 1)
                            if c == 3:
                                ins.then_inc(acc_full, 1)
            pe.wait_ge(ctx_in, 16)
            for c in range(4):
                t = T0["ctx"] + c
                claim(t)
                for k in range(2):
                    for m in range(CT):
                        ins = flip(acc[t % BANKS][:, k * C + m * P:k * C + (m + 1) * P],
                                   ctx_tok[:, m, (2 * c + k) * P:(2 * c + k + 1) * P])
                ins.then_inc(acc_full, 1)
            norms = DT + 6 + DT
            mean_square(norms, 2 * DT, C)
            pe.wait_ge(rstd_ready, 3)
            mean_square(norms + DT, 3 * DT, T)
            pe.wait_ge(h_ready, 4 * DT)
            for m, src in enumerate((hT, hcT)):
                t, n = T0["gate_rows"] + m, (T, C)[m]
                claim(t)
                for k in range(DT):
                    ins = pe.matmul(acc[t % BANKS][0:4 * MH, 0:n], w_mgate[:, k, :], src[:, k, 0:n],
                                    start=k == 0, stop=k == DT - 1)
                ins.then_inc(acc_full, 1)
            for m in range(2):
                n = C0["v2"] + 2 * m
                arrived(n)
                for b in range(ST):
                    t = T0["v2"] + ST * m + b
                    claim(t)
                    for k in range(DT):
                        if (b, k) == (0, DT // 2):
                            arrived(n + 1)
                        src = hcT[:, k, b * P:(b + 1) * P] if b < CT else hT[:, k, (b - CT) * P:(b - CT + 1) * P]
                        w = ring[:, (n + k // 4) % SLOTS, :].rearrange("p (k n) -> p k n", k=DT // 2)[:, k % 4, :]
                        ins = pe.matmul(acc[t % BANKS][:], src, w, start=k == 0, stop=k == DT - 1)
                        if (b, k) in ((0, 0), (ST - 1, DT // 2)):
                            ins.then_inc(chunk_used, 1)
                    ins.then_inc(acc_full, 1)
            t = T0["gate_cols"]
            claim(t)
            pe.wait_ge(rows_ready, 1)
            for d in range(2):
                for b in range(ST):
                    at = (d * ST + b) * MH
                    flip(acc[t % BANKS][:, at:at + MH], row_g[0:MH, d, b * P:(b + 1) * P], MH)
                for b in range(TT):
                    at = (2 * ST + d * TT + b) * MH
                    ins = flip(acc[t % BANKS][:, at:at + MH], row_b[0:MH, d, C + b * P:C + (b + 1) * P], MH)
            ins.then_inc(acc_full, 1)

            with pe.Fori(0, MH) as i:
                t = T0["hg_in"]
                for c in range(2):
                    n = C0["hg_in"] + c
                    arrived(n, i)
                    w = ring[:, n % SLOTS, :].rearrange("p (m k n) -> p m k n", m=2, k=DT)
                    for m in range(2):
                        b = t + 2 * c + m
                        claim(b, i)
                        for k in range(DT):
                            ins = pe.matmul(acc[b % BANKS][:], w[:, m, k, :], hT[:, k, :], start=k == 0, stop=k == DT - 1)
                            if m == 0 and k == 0:
                                ins.then_inc(chunk_used, 1)
                        ins.then_inc(acc_full, 1)
                        if m != c:
                            if c == 0:
                                pe.wait_ge(z_ready, i + 1)
                            for k in range(DT):
                                ins = pe.matmul(banks[5][:, c * C:(c + 1) * C], w[:, m, k, :], hcT[:, k, :],
                                                start=k == 0, stop=k == DT - 1)
                            ins.then_inc(z_ctx, 1)
            for b in range(ST):
                copied(pe, T0["v2"] + b)
            with pe.Fori(0, MH) as i:
                t = T0["hg"]
                for m, (c, src) in enumerate(((0, hT), (1, hT), (1, hcT))):
                    n = C0["ml_in"] + c
                    if m < 2:
                        arrived(n, i)
                    w = ring[:, n % SLOTS, 0:DT * P].rearrange("p (k n) -> p k n", k=DT)
                    claim(t + m, 4 * i)
                    cols = C if m == 2 else T
                    for k in range(DT):
                        ins = pe.matmul(acc[(t + m) % BANKS][:, 0:cols], w[:, k, :], src[:, k, :],
                                        start=k == 0, stop=k == DT - 1)
                        if m < 2 and k == 0:
                            ins.then_inc(chunk_used, 1)
                    ins.then_inc(acc_full, 1)
                for u in range(UNITS):
                    tiles = unit_tiles(u)
                    for b in tiles:
                        claim(b, 4 * i)
                    pe.wait_ge(kq_ready, UNITS * i + u + 1)
                    o = [acc[b % BANKS] for b in tiles]
                    k_, q_ = ek[:, u % 2, :], eq[:, u % 2, :]
                    for s in range(TT):
                        ks = k_[:, s * P:(s + 1) * P]
                        if u <= PAIRS:
                            other = s if u < PAIRS else s ^ 1
                            ins = pe.matmul(o[0][:, s * P:(s + 1) * P], ks, q_[:, other * P:(other + 1) * P],
                                            start=True, stop=True)
                        elif u == HALVES:
                            other = C if s < 2 else 0
                            ins = pe.matmul(o[s // 2][:, s % 2 * C:(s % 2 + 1) * C], ks, q_[:, other:other + C],
                                            start=True, stop=True)
                            if s % 2:
                                ins.then_inc(acc_full, 1)
                        else:
                            c, d = divmod(s, 2)
                            ins = pe.matmul(o[c][:], k_[:, d * C + c * P:d * C + (c + 1) * P], (q_, eq_b[:])[d],
                                            start=d == 0, stop=d == 1)
                            if d:
                                ins.then_inc(acc_full, 1)
                    if u <= PAIRS:
                        ins.then_inc(acc_full, 1)
                for b in range(16 - BANKS, 16):
                    copied(pe, t + b, 4 * i)
                for b in range(TT):
                    for s in range(ST):
                        if s < CT:
                            w = a_ctx[:, s, b * P:(b + 1) * P]
                        elif s - CT == b:
                            w = a_own[:, b, :]
                        elif s - CT == b ^ 1:
                            w = a_pair[:, s - CT, :]
                        else:
                            w = a_half[:, s - CT, b % 2 * P:(b % 2 + 1) * P]
                        ins = pe.matmul(banks[4][:, b * P:(b + 1) * P], w,
                                        hg_v[:, s, ds(i * P, P)], start=s == 0, stop=s == ST - 1)
                ins.then_inc(hg_o, 1)
                pe.wait_ge(hg_y, i + 1)
                for b in range(TT):
                    ins = flip(banks[6][:, b * P:(b + 1) * P], y_tok[:, b, :])
                ins.then_inc(hg_flipped, 1)
            pe.wait_ge(hg_done, MH)
            for b in range(ST):
                copied(pe, T0["v2"] + ST + b)
            pe.wait_ge(ones_ready, 1)
            with pe.Fori(0, MH) as i:
                t = T0["ml"]
                claim(t, 2 * i)
                for c in range(2):
                    n = C0["ml_o"] + c
                    arrived(n, i)
                    w = ring[:, n % SLOTS, 0:DT // 2 * P].rearrange("p (k n) -> p k n", n=P)
                    for k in range(DT // 2):
                        ins = pe.matmul(acc[t % BANKS][:], w[:, k, :], hT[:, c * DT // 2 + k, :],
                                        start=c == 0 and k == 0, stop=c == 1 and k == DT // 2 - 1)
                        if k == 0:
                            ins.then_inc(chunk_used, 1)
                ins.then_inc(acc_full, 1)
                pe.wait_ge(qk_ready, 3 * i + 3)
                for s in range(ST):
                    b = t + 1 + s
                    claim(b, 2 * i)
                    pe.matmul(acc[b % BANKS][:], kc2[:, s * P:(s + 1) * P], qc, start=True, stop=True).then_inc(acc_full, 1)
                pe.wait_ge(p_ready, ST * (i + 1))
                for s in range(ST - BANKS, ST):
                    copied(pe, t + 1 + s, 2 * i)
                pe.wait_ge(p_masked, 2 * TT * (i + 1))
                for b in range(TT):
                    for d in range(2):
                        srcs = [s for s in range(ST) if s < CT or (s - CT <= b if d == 0 else s - CT >= b)]
                        for s in srcs:
                            ins = pe.matmul(banks[4 + b][:, d * (P + 1):(d + 1) * (P + 1)],
                                            weight[:, d, s, b * P:(b + 1) * P],
                                            ml_v[:, s, ds(i, 1), :].rearrange("p o n -> p (o n)"),
                                            start=s == srcs[0], stop=s == srcs[-1])
                    ins.then_inc(ml_o, 1)
                claim(t + 7, 2 * i)
                pe.wait_ge(ml_y, i + 1)
                for b in range(TT):
                    ins = flip(acc[(t + 7) % BANKS][:, b * P:(b + 1) * P], h_tok[:, b, :])
                ins.then_inc(acc_full, 1)
            for b in range(MH * 8 - 4, MH * 8):
                copied(pe, T0["ml"] + b)
            looped("out2", y_all, 2)
            mean_square(norms + 2 * DT, 4 * DT, T)
            pe.wait_ge(h_ready, 5 * DT)
            with pe.Fori(0, F2T // 2) as i:
                for j in range(2):
                    n = C0["up2"] + j
                    arrived(n, i)
                    w = ring[:, n % SLOTS, :].rearrange("p (m k n) -> p m k n", m=2, k=DT)
                    for m in range(2):
                        t = T0["up2"] + 2 * j + m
                        claim(t, i)
                        for k in range(DT):
                            ins = pe.matmul(acc[t % BANKS][:], w[:, m, k, :], hT[:, k, :], start=k == 0, stop=k == DT - 1)
                            if m == 0 and k == 0:
                                ins.then_inc(chunk_used, 1)
                        ins.then_inc(acc_full, 1)
            pe.wait_ge(act2_ready, F2T + 2)
            with pe.Fori(0, 2) as i:
                for m in range(4):
                    t = T0["down2"] + m
                    claim(t, i)
                    for c in range(2):
                        n, kt = C0["down2"] + 2 * m + c, F2T // 2
                        arrived(n, 4 * i)
                        w = ring[:, n % SLOTS, 0:kt * P].rearrange("p (k n) -> p k n", n=P)
                        for k in range(kt):
                            ins = pe.matmul(acc[t % BANKS][:], w[:, k, :], act2[:, c * kt + k, :],
                                            start=c == 0 and k == 0, stop=c == 1 and k == kt - 1)
                            if k == 0:
                                ins.then_inc(chunk_used, 1)
                    ins.then_inc(acc_full, 1)
            mean_square(norms + 3 * DT, 5 * DT, T)
            pe.wait_ge(out_ready, DT)
            for t in range(TT):
                for k in range(2):
                    b = T0["final"] + 2 * t + k
                    claim(b)
                    for c in range(4):
                        ins = flip(acc[b % BANKS][:, c * P:(c + 1) * P], hT[:, 4 * k + c, t * P:(t + 1) * P])
                    ins.then_inc(acc_full, 1)

        @block.scalar
        def _(sc):
            step = Steps(sc, act_step)

            def squares(src, n, used):
                for k in range(DT):
                    if used + k >= 2:
                        sc.wait_ge(sq_used, used + k - 1)
                    sc.activation(sq[:, k % 2, 0:n], src[:, k, 0:n], ACT.Square).then_inc(sq_ready, 1)

            def inverse_root(dst, src):
                step(sc.activation(dst, src, ACT.Ln, bias=eps[0:dst.shape[0]]))
                return sc.activation(dst, dst, ACT.Exp, scale=-0.5)

            for dst, src in param_loads:
                sc.dma_start(dst, src).then_inc(params, 16)
            for dst, src in small_loads:
                sc.dma_start(dst, src).then_inc(w_small, 16)
            sc.wait_ge(consts, CONSTS)
            full(sc, 0)
            out_of(0, sc.copy(vec[:], acc[0][:, 0:VEC_COLS]))
            full(sc, 1)
            out_of(1, sc.copy(ffn_taps[:], acc[1][:, 0:TAPS * 2 * F2T]))
            full(sc, 2)
            out_of(2, sc.mul(cu.rearrange("p g c -> p (g c)"), acc[2][:], sign[:]))
            full(sc, 3)
            out_of(3, sc.mul(cv.rearrange("p g c -> p (g c)"), acc[3][:], -1.0))
            sc.wait_ge(params, 16 * len(param_loads))
            sc.activation(s5[:, DT_], s5[:, LOG_DT], ACT.Exp).then_inc(s5_exp, 1)
            for c in range(DT):
                t = T0["x"] + c
                full(sc, t)
                out_of(t, sc.copy(xT[:, c, :], acc[t % BANKS][:]))
            for c in range(BANKS):
                copied(sc, T0["x"] + DT - BANKS + c)
            squares(xT, T, 0)
            sc.wait_ge(sq_used, DT)
            inverse_root(rstd[:], stat[:]).then_inc(rstd_ready, 1)
            sc.wait_ge(s5_small, 1)
            sc.activation(s5[:, MAG], s5[:, AR_DT], ACT.Exp).then_inc(s5_exp, 1)
            sc.activation(s5[:, MAG_STEP], s5[:, AR_DT], ACT.Exp, scale=float(STEP)).then_inc(s5_exp, 1)
            sc.wait_ge(s5_angle, 1)
            sc.activation(s5[:, SIN_H], s5[:, ANGLE], ACT.Sin, scale=0.5).then_inc(s5_sin, 1)
            sc.activation(s5[:, SIN], s5[:, ANGLE], ACT.Sin).then_inc(s5_sin, 1)
            copied(sc, 0)
            for k, name in enumerate(("c_2", "c_ctx_2")):
                sc.activation(silu_c[:, :, k], vec[:, VEC[name]:VEC[name] + DT], ACT.Silu).then_inc(silu_ready, 1)
            for m in range(UT):
                t = T0["u"] + m
                full(sc, t)
                out_of(t, sc.copy(u_st[:, m], acc[t % BANKS][:].rearrange("p (j s) -> p s j", s=STEP)))
            for m in range(4):
                t = T0["q"] + m
                full(sc, t)
                out_of(t, sc.copy(qT[:, m, :], acc[t % BANKS][:]))
            for m in range(6):
                t = T0["kv"] + m
                full(sc, t)
                out_of(t, sc.copy(kvT[:, m, :], acc[t % BANKS][:]))
            t = T0["gates"]
            full(sc, t)
            out_of(t, sc.activation(gsig.rearrange("p t n -> p (t n)"), acc[t % BANKS][:, 0:TT * 3 * HEADS], ACT.Sigmoid))
            sc.wait_ge(s5_bbar, 2)
            for m in range(8):
                t = T0["kernel"] + m
                full(sc, t)
                out_of(t, sc.copy(kern[0:GROUP, 4 * m:4 * (m + 1)].rearrange("p g n -> p (g n)"), acc[t % BANKS][0:GROUP, :]))
            for m in range(4):
                t = T0["state"] + m
                full(sc, t)
                out_of(t, sc.copy(e1[:, 8 * m:8 * (m + 1)].rearrange("p g j -> p (g j)"), acc[t % BANKS][:]))
            for m in range(4):
                copied(sc, T0["q"] + m)
            for m in range(2, 6):
                copied(sc, T0["kv"] + m)

            def qk_root(m):
                t = T0["qk_norm"] + m
                full(sc, t)
                if m >= 2:
                    sc.wait_ge(qk_rstd, m - 1)
                step(sc.activation(root[:, m % 2, :], acc[t % BANKS][:], ACT.Ln, bias=eps[:]))
                sc.activation(root[:, m % 2, :], root[:, m % 2, :], ACT.Exp, scale=-0.5).then_inc(qk_sq, 1)

            sc.wait_ge(sq_used, DT)
            for m in range(6):
                src = qT[:, m, :] if m < 4 else kvT[:, 2 * (m - 3), :]
                if m >= 2:
                    full(sc, T0["qk_norm"] + m - 2)
                sc.activation(sq[:, m % 2, :], src, ACT.Square).then_inc(sq_ready, 1)
                if m >= 1:
                    qk_root(m - 1)
            qk_root(5)
            for m in range(2):
                t = T0["v_tok"] + m
                full(sc, t)
                out_of(t, sc.copy(v_tok[:, m].rearrange("p b n -> p (b n)"), acc[t % BANKS][:]))
            for kind in range(2):
                sc.wait_ge(hid_full, kind + 1)
                step(sc.copy(hbias[:, kind:kind + 1], stat[:, kind:kind + 1]))
                for g in range(KVG):
                    sc.activation(hid[:, kind, g * NCMP:(g + 1) * NCMP], banks[6 + g][:, 64 * kind:64 * kind + NCMP],
                                  ACT.Gelu_apprx_tanh, bias=hbias[:, kind:kind + 1]).then_inc(hid_ready, 1)
            n = KVG * NCMP
            sc.wait_ge(kc_full, 1)
            sc.activation(knorm[:, 0:n], stat[:, 64:64 + n], ACT.Square).then_inc(kc_sq, 1)
            sc.wait_ge(vc_full, 1)
            sc.copy(vc[0:NCMP].rearrange("p g n -> p (g n)"), banks[6][0:NCMP, 0:P]).then_inc(vc_ready, 1)
            sc.wait_ge(kc_mean, 1)
            inverse_root(knorm[:, 0:n], banks[7][:, 0:n]).then_inc(kc_sq, 1)
            sc.wait_ge(xprev_ready, 1)
            for m in range(4):
                t = T0["y"] + m
                full(sc, t)
                out_of(t, sc.copy(ych[:, 8 * m:8 * (m + 1)].rearrange("p g j -> p (g j)"), acc[t % BANKS][:]))
            for m in range(UT):
                sc.wait_ge(y_sum, m + 1)
                sc.activation(gelu_y[:, m, :].rearrange("p (j s) -> p s j", s=STEP), yT[:, m], ACT.Gelu_apprx_tanh)\
                  .then_inc(gelu_done, 1)
            sc.wait_ge(gelu_done, UT)
            for m in range(UT):
                t = T0["glu"] + m
                full(sc, t)
                out_of(t, sc.activation(yT[:, m].rearrange("p s j -> p (s j)"), acc[t % BANKS][:], ACT.Sigmoid,
                                        bias=vcol("ssm_b_glu", m)))
            QUERIES = HPG * TT
            with sc.Fori(0, KVG) as gi:
                def exps(n):
                    w = (n % TT + 1) * P
                    st = stats[:, n % 2]
                    sc.wait_ge(score_ready, gi * QUERIES + n + 1)
                    if n >= 2:
                        sc.wait_ge(pt_full, gi * QUERIES + n - 1)
                    sc.activation(cprob[:, n % 2, :], cscore[:, n % 2, :], ACT.Exp, bias=st[:, 3:4], accum_out=st[:, 6:7])
                    for m in range(2):
                        ins = sc.activation(prob[:, n % 2, m, 0:w], score[:, n % 2, m, 0:w], ACT.Exp,
                                            bias=st[:, 4 + m:5 + m], accum_out=st[:, 7 + m:8 + m])
                    ins.then_inc(prob_ready, 1)

                exps(0)
                for n in range(QUERIES):
                    w = (n % TT + 1) * P
                    if n + 1 < QUERIES:
                        exps(n + 1)
                    sc.wait_ge(pt_full, gi * QUERIES + n + 1)
                    if n >= 2:
                        sc.wait_ge(o_full, gi * QUERIES + n - 1)
                    sc.copy(cprobT[0:NCMP, n % 2, :], banks[3][0:NCMP, 0:P])
                    sc.copy(probT[:, n % 2, 1, 0:w], banks[6][:, 0:w]).then_inc(pt_out, 1)
                sc.wait_ge(o_full, gi * QUERIES + QUERIES)
            for c in range(4):
                t = T0["o_nsa"] + c
                full(sc, t)
                out_of(t, sc.copy(y_nsa[:, c, :], acc[t % BANKS][:]))
            with sc.Fori(0, DT) as i:
                sc.wait_ge(merged_ready, i + 1)
                for m in range(2):
                    t = T0["merge"] + 2 * m
                    full(sc, t, 4 * i)
                    out_of(t, sc.activation(sig[:, m, :], acc[t % BANKS][:], ACT.Sigmoid))
            sc.wait_ge(x1_ready, 1)
            squares(xT, T, DT)
            sc.wait_ge(sq_used, 2 * DT)
            inverse_root(rstd[:], stat[:]).then_inc(rstd_ready, 1)
            with sc.Fori(0, FT // 4) as i:
                sc.wait_ge(act_ready, 4 * i + 4)
                for k in range(4):
                    t = T0["up1"] + k
                    full(sc, t, 4 * i)
                    out_of(t, sc.activation(relu[:, k, :], acc[t % BANKS][:], ACT.Relu))
            sc.wait_ge(lb_logit, 1)
            sc.activation(lb[:, 0], lb[:, 2], ACT.Sigmoid, scale=-1.0).then_inc(lb_sig, 1)
            sc.activation(lb[:, 1], lb[:, 2], ACT.Sigmoid).then_inc(lb_sig, 1)
            for c in range(4):
                t = T0["ctx"] + c
                full(sc, t)
                out_of(t, sc.copy(xcT[:, 2 * c:2 * c + 2].rearrange("p k n -> p (k n)"), acc[t % BANKS][:]))
            for c in range(4):
                copied(sc, T0["ctx"] + c)
            squares(xcT, C, 2 * DT)
            sc.wait_ge(sq_used, 3 * DT)
            inverse_root(root[:, 0, 0:C], stat[:, 0:C]).then_inc(rstd_ready, 1)
            sc.wait_ge(x1_ready, 2)
            squares(xT, T, 3 * DT)
            sc.wait_ge(sq_used, 4 * DT)
            inverse_root(rstd[:], stat[:]).then_inc(rstd_ready, 1)

            def shifted(dst, shift, col, scaled):
                for c in range(DT):
                    sc.wait_ge(h_scaled, scaled + c + 1)
                    sc.activation(dst[:, c, :], dst[:, c, :], ACT.Identity, bias=mod[:, shift * DT + c, col:col + 1])\
                      .then_inc(h_ready, 1)

            sc.wait_ge(mod_ready, 1)
            shifted(hcT, 0, 1, 0)
            shifted(hT, 0, 0, DT)
            for m in range(2):
                t, n = T0["gate_rows"] + m, (T, C)[m]
                full(sc, t)
                g16 = sq[0:4 * MH].rearrange("p a n -> p (a n)")[:, C * (1 - m):C * (1 - m) + n]
                out_of(t, sc.activation(g16, acc[t % BANKS][0:4 * MH, 0:n], ACT.Identity, bias=mgate_b[:]))
            for m in range(2):
                copied(sc, T0["gate_rows"] + m)
            free(sc, g16_ready)
            sc.wait_ge(neg_ready, 1)
            step(sc.activation(row_b[0:MH], row_b[0:MH], ACT.Exp))
            sc.activation(row_b[0:MH], row_b[0:MH], ACT.Ln, bias=1.0).then_inc(ln_ready, 1)
            for m in range(2):
                for b in range(ST):
                    t = T0["v2"] + ST * m + b
                    full(sc, t)
                    if m == 0:
                        out_of(t, sc.copy(hg_v[:, b, :], acc[t % BANKS][:]))
                    else:
                        out_of(t, sc.copy(ml_v[:, b, :, 0:P], acc[t % BANKS][:].rearrange("p (h n) -> p h n", n=P)))
            t, n = T0["gate_cols"], 2 * ST * MH
            full(sc, t)
            sc.copy(gcol.rearrange("p d b h -> p (d b h)"), acc[t % BANKS][:, 0:n]).then_inc(cols_ready, 1)
            out_of(t, sc.activation(floor.rearrange("p d b h -> p (d b h)"), acc[t % BANKS][:, n:n + 2 * TT * MH],
                                    ACT.Exp, scale=-1.0))
            sc.wait_ge(max_out, 32)
            copied(sc, t)
            free(sc, z_ready)
            free(sc, sums_kept)
            with sc.Fori(0, MH) as i:
                t = T0["hg_in"]

                def bank(k):
                    return acc[(t + k) % BANKS][:]

                full(sc, t, 4 * i)
                out_of(t, sc.activation(hg_q[:, ds(i, 1), :], bank(0).unsqueeze(1), ACT.Silu))
                for d in range(2):
                    full(sc, t + 1 + d, 4 * i)
                    sc.activation(logf[:, d, CT:, 1:], bank(1 + d).rearrange("p (b n) -> p b n", n=P), ACT.Sigmoid)
                    out_of(t + 1 + d, sc.activation(hg_k[:, ds(i, 1), d, C:], bank(1 + d).unsqueeze(1), ACT.Sigmoid,
                                                    scale=-1.0))
                sc.wait_ge(z_ctx, 2 * i + 2)
                z = banks[5][:].rearrange("p (d n) -> p d n", d=2)
                for d in range(2):
                    sc.activation(logf[:, d, 0:CT, 1:], z[:, d].rearrange("p (b n) -> p b n", n=P), ACT.Sigmoid)
                for d in range(2):
                    ins = sc.activation(hg_k[:, ds(i, 1), d, 0:C], z[:, d].unsqueeze(1), ACT.Sigmoid, scale=-1.0)
                ins.then_inc(z_ready, 1)
                full(sc, t + 3, 4 * i)
                out_of(t + 3, sc.activation(hg_g[:, ds(i, 1), :], bank(3).unsqueeze(1), ACT.Silu))
                for d in range(2):
                    sc.wait_ge(f_ready, 2 * i + d + 1)
                    sc.activation(logf[:, d, :, 1:], logf[:, d, :, 1:], ACT.Ln).then_inc(logf_ready, 1)
                sc.wait_ge(sums_ready, i + 1)
                sc.copy(sums[:, ds(i, 1), :], sums1.unsqueeze(1)).then_inc(sums_kept, 1)
            sc.wait_ge(sums_kept, MH + 1)
            with sc.Fori(0, MH) as i:
                t = T0["hg"]

                def upto(d, b, inclusive, n=1, by=1):
                    return sums_v[:, ds(i, 1), d, b:b + (n - 1) * by + 1:by, inclusive:inclusive + P]\
                        .rearrange("p o a n -> p (o a) n")

                def total(d, b):
                    return sums_v[:, ds(i, 1), d, b, P:P + 1].rearrange("p o n -> p (o n)")

                def over(k):
                    return sums[:, ds(i, 1), k:k + 1].rearrange("p o n -> p (o n)")

                def decay(dst, x, bias=None, sign=1):
                    dst = dst.rearrange("p (a n) -> p a n", n=P) if len(dst.shape) == 2 else dst
                    if bias is None:
                        return sc.activation(dst, x, ACT.Exp, scale=float(sign))
                    return sc.activation(dst, x, ACT.Exp, scale=float(sign), bias=bias)

                def exps(u):
                    k_, q_ = ek[:, u % 2, :], eq[:, u % 2, :]
                    ks, qs = ([x[:, s * P:(s + 1) * P] for s in range(TT)] for x in (k_, q_))
                    if u < DIAG:
                        sc.wait_ge(diff_ready, DIAG * i + u + 1)
                        sc.activation(k_, k_, ACT.Exp)
                        sc.activation(q_, q_, ACT.Exp).then_inc(exp_ready, 1)
                        return
                    full(sc, unit_tiles(u - 2)[-1], 16 * i)
                    if u == PAIRS:
                        for s in (0, 2):
                            decay(ks[s], upto(0, CT + s, 1), total(0, CT + s), -1)
                            decay(qs[s], upto(1, CT + s, 0), total(1, CT + s), -1)
                        odd = [x.rearrange("p (a t n) -> p a t n", t=2, n=P)[:, :, 1] for x in (k_, q_)]
                        decay(odd[0], upto(1, CT + 1, 0, 2, 2))
                        ins = decay(odd[1], upto(0, CT + 1, 1, 2, 2))
                    elif u == HALVES:
                        decay(ks[0], upto(0, CT, 1), over(PRE_F + 1), -1)
                        decay(ks[1], upto(0, CT + 1, 1), total(0, CT + 1), -1)
                        decay(ks[2], upto(1, CT + 2, 0))
                        decay(ks[3], upto(1, CT + 3, 0), total(1, CT + 2))
                        decay(qs[0], upto(1, CT, 0), over(PRE_B + 1), -1)
                        decay(qs[1], upto(1, CT + 1, 0), total(1, CT + 1), -1)
                        decay(qs[2], upto(0, CT + 2, 1))
                        ins = decay(qs[3], upto(0, CT + 3, 1), total(0, CT + 2))
                    else:
                        decay(ks[0], upto(0, 0, 1), over(CTX_F + 1), -1)
                        decay(ks[1], upto(0, 1, 1), total(0, 1), -1)
                        decay(ks[2], upto(1, 0, 0))
                        decay(ks[3], upto(1, 1, 0), total(1, 0))
                        for s in range(TT):
                            decay(qs[s], upto(0, CT + s, 1), over(PRE_F + s - 1) if s else None)
                            ins = decay(eq_b[:, s * P:(s + 1) * P], upto(1, CT + s, 0), over(SUF_B + s), -1)
                    ins.then_inc(exp_ready, 1)

                exps(0)
                exps(1)
                for m in range(3):
                    full(sc, t + m, 16 * i)
                    dst = (ml_q[:, ds(i, 1), :], ml_k[:, ds(i, 1), C:], ml_k[:, ds(i, 1), 0:C])[m]
                    out_of(t + m, sc.copy(dst, acc[(t + m) % BANKS][:, 0:(T, T, C)[m]].unsqueeze(1)))
                for u in range(2, DIAG):
                    exps(u)
                exps(PAIRS)
                exps(HALVES)

                def weights(b, dst):
                    full(sc, b, 16 * i)
                    out_of(b, sc.copy(dst.rearrange("p s n -> p (s n)") if len(dst.shape) == 3 else dst, acc[b % BANKS][:]))

                weights(unit_tiles(PAIRS)[0], a_pair)
                exps(CONTEXT)
                for k in range(2):
                    weights(unit_tiles(HALVES)[k], a_half[:, 2 * k:2 * k + 2])
                for k in range(2):
                    weights(unit_tiles(CONTEXT)[k], a_ctx[:, k])
                step.enter(i, TT + 1)
                sc.wait_ge(hg_o, i + 1)
                for b in range(TT):
                    last = step.mark(sc.activation(squared[:, b, :], banks[4][:, b * P:(b + 1) * P], ACT.Square,
                                                   accum_out=stat2[:, 0, b:b + 1]))
                step.wait(last)
                step(sc.activation(stat2[:, 1, 0:TT], stat2[:, 0, 0:TT], ACT.Ln, scale=1.0 / P, bias=eps[:]))
                sc.activation(stat2[:, 2, 0:TT], stat2[:, 1, 0:TT], ACT.Exp, scale=-0.5).then_inc(hg_rstd, 1)
                step.leave(MH)
            with sc.Fori(0, MH) as i:
                t = T0["ml"]
                for m, x in enumerate((kc2[:, 0:C], qc, kc2[:, C:])):
                    sc.wait_ge(qk_conv, 3 * i + m + 1)
                    sc.activation(x, x, ACT.Silu).then_inc(qk_ready, 1)
                full(sc, t, 8 * i)
                copied(sc, t - 1, 2 * i)
                out_of(t, sc.activation(o_sig, acc[t % BANKS][:], ACT.Sigmoid))
                for n in range(2 * ST):
                    s, d = divmod(n, 2)
                    sc.wait_ge(gap_ready, 2 * ST * i + 2 * ST + n + 1)
                    w = targets(weight, d, s)
                    sc.activation(w, w, ACT.Exp, scale=-1.0).then_inc(w_ready, 1)
                step.enter(i, TT + 1)
                for b in range(TT):
                    sc.wait_ge(ml_h, TT * i + b + 1)
                    last = step.mark(sc.activation(squared[:, b, :], h_tok[:, b, :], ACT.Square,
                                                   accum_out=stat2[:, 0, TT + b:TT + b + 1]))
                step.wait(last)
                step(sc.activation(stat2[:, 1, TT:], stat2[:, 0, TT:], ACT.Ln, scale=1.0 / P, bias=eps[:]))
                sc.activation(stat2[:, 2, TT:], stat2[:, 1, TT:], ACT.Exp, scale=-0.5).then_inc(ml_rstd, 1)
                step.leave(MH)
            sc.wait_ge(x1_ready, 3)
            squares(xT, T, 4 * DT)
            sc.wait_ge(sq_used, 5 * DT)
            inverse_root(rstd[:], stat[:]).then_inc(rstd_ready, 1)
            shifted(hT, 3, 0, 2 * DT)
            with sc.Fori(0, F2T // 2) as i:
                sc.wait_ge(act2_ready, 2 * i + 2)
                for k in range(4):
                    t = T0["up2"] + k
                    full(sc, t, 4 * i)
                    sc.wait_ge(conv_ready, 4 * i + k + 1)
                    sc.copy(raw[:, k], acc[t % BANKS][:])
                    centre = ffn_taps[:, ds(i * 2 + TAPS // 2 * 2 * F2T + k % 2 * F2T + k // 2, 1)]
                    out_of(t, sc.mul(conv[:, k], acc[t % BANKS][:], centre))
                for j in range(2):
                    sc.wait_ge(conv_ready, 4 * i + 4 + 2 * j + 2)
                    sc.activation(conv[:, 2 * j], conv[:, 2 * j], ACT.Silu).then_inc(silu2_ready, 1)
            sc.wait_ge(x1_ready, 4)
            squares(xT, T, 5 * DT)
            sc.wait_ge(sq_used, 6 * DT)
            inverse_root(rstd[:], stat[:]).then_inc(rstd_ready, 1)
            for t in range(TT):
                for k in range(2):
                    b = T0["final"] + 2 * t + k
                    full(sc, b)
                    out_of(b, sc.copy(out_tok[:, t, k * 4 * P:(k + 1) * 4 * P], acc[b % BANKS][:]))

        @block.vector
        def _(ve):
            step = Steps(ve, dve_step)

            def product(out, x, y):
                return ve.tensor_tensor(out, x, y, ALU.mult)

            def complex_product(oc, os, xc, xs, yc, ys, n):
                t = [ptmp[:, k // 2, k % 2 * 256:k % 2 * 256 + n * GROUPS].rearrange("p (k g) -> p k g", g=GROUPS)
                     for k in range(4)]
                for o, x, y in zip(t, (xc, xs, xc, xs), (yc, ys, ys, yc)):
                    last = step.mark(product(o, x, y))
                step.wait(last)
                step.mark(ve.tensor_tensor(oc, t[0], t[1], ALU.subtract))
                step(ve.tensor_tensor(os, t[2], t[3], ALU.add))

            def newton(y, mean, t):
                step(product(t, y, y))
                last = ve.scalar_tensor_tensor(t, mean, EPS, t, ALU.add, ALU.mult)
                step(last)
                step(ve.tensor_scalar(t, t, -0.5, 1.5, ALU.mult, ALU.add))
                step(product(y, y, t))

            step.mark(ve.memset(sign[:], 1.0))
            step.mark(ve.memset(nsign[:], -1.0))
            step(ve.memset(mean_hd[:], 0.0))
            ve.memset(sign[HD:P], -1.0).then_inc(consts, 1)
            ve.memset(nsign[HD:P], 1.0).then_inc(consts, 1)
            for h in range(2):
                ve.memset(mean_hd[h * HD:(h + 1) * HD, h * HD:(h + 1) * HD], 1.0 / HD).then_inc(consts, 1)
            ve.memset(zero[:], 0.0).then_inc(consts, 1)
            ve.wait_ge(consts, CONSTS)
            step.mark(ve.tensor_scalar(cmask[:], cdist[:], FAR / 2, None, ALU.is_lt))
            copied(ve, 0)
            ar, ai = (vec[:, VEC[n]:VEC[n] + GROUPS] for n in ("a_re", "a_im"))
            ve.wait_ge(s5_exp, 1)
            product(s5[:, AR_DT], ar, s5[:, DT_]).then_inc(s5_small, 1)
            step.mark(ve.tensor_scalar(g_q[:], vcol("q_norm_g"), HD ** -0.5, None, ALU.mult))
            step(product(s5[:, ANGLE], ai, s5[:, DT_]))
            step(ve.tensor_scalar(s5[:, TURNS], s5[:, ANGLE], 1.0 / TWO_PI, ROUND, ALU.mult, ALU.add))
            step(ve.tensor_scalar(s5[:, TURNS], s5[:, TURNS], -ROUND, None, ALU.add))
            for part in (TURN_A, TURN_B, TURN_C):
                step(ve.scalar_tensor_tensor(s5[:, ANGLE], s5[:, TURNS], -part, s5[:, ANGLE], ALU.mult, ALU.add))
            ve.tensor_scalar(s5[:, ANGLE], s5[:, ANGLE], -3.1415925, 3.1415925, ALU.max, ALU.min).then_inc(s5_angle, 1)
            def norm(gain, start):
                ve.wait_ge(rstd_ready, start + 1)
                for c in range(DT):
                    ve.scalar_tensor_tensor(hT[:, c, :], xT[:, c, :], vcol(gain, c), rstd[:], ALU.mult, ALU.mult)\
                      .then_inc(h_ready, 1)

            norm("norm1_g", 0)
            ve.wait_ge(s5_sin, 2)
            ve.wait_ge(s5_exp, 3)
            step(product(s5[:, COS], s5[:, SIN_H], s5[:, SIN_H]))
            step(ve.tensor_scalar(s5[:, COS], s5[:, COS], -2.0, 1.0, ALU.mult, ALU.add))
            re, im = s5[:, PR:PR + STEP + 1], s5[:, PI:PI + STEP + 1]
            step.mark(ve.memset(re[:, 0], 1.0))
            step.mark(ve.memset(im[:, 0], 0.0))
            step.mark(product(re[:, 1], s5[:, MAG], s5[:, COS]))
            step(product(im[:, 1], s5[:, MAG], s5[:, SIN]))
            m = 1
            while m < STEP:
                shape = [P, m, GROUPS]
                complex_product(re[:, m + 1:2 * m + 1], im[:, m + 1:2 * m + 1], re[:, 1:m + 1], im[:, 1:m + 1],
                                re[:, m:m + 1].to_broadcast(shape), im[:, m:m + 1].to_broadcast(shape), m)
                m *= 2
            xc, xs = s5[:, COS:COS + 1], s5[:, SIN:SIN + 1]
            for n in range(3):
                oc, os = ((s5[:, E1C:E1C + 1], s5[:, E1S:E1S + 1]), (s5[:, COS:COS + 1], s5[:, SIN:SIN + 1]),
                          (s5[:, E8C:E8C + 1], s5[:, E8S:E8S + 1]))[n]
                complex_product(oc, os, xc, xs, xc, xs, 1)
                xc, xs = oc, os
            step.mark(product(s5[:, DEN], ar, ar))
            step(product(s5[:, TMP], ai, ai))
            step(ve.tensor_tensor(s5[:, DEN], s5[:, DEN], s5[:, TMP], ALU.add))
            step.mark(ve.reciprocal(s5[:, DEN], s5[:, DEN]))
            step(ve.tensor_scalar(s5[:, NR], re[:, 1], -1.0, None, ALU.add))
            step.mark(product(s5[:, _1], s5[:, NR], ar))
            step.mark(product(s5[:, _2], im[:, 1], ai))
            step.mark(product(s5[:, _3], im[:, 1], ar))
            step(product(s5[:, _4], s5[:, NR], ai))
            step.mark(ve.tensor_tensor(s5[:, FR], s5[:, _1], s5[:, _2], ALU.add))
            step(ve.tensor_tensor(s5[:, FI], s5[:, _3], s5[:, _4], ALU.subtract))
            step.mark(product(s5[:, FR], s5[:, FR], s5[:, DEN]))
            step(product(s5[:, FI], s5[:, FI], s5[:, DEN]))
            bu_, bv_, ub, vb = (x.rearrange("p g c -> p (g c)") for x in (bu, bv, ubar, vbar))
            step(ve.tensor_scalar(bv_, bv_, nsign[:], None, ALU.mult))
            fr, fi = (s5[:, k].unsqueeze(2).to_broadcast([P, GROUPS, GROUP]) for k in (FR, FI))
            t0, t1 = (ptmp[:, k].rearrange("p (g c) -> p g c", c=GROUP) for k in range(2))
            step.mark(product(t0, bu, fr))
            step(product(t1, bv, fi))
            ve.tensor_tensor(ubar, t0, t1, ALU.add).then_inc(s5_bbar, 1)
            ve.wait_ge(s5_bbar, 1)
            step.mark(product(t0, bv, fr))
            step(product(t1, bu, fi))
            ve.tensor_tensor(vbar, t0, t1, ALU.subtract).then_inc(s5_bbar, 1)
            ve.wait_ge(ca_ready, 1)
            for m in range(8):
                t = T0["bt"] + m
                full(ve, t)
                out_of(t, ve.tensor_copy(bt[:, 4 * m:4 * (m + 1)].rearrange("p g n -> p (g n)"), acc[t % BANKS][:]))
            for t in range(4):
                copied(ve, T0["state"] + t)
            ve.wait_ge(rot_ready, 1)
            def flat(x):
                return x.rearrange("p g j -> p (g j)")
            step.mark(product(flat(z1), flat(e1), flat(rot_c)))
            ve.wait_ge(e_swapped, 32)
            step(product(flat(zs), flat(e2), flat(rot_s)))
            step(ve.tensor_tensor(flat(z1), flat(z1), flat(zs), ALU.add))
            for g in range(GROUPS):
                ins = ve.tensor_tensor_scan(zs[:, g, :], s5[:, MAG_STEP, g:g + 1].to_broadcast([P, CHUNKS]), z1[:, g, :],
                                            0.0, ALU.mult, ALU.add)
                if g < GROUPS - 1:
                    step.mark(ins)
            ins.then_inc(z_scanned, 1)
            ve.wait_ge(z_scanned, 1)
            n = CHUNKS - 1
            step.mark(ve.memset(xprev[:, :, 0:1], 0.0))
            step(product(xprev[:, :, 1:], zs[:, :, 0:n], rot_c[:, :, 0:n]))
            ve.wait_ge(z_swapped, 32)
            step(product(z1[:, :, 0:n], z2[:, :, 0:n], rot_s[:, :, 0:n]))
            ve.tensor_tensor(xprev[:, :, 1:], xprev[:, :, 1:], z1[:, :, 0:n], ALU.subtract).then_inc(xprev_ready, 1)
            for m in range(6):
                t = T0["qk_norm"] + m
                ve.wait_ge(qk_sq, m + 1)
                y, tmp = root[:, m % 2, :], rstd[:]
                step(product(tmp, y, y))
                step.mark(ve.scalar_tensor_tensor(tmp, acc[t % BANKS][:], EPS, tmp, ALU.add, ALU.mult))
                step.wait(step.base + step.n)
                out_of(t, ve.tensor_scalar(tmp, tmp, -0.5, 1.5, ALU.mult, ALU.add))
                copied(ve, t)
                step(product(y, y, tmp))
                if m < 4:
                    ve.scalar_tensor_tensor(qT[:, m, :], qT[:, m, :], g_q[:], y, ALU.mult, ALU.mult).then_inc(qk_rstd, 1)
                else:
                    for h in range(KVG):
                        half = slice(h * HD, (h + 1) * HD)
                        ins = ve.scalar_tensor_tensor(kk[half, m - 4, h, :], kvT[half, 2 * (m - 3), :],
                                                      vcol("k_norm_g", m - 3)[half], y[half], ALU.mult, ALU.mult)
                        ins.then_inc(k_normed, 1)
            n = KVG * NCMP
            ve.wait_ge(kc_sq, 2)
            newton(knorm[:, 0:n], banks[7][:, 0:n], rstd[:, 0:n])
            ve.scalar_tensor_tensor(kc, stat[:, 64:64 + n], vcol("k_norm_g", 0), knorm[:, 0:n], ALU.mult, ALU.mult)\
              .then_inc(kc_ready, 1)
            ve.wait_ge(mod_full, 24)
            b = vec[:, VEC["b_mod_2"]:VEC["b_mod_2"] + NMOD * DT].unsqueeze(2).to_broadcast([P, NMOD * DT, 2])
            ve.tensor_tensor(mod[:], modp[:, 0:2 * NMOD * DT].rearrange("p (m c) -> p m c", c=2), b, ALU.add)\
              .then_inc(mod_ready, 1)
            ve.wait_ge(y_in, 32)
            for m in range(UT):
                y = yT[:, m].rearrange("p s j -> p (s j)")
                ve.scalar_tensor_tensor(y, us[:, m].rearrange("p s j -> p (s j)"), vcol("ssm_d", m), y, ALU.mult, ALU.add)\
                  .then_inc(y_sum, 1)
            for m in range(UT):
                copied(ve, T0["glu"] + m)
                product(y_ssm[:, m, :], gelu_y[:, m, :], yT[:, m].rearrange("p s j -> p (s j)")).then_inc(yssm_ready, 1)
            QUERIES = HPG * TT
            ve.wait_ge(qk_rstd, 4)
            ve.wait_ge(kc_ready, 1)
            ve.wait_ge(k_normed, 4)
            ve.wait_ge(k_dup, 64)
            with ve.Fori(0, KVG) as gi:
                step.enter(gi, ATT_STEPS)
                ve.tensor_copy(kcg, kc[:, ds(gi * NCMP, NCMP)]).then_inc(qn_ready, 1)
                for k in range(2):
                    ve.tensor_copy(kkg[:, k, :], kk[:, k, ds(gi, 1), :].rearrange("p a n -> p (a n)")).then_inc(qn_ready, 1)
                for k in range(2):
                    ve.tensor_copy(qn[:, k, :], qT[:, ds(2 * gi + k, 1), :].rearrange("p a n -> p (a n)")).then_inc(qn_ready, 1)

                def maxima(n):
                    hg, tt = divmod(n, TT)
                    w, st = (tt + 1) * P, stats[:, n % 2]
                    if tt == 0:
                        slope = negslope[:, ds(HPG * gi + hg, 1)]
                        step.mark(ve.tensor_scalar(bias[:, hg % 2, :], dist[:], slope, None, ALU.mult))
                        step(ve.tensor_scalar(cbias[:, hg % 2].rearrange("p t n -> p (t n)"),
                                              cdist[:].rearrange("p t n -> p (t n)"), slope, None, ALU.mult))
                    ve.wait_ge(score_full, gi * QUERIES + n + 1)
                    if n >= 2:
                        ve.wait_ge(prob_ready, gi * QUERIES + n - 1)
                    step.mark(ve.memset(tick[:, 0:1], 0.0))
                    step.mark(ve.tensor_tensor_reduce(cscore[:, n % 2, :], stat[:, 0:NCMP],
                                                      cbias[:, hg % 2, tt, :], 1.0, -3e38, ALU.add, ALU.max, st[:, 0:1]))
                    for m in range(2):
                        last = step.mark(ve.tensor_tensor_reduce(
                            score[:, n % 2, m, 0:w], banks[m][:, 0:w], bias[:, hg % 2, T - w:T],
                            1.0, -3e38, ALU.add, ALU.max, st[:, 1 + m:2 + m]))
                    step.wait(last)
                    ve.tensor_scalar(st[:, 3:6], st[:, 0:3], -1.0, None, ALU.mult).then_inc(score_ready, 1)

                def weights(n):
                    hg, tt = divmod(n, TT)
                    st = stats[:, n % 2]
                    ve.wait_ge(prob_ready, gi * QUERIES + n + 1)
                    product(cprob[:, n % 2, :], cprob[:, n % 2, :], cmask[:, tt, :]).then_inc(cprob_ready, 1)
                    step(ve.reciprocal(st[:, 9:12], st[:, 6:9]))
                    return step.mark(product(st[:, 12:15], st[:, 9:12], gsig[:, tt, ds(HPG * gi + hg, 3, HEADS)]))

                def combine(n, weighed):
                    hg, tt = divmod(n, TT)
                    st = stats[:, n % 2]
                    o = o_tok[:, tt, ds(gi * HPG * HD + hg * HD, HD)]
                    p = banks[(2, 7)[n % 2]]
                    ve.wait_ge(o_full, gi * QUERIES + n + 1)
                    step.wait(weighed)
                    step(ve.tensor_scalar(o, p[:, 0:HD], st[:, 12:13], None, ALU.mult))
                    step(ve.scalar_tensor_tensor(o, p[:, HD:2 * HD], st[:, 13:14], o, ALU.mult, ALU.add))
                    ve.scalar_tensor_tensor(o, p[:, 2 * HD:3 * HD], st[:, 14:15], o, ALU.mult, ALU.add).then_inc(o_ready, 1)

                maxima(0)
                weighed = None
                for n in range(QUERIES):
                    if n >= 1:
                        before = weighed
                    weighed = weights(n)
                    if n >= 1:
                        combine(n - 1, before)
                    if n + 1 < QUERIES:
                        maxima(n + 1)
                    w = (n % TT + 1) * P
                    ve.wait_ge(pt_full, gi * QUERIES + n + 1)
                    ve.tensor_copy(probT[:, n % 2, 0, 0:w], banks[5][:, 0:w]).then_inc(cpt_out, 1)
                combine(QUERIES - 1, weighed)
                step.leave(KVG)
            free(ve, merged_ready)
            with ve.Fori(0, DT) as i:
                ve.wait_ge(merged_ready, i + 1)
                for m in range(2):
                    t = T0["merge"] + 2 * m + 1
                    copied(ve, t - 1, i)
                    full(ve, t, 4 * i)
                    out_of(t, product(prod[:, 0, m, :], sig[:, m, :], acc[t % BANKS][:]))
                for m in range(2):
                    copied(ve, T0["merge"] + 2 * m + 1, i)
                ve.tensor_tensor(merged[:, ds(i, 1), :], prod[:, 0, 0:1, :], prod[:, 0, 1:2, :], ALU.add)\
                  .then_inc(merged_ready, 1)

            def residual(name, rounds, gain=None):
                with ve.Fori(0, rounds) as i:
                    for k in range(4):
                        t = T0[name] + k
                        full(ve, t, 4 * i)
                        x = xT[:, ds(4 * i + k, 1), :].rearrange("p a n -> p (a n)")
                        if gain is None:
                            out_of(t, ve.tensor_tensor(x, acc[t % BANKS][:], x, ALU.add))
                        else:
                            out_of(t, ve.scalar_tensor_tensor(x, acc[t % BANKS][:], mod[:, ds(gain * DT + k + 4 * i, 1), 0],
                                                              x, ALU.mult, ALU.add))

            def residual_done(name):
                for k in range(BANKS):
                    copied(ve, T0[name] + DT - BANKS + k)
                ve.memset(tick[:, 1:2], 0.0).then_inc(x1_ready, 1)

            residual("out1", 2)
            residual_done("out1")
            norm("norm2_g", 1)
            free(ve, act_ready, 4)
            with ve.Fori(0, FT // 4) as i:
                for k in range(4):
                    copied(ve, T0["up1"] + k, i)
                    r = relu[:, k, :].unsqueeze(1)
                    product(act[:, ds(4 * i + k, 1), :], r, r).then_inc(act_ready, 1)
            residual("down1", 2)
            residual_done("down1")
            logits = vec[:, VEC["hgrn_lb_logits_2"]:VEC["hgrn_lb_logits_2"] + 4 * MH]\
                .rearrange("p (d l h) -> p d l h", d=2, l=2)
            ve.tensor_tensor(lb[:, 2], logits[:, :, 1], logits[:, :, 0], ALU.subtract).then_inc(lb_logit, 1)
            ve.wait_ge(lb_sig, 2)
            ve.tensor_scalar(lb[:, 0], lb[:, 0], TINY, None, ALU.max).then_inc(lb_ready, 1)
            ve.wait_ge(mod_ready, 1)
            for k, (name, scale, col) in enumerate((("norm1_w_2", 1, 0), ("norm1_w_2", 1, 1), ("norm2_w_2", 4, 0))):
                last = step.mark(ve.scalar_tensor_tensor(amod[:, k], mod[:, scale * DT:(scale + 1) * DT, col], 1.0,
                                                         vec[:, VEC[name]:VEC[name] + DT], ALU.add, ALU.mult))
            step.wait(last)

            def scaled(dst, src, gain, r):
                for c in range(DT):
                    ve.scalar_tensor_tensor(dst[:, c, :], src[:, c, :], amod[:, gain, c:c + 1], r, ALU.mult, ALU.mult)\
                      .then_inc(h_scaled, 1)

            ve.wait_ge(rstd_ready, 3)
            scaled(hcT, xcT, 1, root[:, 0, 0:C])
            ve.wait_ge(rstd_ready, 4)
            scaled(hT, xT, 0, rstd[:])
            f, g, b = (x[0:MH] for x in (row_f, row_g, row_b))
            ve.wait_ge(rows_in, 64)
            ve.scalar_tensor_tensor(b, f, -1.0, f, ALU.mult, ALU.min).then_inc(neg_ready, 1)
            ve.wait_ge(ln_ready, 1)
            step(ve.scalar_tensor_tensor(f, f, 0.0, b, ALU.min, ALU.subtract))

            def scan(out, x, initial, op):
                n = x.shape[-1]
                if op == ALU.add:
                    return ve.tensor_tensor_scan(out, x, zero[0:x.shape[0]].to_broadcast([x.shape[0], n]), initial,
                                                 ALU.add, ALU.add)
                return ve.tensor_tensor_scan(out, x, x, initial, op, op)

            def both_ways(out, x, op):
                step.mark(scan(out[:, 0], x[:, 0], 0.0, op))
                step(scan(out[:, 1, 0:C][:, ::-1], x[:, 1, 0:C][:, ::-1], 0.0, op))
                step(scan(out[:, 1, C:][:, ::-1], x[:, 1, C:][:, ::-1], out[:, 1, 0:1], op))

            both_ways(b, f, ALU.add)
            step(ve.tensor_tensor(g, g, b, ALU.subtract))
            both_ways(f, g, ALU.max)
            ve.tensor_tensor(b, b, f, ALU.add).then_inc(rows_ready, 1)
            ve.wait_ge(max_out, 32)
            copied(ve, T0["gate_cols"])
            step(ve.memset(sums1, 0.0))
            s1 = sums1[:, 0:2 * SEGS].rearrange("p (d a n) -> p d a n", d=2, a=ST)
            ve.wait_ge(lb_ready, 1)
            with ve.Fori(0, MH) as i:
                step.enter(i, 2 + 2 * ST + 3)
                ve.wait_ge(z_ready, i + 2)
                for d in range(2):
                    x = logf[:, d, :, 1:]
                    ve.tensor_scalar(x, x, lb[:, 1, d, ds(i, 1)], lb[:, 0, d, ds(i, 1)], ALU.mult, ALU.add).then_inc(f_ready, 1)
                for d in range(2):
                    x = hg_k[:, ds(i, 1), d, :]
                    step.mark(ve.tensor_scalar(x, x, lb[:, 1, d, ds(i, 1)], None, ALU.mult))
                ve.wait_ge(sums_kept, i + 1)
                ve.wait_ge(logf_ready, 2 * i + 2)
                for d in range(2):
                    for b in range(ST):
                        last = step.mark(scan(s1[:, d, b, 1:], logf[:, d, b, 1:], 0.0, ALU.add))
                step.wait(last)
                tot = [s1[:, d, CT:, P] for d in range(2)]
                step.mark(scan(sums1[:, PRE_F:PRE_F + TT], tot[0], 0.0, ALU.add))
                step.mark(scan(sums1[:, SUF_B:SUF_B + TT][:, ::-1], tot[1][:, ::-1], 0.0, ALU.add))
                step.mark(scan(sums1[:, PRE_B:PRE_B + 2], tot[1][:, 0:2], 0.0, ALU.add))
                scan(sums1[:, CTX_F:CTX_F + CT], s1[:, 0, 0:CT, P], 0.0, ALU.add).then_inc(sums_ready, 1)
                step.leave(MH)
            ve.wait_ge(same_ready, len(LEVELS))
            ve.wait_ge(sums_kept, MH + 1)
            step.wait(step.base + step.n)
            with ve.Fori(0, MH) as i:
                def k_of(d, at=C):
                    n = T if at else C
                    return hg_k[:, ds(i, 1), d, at:at + n].rearrange("p o n -> p (o n)")

                q = hg_q[:, ds(i, 1), :].rearrange("p o n -> p (o n)")

                def decayed(u):
                    k_, q_ = ek[:, u % 2, :], eq[:, u % 2, :]
                    if u == DIAG:
                        full(ve, unit_tiles(u - 2)[0], 16 * i)
                        ve.tensor_tensor(k_, k_of(0), k_of(1), ALU.add)
                        ve.tensor_scalar(q_, q, P ** -0.5, None, ALU.mult).then_inc(kq_ready, 1)
                        return
                    ve.wait_ge(exp_ready, (UNITS - 1) * i + u + (u < DIAG))
                    if u < HALVES:
                        m = LEVELS[u] if u < DIAG else P

                        def halves(x):
                            return x.rearrange("p (b t m) -> p b t m", t=2, m=m)

                        for h in range(2):
                            product(halves(k_)[:, :, h], halves(k_)[:, :, h], halves(k_of(h))[:, :, h])
                    elif u == HALVES:
                        for h in range(2):
                            half = slice(h * C, (h + 1) * C)
                            product(k_[:, half], k_[:, half], k_of(h)[:, half])
                    else:
                        for d in range(2):
                            half = slice(d * C, (d + 1) * C)
                            product(k_[:, half], k_[:, half], k_of(d, 0))
                        ve.scalar_tensor_tensor(eq_b[:], eq_b[:], P ** -0.5, q, ALU.mult, ALU.mult)
                    ve.scalar_tensor_tensor(q_, q_, P ** -0.5, q, ALU.mult, ALU.mult).then_inc(kq_ready, 1)

                def assemble(u):
                    b = unit_tiles(u)[0]
                    full(ve, b, 16 * i)
                    own = acc[b % BANKS][:].rearrange("p (s n) -> p s n", n=P)
                    if u == 0:
                        out_of(b, ve.tensor_copy(a_own, own))
                        return
                    copied(ve, b - 1, 4 * i)
                    ve.memset(tick[:, 0:1], 0.0)
                    mask = same[:, u - 1, :].unsqueeze(1).to_broadcast([P, TT, P])
                    out_of(b, ve.copy_predicated(a_own, mask, own))

                for u in range(UNITS):
                    decayed(u)
                    if 1 <= u <= DIAG + 1:
                        assemble(u - 1)
                ve.wait_ge(hg_rstd, i + 1)
                for b in range(TT):
                    ins = ve.tensor_scalar(y_tok[:, b, :], banks[4][:, b * P:(b + 1) * P], stat2[:, 2, b:b + 1], None, ALU.mult)
                ins.then_inc(hg_y, 1)
                ve.wait_ge(hg_flipped, i + 1)
                g = hg_g[:, ds(i, 1), :]
                ve.scalar_tensor_tensor(g, banks[6][:].unsqueeze(1), vec[:, ds(i + VEC["hgrn_norm_w_2"], 1)], g,
                                        ALU.mult, ALU.mult).then_inc(hg_done, 1)

            def convolve(chains, done):
                rounds = []
                for out, src, rows_, col, first in chains:
                    taps = [4] + [k for k in range(TAPS) if k != 4 and (rows_ > 1 or k // 3 == 1)]
                    for n, k in enumerate(taps[1 - first:]):
                        dy, dx = k // 3 - 1, k % 3 - 1
                        w = out.shape[-1] // rows_
                        o, x = (v.rearrange("p (y x) -> p y x", x=w) for v in (out, src))
                        ys, xs = slice(max(0, -dy), rows_ - max(0, dy)), slice(max(0, -dx), w - max(0, dx))
                        yt, xt = (slice(v.start + e, v.stop + e) for v, e in ((ys, dy), (xs, dx)))
                        rounds += [[]] if n >= len(rounds) else []
                        rounds[n].append((o[:, ys, xs], x[:, yt, xt], col(k), k == 4, k == taps[-1]))
                for ops in rounds:
                    last = None
                    for o, x, c, alone, final in ops:
                        if alone:
                            ins = ve.tensor_scalar(o, x, c, None, ALU.mult)
                        else:
                            ins = ve.scalar_tensor_tensor(o, x, c, o, ALU.mult, ALU.add)
                        if final:
                            ins.then_inc(done, 1)
                        else:
                            last = step.mark(ins)
                    if last is not None:
                        step.wait(last)

            free(ve, gap_ready, 2 * ST)
            ve.wait_ge(hg_done, MH)
            ve.wait_ge(cols_ready, 1)
            copied(ve, T0["gate_cols"])
            with ve.Fori(0, MH) as i:
                step.enter(i, 2 * (TAPS - 1) + 2 + 2 * TT + 3)
                t = T0["ml"]
                for m in range(3):
                    copied(ve, T0["hg"] + m, 4 * i)

                def chain(out, src, rows_, head):
                    return (out, src.rearrange("p o n -> p (o n)"), rows_,
                            lambda k: vec[:, ds(i + VEC["mlstm_conv_w_2"] + k * DT + head, 1)], 1)

                convolve([chain(qc, ml_q[:, ds(i, 1), :], ROWS, 0), chain(kc2[:, C:], ml_k[:, ds(i, 1), C:], ROWS, MH),
                          chain(kc2[:, 0:C], ml_k[:, ds(i, 1), 0:C], 1, MH)], qk_conv)
                ve.wait_ge(max_in, 32 * (i + 1))
                for n in range(2 * ST):
                    s, d = divmod(n, 2)
                    x = targets(cummax.unsqueeze(2).to_broadcast([P, 2, ST, T]), d, s)
                    ve.tensor_scalar(targets(weight, d, s), x, gcol[:, d, s, ds(i, 1)], 0.0, ALU.subtract, ALU.max)\
                      .then_inc(gap_ready, 1)
                for n in range(2 * ST):
                    s, d = divmod(n, 2)
                    w, b = targets(weight, d, s), t + 1 + s
                    full(ve, b, 8 * i)
                    ve.wait_ge(w_ready, 2 * ST * i + n + 1)
                    x = acc[b % BANKS][:].unsqueeze(1).unsqueeze(1).to_broadcast([P, 2, ST, T])
                    ins = ve.scalar_tensor_tensor(w, targets(x, d, s), P ** -0.5, w, ALU.mult, ALU.mult)
                    if d:
                        out_of(b, ins)
                    else:
                        ins.then_inc(p_ready, 1)
                den = stat2[:, 3].rearrange("p (d b) -> p d b", d=2)
                for b in range(TT):
                    ve.wait_ge(ml_o, TT * i + b + 1)
                    x = banks[4 + b][:, P:2 * P + 2:P + 1]
                    last = step.mark(ve.tensor_copy(den[:, :, b], x))
                step.wait(last)
                step(ve.scalar_tensor_tensor(den, den, -1.0, den, ALU.mult, ALU.max))
                step(ve.tensor_tensor(den, den, floor[:, :, :, ds(i, 1)].rearrange("p d b o -> p d (b o)"), ALU.max))
                step(ve.reciprocal(stat2[:, 3], stat2[:, 3]))
                for b in range(TT):
                    last = step.mark(ve.tensor_scalar(h_tok[:, b, :], banks[4 + b][:, 0:P], den[:, 0, b:b + 1], None, ALU.mult))
                step.wait(last)
                for b in range(TT):
                    ve.scalar_tensor_tensor(h_tok[:, b, :], banks[4 + b][:, P + 1:2 * P + 1], den[:, 1, b:b + 1],
                                            h_tok[:, b, :], ALU.mult, ALU.add).then_inc(ml_h, 1)
                ve.wait_ge(ml_rstd, i + 1)
                for b in range(TT):
                    ins = ve.tensor_scalar(h_tok[:, b, :], h_tok[:, b, :], stat2[:, 2, TT + b:TT + b + 1], None, ALU.mult)
                ins.then_inc(ml_y, 1)
                full(ve, t + 7, 8 * i)
                copied(ve, t, 2 * i)
                out_of(t + 7, ve.scalar_tensor_tensor(ml_q[:, ds(i, 1), :], acc[(t + 7) % BANKS][:].unsqueeze(1),
                                                      vec[:, ds(i + VEC["mlstm_norm_w_2"], 1)], o_sig.unsqueeze(1),
                                                      ALU.mult, ALU.mult))
                step.leave(MH)
            residual("out2", 2, 2)
            residual_done("out2")
            ve.wait_ge(rstd_ready, 5)
            scaled(hT, xT, 2, rstd[:])
            free(ve, conv_ready, 4)
            with ve.Fori(0, F2T // 2) as i:
                step.enter(i, 4 * (TAPS - 2))
                for j in range(2):
                    for m in range(2):
                        copied(ve, T0["up2"] + 2 * j + m, i)
                    convolve([(conv[:, 2 * j + m], raw[:, 2 * j + m], ROWS,
                               lambda k, m=m: ffn_taps[:, ds(i * 2 + k * 2 * F2T + m * F2T + j, 1)], 0) for m in range(2)],
                             conv_ready)
                step.leave(F2T // 2)
            residual("down2", 2, 5)
            residual_done("down2")
            ve.wait_ge(rstd_ready, 6)
            for c in range(DT):
                ve.scalar_tensor_tensor(hT[:, c, :], xT[:, c, :], vcol("final_norm_w_2", c), rstd[:], ALU.mult, ALU.mult)\
                  .then_inc(out_ready, 1)


_INS = ['x', 'norm1_g', 'w_in', 'ssm_a_re', 'ssm_a_im', 'ssm_log_dt', 'ssm_b_re', 'ssm_b_im', 'ssm_c_re', 'ssm_c_im',
        'ssm_d', 'ssm_w_glu', 'ssm_b_glu', 'cmp_pe_k', 'cmp_pe_v', 'cmp_wk1', 'cmp_wk2', 'cmp_wv1', 'cmp_wv2',
        'q_norm_g', 'k_norm_g', 'w_proj_ssm', 'w_proj_nsa', 'w_out', 'norm2_g', 'w_up', 'w_down', 'c_2', 'ctx_2',
        'c_ctx_2', 'w_mod_2', 'b_mod_2', 'norm1_w_2', 'w_in_2', 'mlstm_gate_b_2', 'mlstm_conv_w_2',
        'mlstm_norm_w_2', 'hgrn_lb_logits_2', 'hgrn_norm_w_2', 'w_out_2', 'norm2_w_2', 'w_up_2', 'ffn_conv_w_2',
        'w_down_2', 'final_norm_w_2']


def kernel(**inputs):
    import numpy as _np
    import concourse.bacc as _bacc
    from concourse import mybir as _mybir
    from concourse.bass_utils import run_bass_kernel_spmd as _run

    nc = _bacc.Bacc("TRN2", target_bir_lowering=False, num_devices=1)
    arrays, args = {}, {}
    for name in _INS:
        arr = _np.ascontiguousarray(inputs[name])
        arrays["in_" + name] = arr
        args[name] = nc.dram_tensor("in_" + name, arr.shape, _mybir.dt.from_np(arr.dtype), kind="ExternalInput").ap()
    out = nc.dram_tensor("out_x", (1, T, D), _mybir.dt.float32, kind="ExternalOutput").ap()
    two_block_program(nc, args, out)
    r = _run(nc, [arrays], core_ids=[0])
    return r.results[0]["out_x"]
```

```python
import concourse.bass as bass
from concourse import mybir
from contextlib import ExitStack

F32 = mybir.dt.float32
F32R = mybir.dt.float32r
U8 = mybir.dt.uint8
ACT = mybir.ActivationFunctionType
ALU = mybir.AluOpType
AX = mybir.AxisListType
ds = bass.ds

P = 128
T, C, D = 512, 256, 1024
S = C + T
TT, CT, DT = T // P, C // P, D // P
ST = CT + TT
EPS = 1e-6

GROUPS, GROUP, STATE = 32, 16, 64
STEP = P // GROUP
CHUNKS = T // STEP
UT = GROUPS * GROUP // P
HEADS, HD = 8, 64
KVG = 2
HPG = HEADS // KVG
CMP_STRIDE, CMP_BLOCK = 16, 32
NCMP = T // CMP_STRIDE - 1
FF = 4 * D
FT = FF // P
FAR = 2.56e32

MH = 4
FF2 = 2816
F2T = FF2 // P
TAPS = 9
GRID_W, ROWS = 64, 8
NMOD = 6

VEC = {}
_at = 0
for _name, _rows in (("norm1_g", DT), ("ssm_d", UT), ("ssm_b_glu", UT), ("norm2_g", DT), ("c_2", DT),
                     ("c_ctx_2", DT), ("norm1_w_2", DT), ("norm2_w_2", DT), ("final_norm_w_2", DT),
                     ("hgrn_lb_logits_2", 4 * MH), ("b_mod_2", NMOD * DT),
                     ("mlstm_conv_w_2", TAPS * DT), ("q_norm_g", 1), ("k_norm_g", 3),
                     ("mlstm_norm_w_2", MH), ("hgrn_norm_w_2", MH), ("pe", CMP_BLOCK),
                     ("a_re", GROUPS), ("a_im", GROUPS)):
    VEC[_name] = _at
    _at += _rows
VEC_COLS = _at
VEC0 = VEC["mlstm_conv_w_2"]
VEC1 = VEC["pe"]

TILES = (("params", 4), ("x", DT), ("u", UT), ("q", 4), ("kernel", 8), ("bt", 8), ("kv", 6), ("gates", 1),
         ("state", 4), ("v_tok", 2), ("qk_norm", 6), ("y", 4), ("o_nsa", 4), ("glu", UT), ("merge", 32),
         ("out1", DT), ("up1_0", FT // 2), ("down1_0", DT), ("up1_1", FT // 2), ("down1_1", DT),
         ("ctx", 4), ("gate_rows", 2), ("v2", 12), ("gate_cols", 1), ("hg_in", 16), ("hg", 64), ("ml", 32),
         ("out2", DT), ("up2_0", 24), ("down2_0", DT), ("up2_1", 20), ("down2_1", DT), ("final", 8))
CHUNK_OF = (("u", 2), ("q", 2), ("kv", 3), ("mod0", 8), ("cmp", 2), ("mod1", 8), ("mod2", 8), ("glu", 1),
            ("merge", 16), ("out1", 4),
            ("up1_0", 8), ("down1_0", 8), ("up1_1", 8), ("down1_1", 8), ("v2", 4), ("hg_in", 8), ("ml_in", 8),
            ("ml_o", 8), ("out2", 4), ("up2_0", 12), ("down2_0", 8), ("up2_1", 10), ("down2_1", 8))


def offsets(plan):
    at, out = 0, {}
    for name, n in plan:
        out[name] = at
        at += n
    return out


T0, C0 = offsets(TILES), offsets(CHUNK_OF)
BANKS, SLOTS = 4, 2

ARENA = 34 * 1024 - 160

(LOG_DT, DT_, AR_DT, ANGLE, TURNS, SIN_H, SIN, COS, MAG, MAG_STEP, DEN, NR, FR, FI, TMP, _1, _2, _3, _4) = range(19)
PR, PI = 20, 20 + STEP + 1
E1C, E1S, E8C, E8S = 38, 39, 40, 41
S5_TERMS = 44
TWO_PI = 6.283185307179586
TURN_A = 6.28125
TURN_B = 0.0019350051879882812
TURN_C = TWO_PI - TURN_A - TURN_B
ROUND = 12582912.0
ATT_STEPS = 136



SPLITS1 = C0["v2"] - C0["merge"]
SPLIT0 = {name: C0[name] - C0["merge"] for name in ("merge", "out1", "up1_0", "down1_0", "up1_1", "down1_1")}
SPLIT0.update((name, C0[name] - C0["up2_0"] + SPLITS1) for name in ("up2_0", "down2_0", "up2_1", "down2_1"))
F2_HALF = (12, 10)
SEGS = (P + 1) * ST
SUMS = 2 * SEGS + 16
PRE_F, SUF_B, PRE_B, CTX_F = (2 * SEGS + k for k in (0, 4, 8, 10))
LEVELS = (64, 32, 16, 8, 4, 2, 1)
UNITS = 11
DIAG, PAIRS, HALVES, CONTEXT = 7, 8, 9, 10
ML_AFTER = 1, 3, 3
TINY = 1e-37


class Steps:

    def __init__(self, eng, sem):
        self.eng, self.sem, self.base, self.n = eng, sem, 0, 0

    def mark(self, ins):
        ins.then_inc(self.sem, 1)
        self.n += 1
        return self.base + self.n

    def wait(self, value):
        self.eng.wait_ge(self.sem, value)

    def __call__(self, ins):
        self.wait(self.mark(ins))

    def enter(self, i, steps):
        self.start, self.steps = self.base + self.n, steps
        self.base, self.n = self.start + i * steps, 0

    def leave(self, rounds):
        assert self.n == self.steps, f"{self.n} steps, not {self.steps}"
        self.base, self.n = self.start + rounds * self.steps, 0


def two_block_program(nc, a, out):
    ctx = ExitStack()
    with ctx:
        def sb(name, shape, dt=F32):
            return ctx.enter_context(nc.sbuf_tensor(name, shape, dt))

        def parts(**shapes):
            with ExitStack() as shared:
                return [shared.enter_context(nc.sbuf_tensor(name, [P, *shape], F32R)) for name, shape in shapes.items()]

        def sem(name):
            return ctx.enter_context(nc.semaphore(name))

        ident = sb("ident", [P, P])
        mean_d = sb("mean_d", [P, P])
        mean_hd = sb("mean_hd", [P, P])
        dist = sb("dist", [P, T])
        cdist = sb("cdist", [P, TT, NCMP])
        cmask = sb("cmask", [P, TT, NCMP])
        negslope = sb("negslope", [P, HEADS])
        sign = sb("sign", [P, 1])
        nsign = sb("nsign", [P, 1])
        g_q = sb("g_q", [P, 1])
        eps = sb("eps", [P, 1])
        vec = sb("vec", [P, VEC_COLS])
        ffn_taps = sb("ffn_taps", [P, TAPS * 2 * F2T])
        w_gate = sb("w_gate", [P, DT, 3 * HEADS])
        w_mgate = sb("w_mgate", [P, DT, 4 * MH])
        mgate_b = sb("mgate_b", [4 * MH, 1])
        wk2 = sb("wk2", [P, 2, HD])
        wv2 = sb("wv2", [P, HD])
        mod = sb("mod", [P, NMOD * DT, 2])
        silu_c = sb("silu_c", [P, DT, 2])
        xT = sb("xT", [P, DT, T])
        hT_hi, = parts(hT_hi=(DT, T))
        hT = sb("hT", [P, DT, T])
        ring = sb("ring", [P, SLOTS, DT * 2 * P])
        sq = sb("sq", [P, 2, T])
        rstd = sb("rstd", [P, T])
        root = sb("root", [P, 2, T])
        tick = sb("tick", [P, 24])
        zero = sb("zero", [P, 1])
        same = sb("same", [P, len(LEVELS), P], U8)
        act_hi, act_lo, h_lo, w_hi, w_lo = parts(act_hi=(FT // 2, T), act_lo=(FT // 2, T), h_lo=(DT, T),
                                                 w_hi=(SLOTS, DT * 2 * P), w_lo=(SLOTS, DT * 2 * P))
        arena = sb("arena", [P, ARENA])

        def area(at, *shape):
            n = 1
            for k in shape:
                n *= k
            v = arena[:, at:at + n]
            names = "abcd"[:len(shape)]
            if len(shape) > 1:
                v = v.rearrange(f"p ({' '.join(names)}) -> p {' '.join(names)}",
                                **{k: s for k, s in zip(names[1:], shape[1:])})
            return v

        K = 1024
        pows = area(0, GROUPS, STEP, GROUP)
        e1 = area(0, GROUPS, CHUNKS)
        e2 = area(2 * K, GROUPS, CHUNKS)
        z2 = area(0, GROUPS, CHUNKS)
        xprev = area(2 * K, GROUPS, CHUNKS)
        ubar = area(4 * K, GROUPS, GROUP)
        vbar = area(4 * K + 512, GROUPS, GROUP)
        cu = area(4 * K + 1024, GROUPS, GROUP)
        cv = area(4 * K + 1536, GROUPS, GROUP)
        bt = area(4 * K, GROUPS, P)
        z1 = area(4 * K, GROUPS, CHUNKS)
        zs = area(6 * K, GROUPS, CHUNKS)
        ych = area(4 * K, GROUPS, CHUNKS)
        yT = area(2 * K, UT, STEP, CHUNKS)
        vrows = area(8 * K, 5, P)
        frows = area(9 * K, 4, P)
        ca = area(8 * K, GROUPS, STEP + 1, GROUP)
        AT = 8 * K + GROUPS * (STEP + 1) * GROUP
        bu = area(AT, GROUPS, GROUP)
        bv = area(AT + 512, GROUPS, GROUP)
        cn = area(AT + 1024, 2, UT, P)
        kern = area(AT, GROUPS, P)
        uch = area(AT + 2 * K, GROUPS, CHUNKS)
        rot_c = area(AT + 4 * K, GROUPS, CHUNKS)
        rot_s = area(AT + 6 * K, GROUPS, CHUNKS)
        x_tok = area(AT + 8 * K, TT, D)
        u_st = area(AT + 8 * K, UT, STEP, CHUNKS)
        toep = area(AT + 8 * K, GROUPS, P)
        s5 = area(AT + 12 * K, S5_TERMS, GROUPS)
        ptmp = area(AT + 12 * K + S5_TERMS * GROUPS, 2, 512)
        AT2 = AT + 12 * K + S5_TERMS * GROUPS + K
        twist_tmp = area(AT + 10 * K, 2, 512)
        y_us = area(0, UT, STEP, CHUNKS)
        gelu_y = area(0, UT, T)
        y_ssm = area(8 * K, UT, T)
        qT = area(AT2, 4, T)
        kvT = area(AT2 + 2 * K, 6, T)
        v_tok = area(AT2 + 5 * K, 2, TT, P)
        kc = area(AT2 + 6 * K, KVG * NCMP)
        vc = area(AT2 + 6 * K + 64, KVG, HD)
        gsig = area(AT2 + 6 * K + 192, TT, 3 * HEADS)
        hid = area(AT2 + 6 * K + 288, 2, 64)
        knorm = area(AT2 + 6 * K + 420, 64)
        assert AT2 + 6 * K + 484 <= ARENA
        kv_swapped = area(AT, 2, T)
        blocks = sq, root
        kk = area(AT, 2, KVG, T)
        N = AT + 2 * K
        qn = area(N, 2, T)
        score = area(N + K, 2, 2, T)
        prob = area(N + 3 * K, 2, 2, T)
        probT = area(N + 5 * K, 2, 2, T)
        bias = area(N + 7 * K, 2, T)
        cscore = area(N + 8 * K, 2, NCMP)
        cprob = area(N + 8 * K + 64, 2, NCMP)
        cprobT = area(N + 8 * K + 128, 2, P)
        cbias = area(N + 8 * K + 384, 2, TT, NCMP)
        stats = area(N + 8 * K + 640, 2, 16)
        kcg = area(N + 8 * K + 672, NCMP)
        kkg = area(N + 9 * K, 2, T)
        o_tok = area(6 * K, TT, HEADS * HD)
        merged = area(0, DT, T)
        sig = area(12 * K, 2, T)
        prod = area(28 * K, 2, T)
        mix_hi, mix_lo = h_lo, hT_hi
        ssm_hi, ssm_lo = act_lo[:, 10:10 + UT], act_lo[:, 0:UT]
        nsa_hi, nsa_lo = act_lo[:, 4:8], act_hi[:, 8:12]
        merged_hi, merged_lo = h_lo, act_hi[:, 0:DT]
        h_new = area(8 * K, DT, T)
        assert FT * T + DT * T + 2 * SLOTS * DT * 2 * P == 28 * K
        relu = area(28 * K, 2, T)
        relu2 = root

        ml_q = area(0, MH, T)
        hg_g = area(2 * K, MH, T)
        y_all = area(0, 2 * MH, T)
        ml_k = area(4 * K, MH, S)
        hg_q = area(7 * K, MH, T)
        hg_k = area(9 * K, MH, 2, S)
        sums = area(15 * K, MH, SUMS)
        at = 15 * K + MH * SUMS
        hg_v = area(at, ST, MH * P)
        ml_v = area(at + ST * MH * P, ST, MH, P + 1)
        at += ST * MH * P + ST * MH * (P + 1)
        hcT = area(at, DT, C)
        W2 = at + DT * C
        ctx_tok = area(W2, CT, D)
        xcT = area(W2 + 2 * K, DT, C)
        block_of = area(W2 + 4 * K, P)
        mod_back = area(W2 + 4 * K + P, P)
        row_g = area(W2, 2, S)
        row_f = area(W2 + 2 * S, 2, S)
        row_b = area(W2 + 4 * S, 2, S)
        logf = area(W2, 2, ST, P + 1)
        sums1 = area(W2 + 2 * SEGS, SUMS)
        a_ctx = area(W2, CT, T)
        a_half = area(W2 + CT * T, TT, T // 2)
        a_pair = area(W2 + CT * T + TT * T // 2, TT, P)
        a_own = area(W2 + CT * T + TT * T // 2 + TT * P, TT, P)
        at = W2 + CT * T + TT * T // 2 + 2 * TT * P
        y_tok = area(at, TT, P)
        squared = area(at + TT * P, TT, P)
        at = W2 + 6 * S
        assert W2 + 2 * SEGS + SUMS <= at and W2 + 4 * K + 2 * P <= at
        gcol = area(at, 2, ST, MH)
        floor = area(at + 2 * ST * MH, 2, TT, MH)
        amod = area(at + 2 * ST * MH + 2 * TT * MH, 3, DT)
        lb = area(at + 2 * ST * MH + 2 * TT * MH + 3 * DT, 3, 2, MH)
        at += 2 * ST * MH + 2 * TT * MH + 3 * DT + 6 * MH
        stat2 = area(at, 4, 2 * TT)
        assert at + 8 * TT <= ARENA
        W3 = 7 * K
        qc = area(W3, MH, T)
        kc2 = area(W3 + MH * T, MH, S)
        W4 = W3 + MH * (T + S)
        cummax = area(W4, 2, T)
        o_sig = area(W4 + 2 * T, T)
        h_tok = area(W4 + 3 * T, TT, P)
        weight = area(W4 + 4 * T, 2, ST, T)
        keys = area(W4 + 4 * T + 2 * ST * T, S)
        assert W4 + 4 * T + 2 * ST * T + S <= 15 * K + MH * SUMS
        causal = area(W2, 2, P)
        raw = area(28 * K, 4, T)
        conv = area(30 * K, 4, T)
        gated = sq
        out_tok = area(0, TT, D)
        sums_v = sums[:, :, 0:2 * SEGS].rearrange("p h (d a n) -> p h d a n", d=2, a=ST)
        ek, eq, eq_b = sq, root, rstd

        def unit_tiles(u):
            t = T0["hg"] + u + sum(u > v for v in ML_AFTER)
            return [t] if u < HALVES else [t + u - HALVES + k for k in range(2)]

        def ml_tile(m):
            return unit_tiles(ML_AFTER[m])[0] + 1 + ML_AFTER[0:m].count(ML_AFTER[m])

        m_scr = nc.dram_tensor("m_scr", (2, MH, T), F32, kind="Internal").ap()

        def targets(w, d, s):
            b = s - CT
            if b < 0:
                return w[:, d, s, :]
            return w[:, d, s, b * P:] if d == 0 else w[:, d, s, 0:(b + 1) * P]
        banks = [ctx.enter_context(nc.psum_tensor(f"bank{i}", [P, T], F32)) for i in range(8)]
        acc = banks[:BANKS]
        stat = banks[4]
        mod_banks = banks[5], banks[7]
        mod_rows = ptmp[0:2, :, 0:2 * P]

        u_scr = nc.dram_tensor("u_scr", (UT * P, STEP, CHUNKS), F32, kind="Internal").ap()
        mod_scr = nc.dram_tensor("mod_scr", (2, NMOD * D), F32, kind="Internal").ap()
        y_scr = nc.dram_tensor("y_scr", (UT * P, STEP, CHUNKS), F32, kind="Internal").ap()

        loaded = [sem(f"chunk_loaded{i}") for i in range(SLOTS)]
        chunk_used = sem("chunk_used")
        acc_full = sem("acc_full")
        acc_out = [sem(f"acc_out{i}") for i in range(BANKS)]
        dve_step, act_step, pool_step = sem("dve_step"), sem("act_step"), sem("pool_step")
        consts = sem("consts")
        params, x_in, w_small = sem("params"), sem("x_in"), sem("w_small")
        sq_ready, sq_used = sem("sq_ready"), sem("sq_used")
        rstd_ready, h_ready = sem("rstd_ready"), sem("h_ready")
        s5_exp, s5_angle, s5_sin, s5_small, s5_bbar, pows_ready = (
            sem(n) for n in ("s5_exp", "s5_angle", "s5_sin", "s5_small", "s5_bbar", "pows_ready"))
        ca_ready, rot_ready = sem("ca_ready"), sem("rot_ready")
        u_out, u_in, toep_zero, toep_in = (sem(n) for n in ("u_out", "u_in", "toep_zero", "toep_in"))
        e_swapped, z_scanned, z_swapped, xprev_ready = (sem(n) for n in ("e_swapped", "z_scanned", "z_swapped", "xprev_ready"))
        y_out, y_in, y_sum, gelu_done, yssm_ready = (sem(n) for n in ("y_out", "y_in", "y_sum", "gelu_done", "yssm_ready"))
        silu_ready, mod_full, mod_out, mod_in, mod_flipped, mod_ready = (
            sem(n) for n in ("silu_ready", "mod_full", "mod_out", "mod_in", "mod_flipped", "mod_ready"))
        mod_stored = [sem(f"mod_stored{k}") for k in range(2)]
        kv_in, blocks_ready = sem("kv_in"), sem("blocks_ready")
        hid_full, hid_ready, kc_full, kc_sq, kc_mean, kc_ready, vc_full, vc_ready = (
            sem(n) for n in ("hid_full", "hid_ready", "kc_full", "kc_sq", "kc_mean", "kc_ready", "vc_full", "vc_ready"))
        qk_sq, qk_rstd, k_normed, k_dup = (sem(n) for n in ("qk_sq", "qk_rstd", "k_normed", "k_dup"))
        qn_ready, score_full, score_ready, prob_ready, cprob_ready = (
            sem(n) for n in ("qn_ready", "score_full", "score_ready", "prob_ready", "cprob_ready"))
        pt_full, pt_out, cpt_out, o_full, o_ready = (sem(n) for n in ("pt_full", "pt_out", "cpt_out", "o_full", "o_ready"))
        merged_ready, x1_ready, act_hi_ready, act_ready = (
            sem(n) for n in ("merged_ready", "x1_ready", "act_hi_ready", "act_ready"))
        mix_hi_ready, mix_ready, nsa_hi_ready, merged_hi_ready, merged_parts = (
            sem(n) for n in ("mix_hi_ready", "mix_ready", "nsa_hi_ready", "merged_hi_ready", "merged_parts"))
        h_new_ready, h_hi_ready = sem("h_new_ready"), sem("h_hi_ready")
        hi_ready, split_ready, split_used = sem("hi_ready"), sem("split_ready"), sem("split_used")
        stored = sem("stored")
        ctx_in, h_scaled = sem("ctx_in"), sem("h_scaled")
        g16_ready, rows_in, neg_ready, ln_ready, rows_ready, max_out, cols_ready = (
            sem(n) for n in ("g16_ready", "rows_in", "neg_ready", "ln_ready", "rows_ready", "max_out", "cols_ready"))
        lb_logit, lb_sig, lb_ready, same_ready, ones_ready = (
            sem(n) for n in ("lb_logit", "lb_sig", "lb_ready", "same_ready", "ones_ready"))
        z_ctx, z_ready, f_ready, logf_ready, sums_ready, sums_kept = (
            sem(n) for n in ("z_ctx", "z_ready", "f_ready", "logf_ready", "sums_ready", "sums_kept"))
        diff_ready, exp_ready, kq_ready, hg_o, hg_rstd, hg_y, hg_flipped, hg_done = (
            sem(n) for n in ("diff_ready", "exp_ready", "kq_ready", "hg_o", "hg_rstd", "hg_y", "hg_flipped", "hg_done"))
        max_in, qk_conv, qk_ready, gap_ready, w_ready, p_ready, p_masked, ml_o, ml_h, ml_rstd, ml_y = (
            sem(n) for n in ("max_in", "qk_conv", "qk_ready", "gap_ready", "w_ready", "p_ready", "p_masked", "ml_o",
                             "ml_h", "ml_rstd", "ml_y"))
        conv_ready, silu2_ready, gated_ready, gated_hi_ready, act2_ready = (
            sem(n) for n in ("conv_ready", "silu2_ready", "gated_ready", "gated_hi_ready", "act2_ready"))
        keys_ready = sem("keys_ready")
        out_ready = sem("out_ready")

        def rows(at, name, src, tile=0):
            n = src.shape[0]
            return vrows[VEC[name] - at:VEC[name] - at + n, tile, 0:src.shape[1]], src

        def of128(ap):
            return ap.rearrange("(r c) -> r c", c=P)

        param_loads = [rows(0, n, of128(a[n][0])) for n in ("norm1_g", "ssm_d", "ssm_b_glu", "norm2_g", "c_2",
                                                            "norm1_w_2", "norm2_w_2", "b_mod_2")]
        param_loads += [rows(0, n, of128(a[n])) for n in ("c_ctx_2", "final_norm_w_2")]
        param_loads += [rows(0, "hgrn_lb_logits_2", a["hgrn_lb_logits_2"].rearrange("d l (r c) -> (d l r) c", c=P)),
                        rows(VEC0, "mlstm_conv_w_2", a["mlstm_conv_w_2"][0].rearrange("y x (r c) -> (y x r) c", c=P), 1),
                        rows(VEC0, "mlstm_norm_w_2", of128(a["mlstm_norm_w_2"][0]), 1),
                        rows(VEC0, "hgrn_norm_w_2", of128(a["hgrn_norm_w_2"][0]), 1)]
        for h in range(2):
            half = slice(h * HD, (h + 1) * HD)
            for n, src in (("q_norm_g", a["q_norm_g"]), ("k_norm_g", a["k_norm_g"][0])):
                r = VEC[n] - VEC0
                param_loads.append((vrows[r:r + src.shape[0], 1, half], src))
            pe_rows = slice(h * CMP_BLOCK // 2, (h + 1) * CMP_BLOCK // 2)
            param_loads.append((vrows[pe_rows, 2, :], a[("cmp_pe_k", "cmp_pe_v")[h]][0].rearrange("(k r) d -> k (r d)", r=2)))
            for k, n in enumerate(("ssm_a_re", "ssm_a_im")):
                param_loads.append((vrows[0:GROUPS, 3 + k, half], a[n][0]))
            for k in range(2):
                n = ("re", "im")[(h + k) % 2]
                param_loads.append((cn[:, k, :, half],
                                    a["ssm_c_" + n][0].rearrange("g c p -> (g c) p").rearrange("(m q) p -> q m p", q=P)))
                param_loads.append(((bu, bv)[k][half], a["ssm_b_" + n][0].rearrange("g p c -> p g c")))
        param_loads.append((frows[0:99], a["ffn_conv_w_2"][0].rearrange("y x (r c) -> (y x r) c", c=P)
                            .rearrange("(m r) c -> r m c", r=99)))
        param_loads.append((s5[:, LOG_DT], a["ssm_log_dt"].to_broadcast([P, GROUPS])))
        gate_at = GROUPS * GROUP + HEADS * HD + 6 * KVG * HD
        mgate_at = 4 * MH * P
        small_loads = [(w_gate[:], a["w_in"][0][:, gate_at:gate_at + 3 * HEADS].rearrange("(k p) n -> p k n", p=P)),
                       (w_mgate[:], a["w_in_2"][0][:, mgate_at:mgate_at + 4 * MH].rearrange("(k p) n -> p k n", p=P)),
                       (mgate_b[:], a["mlstm_gate_b_2"].rearrange("a n -> n a")),
                       (wk2[:, 0], a["cmp_wk2"][0]), (wk2[:, 1], a["cmp_wk2"][0]), (wv2[:], a["cmp_wv2"][0])]
        CONSTS = 10 + HEADS


        def value(part):
            return part.bitcast(F32)

        def block_cols(kind):
            n = CMP_BLOCK // 2
            return blocks[kind][:].rearrange("p a n -> p (a n)")[:, 0:n * KVG * NCMP]\
                .rearrange("p (k g n) -> p k g n", k=n, g=KVG)

        block = ctx.enter_context(nc.Block())

        def full(eng, t, more=0):
            eng.wait_ge(acc_full, t + 1 + more)

        def copied(eng, t, more=0):
            eng.wait_ge(acc_out[t % BANKS], t // BANKS + 1 + more)

        def out_of(t, ins):
            ins.then_inc(acc_out[t % BANKS], 1)

        cells = iter(range(2, 24))

        def free(eng, place, n=1):
            cell = tick[:, next(cells)].unsqueeze(1)
            (eng.copy(cell, zero[:]) if eng is nc.scalar else eng.memset(cell, 0.0)).then_inc(place, n)

        def vcol(name, k=0):
            return vec[:, VEC[name] + k:VEC[name] + k + 1]

        @block.sync
        def _(sp):
            skipped = [0]

            def load(n, *pairs, i=0, per=0, split=None):
                if split is not None:
                    sp.wait_ge(split_ready, split + 1 + i * per)
                elif n >= SLOTS or per:
                    sp.wait_ge(chunk_used, n - SLOTS + 1 - skipped[0] + i * per)
                for dst, src in pairs:
                    sp.dma_start(dst, src).then_inc(loaded[n % SLOTS], 16)

            def columns(n, w, at, width, **kw):
                dst = ring[:, n % SLOTS, 0:DT * width].rearrange("p (k n) -> p k n", n=width)
                src = w[:, at:at + width] if isinstance(at, int) else w[:, ds(at, width)]
                src = src.rearrange("(k p) n -> p k n", p=P)
                half = DT // 2
                load(n, (dst[:, :half], src[:, :half]), (dst[:, half:], src[:, half:]), **kw)

            x_v = a["x"][0].rearrange("(t p) c -> p t c", p=P)
            for t in range(TT):
                sp.dma_start(x_tok[:, t], x_v[:, t]).then_inc(x_in, 16)
            w_in = a["w_in"][0]
            width = 2 * P
            for n in range(7):
                columns(n, w_in, n * width, width)
            def modulation(g):
                with sp.Fori(0, 4) as i:
                    for k in range(2):
                        columns(C0[f"mod{g}"] + k, a["w_mod_2"][0], i * (2 * width) + (8 * g + k) * width, width, i=i, per=2)

            modulation(0)
            for n in range(2):
                w1 = (a["cmp_wk1"], a["cmp_wv1"])[n][0].rearrange("(k p) n -> p k n", p=P)
                c = C0["cmp"] + n
                dst = ring[:, c % SLOTS, :].rearrange("p (k n) -> p k n", n=P)
                load(c, (dst[:, 0:8], w1[:, 0:8]), (dst[:, 8:16], w1[:, 8:16]))
            modulation(1)
            modulation(2)
            g = C0["glu"]
            w_glu = a["ssm_w_glu"][0].rearrange("(k p) n -> p k n", p=P)
            dst = ring[:, g % SLOTS, :].rearrange("p (k n) -> p k n", k=UT)
            load(g, (dst[:, 0:2], w_glu[:, 0:2]), (dst[:, 2:4], w_glu[:, 2:4]))
            gates_at = gate_at + 3 * HEADS
            def mixer(m, i, split=None):
                n = C0["merge"] + m
                dst = ring[:, n % SLOTS, 0:12 * P].rearrange("p (k n) -> p k n", n=P)
                load(n, (dst[:, 0:DT], w_in[:, ds(i * P + gates_at + m * D, P)].rearrange("(k p) n -> p k n", p=P)),
                     (dst[:, DT:], (a["w_proj_ssm"], a["w_proj_nsa"])[m][0][:, ds(i * P, P)].rearrange("(k p) n -> p k n", p=P)),
                     i=i, per=2, split=split)

            with sp.Fori(0, 1) as i:
                for m in range(2):
                    mixer(m, i)
            with sp.Fori(1, DT) as i:
                for m in range(2):
                    mixer(m, i, split=m - 2)

            def whole(name, w, chunks, split=None):
                with sp.Fori(0, chunks // 2) as i:
                    for k in range(2):
                        columns(C0[name] + k, w, i * (2 * width) + k * width, width, i=i, per=2,
                                split=None if split is None else split + k - 2)

            whole("out1", a["w_out"][0], 4, SPLIT0["out1"])
            for h in range(2):
                n, q = C0[f"up1_{h}"], SPLIT0[f"up1_{h}"]
                w = a["w_up"][0][:, h * FF // 2:(h + 1) * FF // 2]
                with sp.Fori(0, 4) as i:
                    for k in range(2):
                        columns(n + k, w, i * (2 * width) + k * width, width, i=i, per=2, split=q + k - 2)
                n, q = C0[f"down1_{h}"], SPLIT0[f"down1_{h}"]
                with sp.Fori(0, 2) as i:
                    for k in range(4):
                        w = a["w_down"][0][h * FF // 2 + k % 2 * D:h * FF // 2 + (k % 2 + 1) * D, :]
                        columns(n + k, w, i * (2 * width) + k // 2 * width, width, i=i, per=4, split=q + k - 2)
            skipped[0] += SPLITS1 - 1
            w_in2 = a["w_in_2"][0]
            hg_at = mgate_at + 4 * MH
            for m, at in enumerate((hg_at + 3 * MH * P, 2 * MH * P)):
                for k in range(2):
                    n = C0["v2"] + 2 * m + k
                    dst = ring[:, n % SLOTS, :].rearrange("p (k n) -> p k n", k=DT // 2)
                    src = w_in2[k * D // 2:(k + 1) * D // 2, at:at + MH * P].rearrange("(k p) n -> p k n", p=P)
                    load(n, (dst[:, 0:2], src[:, 0:2]), (dst[:, 2:4], src[:, 2:4]),
                         split=SPLITS1 - SLOTS + k if m == 0 else None)

            def pairs(n, w, ats, i, per, split=None):
                dst = ring[:, n % SLOTS, :].rearrange("p (m k n) -> p m k n", m=2, k=DT)
                load(n, *[(dst[:, m], w[:, ds(at, P)].rearrange("(k p) n -> p k n", p=P)) for m, at in enumerate(ats)],
                     i=i, per=per, split=split)

            with sp.Fori(0, MH) as i:
                for k, (m0, m1) in enumerate(((0, 1), (2, 4))):
                    pairs(C0["hg_in"] + k, w_in2, [i * P + hg_at + m * MH * P for m in (m0, m1)], i, 2)
            with sp.Fori(0, MH) as i:
                for k in range(2):
                    columns(C0["ml_in"] + k, w_in2, i * P + k * MH * P, P, i=i, per=2)
            with sp.Fori(0, MH) as i:
                for k in range(2):
                    n = C0["ml_o"] + k
                    dst = ring[:, n % SLOTS, 0:DT // 2 * P].rearrange("p (k n) -> p k n", n=P)
                    src = w_in2[k * D // 2:(k + 1) * D // 2, ds(i * P + 3 * MH * P, P)].rearrange("(k p) n -> p k n", p=P)
                    load(n, (dst[:, 0:2], src[:, 0:2]), (dst[:, 2:4], src[:, 2:4]), i=i, per=2)
            whole("out2", a["w_out_2"][0], 4)
            for h, width2 in enumerate(F2_HALF):
                n, q = C0[f"up2_{h}"], SPLIT0[f"up2_{h}"]

                def up(i, k, **kw):
                    at = h * F2_HALF[0] * P + k * P
                    pairs(n + k, a["w_up_2"][0], [i * (2 * P) + at + m * FF2 for m in range(2)], i, 2, **kw)

                if h == 0:
                    with sp.Fori(0, 1) as i:
                        for k in range(2):
                            up(i, k)
                with sp.Fori(1 - h, width2 // 2) as i:
                    for k in range(2):
                        up(i, k, split=q + k - 2)
                n, q = C0[f"down2_{h}"], SPLIT0[f"down2_{h}"]
                rows2 = slice(h * F2_HALF[0] * P, (h * F2_HALF[0] + width2) * P)
                with sp.Fori(0, 2) as i:
                    for k in range(4):
                        dst = ring[:, (n + k) % SLOTS, 0:width2 * P].rearrange("p (k n) -> p k n", n=P)
                        src = a["w_down_2"][0][rows2, ds(i * (4 * P) + k * P, P)].rearrange("(k p) n -> p k n", p=P)
                        half = width2 // 2
                        load(n + k, (dst[:, :half], src[:, :half]), (dst[:, half:], src[:, half:]), i=i, per=4,
                             split=q + k - 2)
            out_v = out[0].rearrange("(t p) c -> p t c", p=P)
            for t in range(TT):
                for k in range(2):
                    copied(sp, T0["final"] + 2 * t + k)
                sp.dma_start(out_v[:, t], out_tok[:, t]).then_inc(stored, 16)
            sp.wait_ge(stored, 16 * TT)

        @block.gpsimd
        def _(pool):
            step = Steps(pool, pool_step)

            def select(out, op, fill, base, pattern, mult):
                return pool.affine_select(out=out, in_=out, compare_op=op, fill=fill, base=base,
                                          pattern=pattern, channel_multiplier=mult)

            pool.memset(mean_d[:], 1.0 / D).then_inc(consts, 1)
            pool.memset(eps[:], EPS).then_inc(consts, 1)
            step(pool.memset(ident[:], 0.0))
            select(ident[:], ALU.not_equal, 1.0, 0, [[-1, P]], 1).then_inc(consts, 1)
            step.mark(pool.iota(dist[:], pattern=[[-1, T]], base=T - P, channel_multiplier=1,
                                allow_small_or_imprecise_dtypes=True))
            step(pool.iota(cdist[:], pattern=[[P, TT], [-CMP_STRIDE, NCMP]], base=1 - CMP_BLOCK, channel_multiplier=1,
                           allow_small_or_imprecise_dtypes=True))
            select(dist[:], ALU.is_ge, FAR, T - P, [[-1, T]], 1).then_inc(consts, 1)
            select(cdist[:], ALU.is_ge, FAR, 1 - CMP_BLOCK, [[P, TT], [-CMP_STRIDE, NCMP]], 1).then_inc(consts, 1)
            for h in range(HEADS):
                pool.memset(negslope[:, h:h + 1], -2.0 ** -(8.0 * (h + 1) / HEADS)).then_inc(consts, 1)

            def cols(k):
                return s5[:, k].unsqueeze(2).to_broadcast([P, GROUPS, GROUP])

            def twist(out, re, im, x, y):
                t0, t1 = (ptmp[:, k].rearrange("p (g c) -> p g c", c=GROUP) for k in range(2))
                step.mark(pool.tensor_tensor(t0, cols(re), x, ALU.mult))
                step(pool.tensor_tensor(t1, cols(im), y, ALU.mult))
                return pool.tensor_tensor(out, t0, t1, ALU.add)

            pool.wait_ge(s5_bbar, 2)
            for k in range(STEP):
                ins = twist(pows[:, :, STEP - 1 - k, :], PR + k, PI + k, ubar, vbar)
                if k < STEP - 1:
                    step(ins)
            ins.then_inc(pows_ready, 1)
            for m in range(UT):
                copied(pool, T0["u"] + m)
            pool.dma_start(u_scr.rearrange("(m p) s j -> p m s j", p=P), u_st).then_inc(u_out, 16)
            pool.wait_ge(u_out, 16)
            pool.wait_ge(rot_ready, 1)
            pool.memset(toep, 0.0).then_inc(toep_zero, 1)
            copied(pool, T0["kernel"] + 7)
            copied(pool, T0["kernel"] + 6)
            copied(pool, T0["kernel"] + 5)
            copied(pool, T0["kernel"] + 4)
            pool.wait_ge(toep_zero, 1)
            for s in range(STEP):
                pool.dma_start(toep[s * GROUP:(s + 1) * GROUP, :, s * GROUP:P],
                               kern[0:GROUP, :, 0:P - s * GROUP]).then_inc(toep_in, 16)
            pool.wait_ge(toep_in, 16 * STEP)
            for s in range(STEP):
                pool.dma_start(uch[s * GROUP:(s + 1) * GROUP],
                               u_scr[:, s, :].rearrange("(g c) j -> c g j", c=GROUP)).then_inc(u_in, 16)
            for m in range(2):
                copied(pool, T0["kv"] + m)
                pool.dma_start(kv_swapped[HD:P, m], kvT[0:HD, m]).then_inc(kv_in, 16)
                pool.dma_start(kv_swapped[0:HD, m], kvT[HD:P, m]).then_inc(kv_in, 16)
            for t in range(4):
                copied(pool, T0["state"] + t)
            pool.dma_start(e2[0:HD], e1[HD:P]).then_inc(e_swapped, 16)
            pool.dma_start(e2[HD:P], e1[0:HD]).then_inc(e_swapped, 16)
            pool.wait_ge(z_scanned, 1)
            pool.dma_start(z2[0:HD], zs[HD:P]).then_inc(z_swapped, 16)
            pool.dma_start(z2[HD:P], zs[0:HD]).then_inc(z_swapped, 16)
            for m in range(2):
                pool.wait_ge(k_normed, 2 * m + 2)
                pool.dma_start(kk[HD:P, m, 0], kk[0:HD, m, 0]).then_inc(k_dup, 16)
                pool.dma_start(kk[0:HD, m, 1], kk[HD:P, m, 1]).then_inc(k_dup, 16)
            for t in range(4):
                copied(pool, T0["y"] + t)
            for s in range(STEP):
                pool.dma_start(y_scr[:, s, :].rearrange("(g c) j -> c g j", c=GROUP),
                               ych[s * GROUP:(s + 1) * GROUP]).then_inc(y_out, 16)
            pool.wait_ge(y_out, 16 * STEP)
            pool.dma_start(y_us, u_scr.rearrange("(m p) s j -> p m s j", p=P)).then_inc(y_in, 16)
            pool.dma_start(yT, y_scr.rearrange("(m p) s j -> p m s j", p=P)).then_inc(y_in, 16)
            pool.wait_ge(merged_ready, 2)
            pool.dma_start(ctx_tok, a["ctx_2"][0].rearrange("(t p) c -> p t c", p=P)).then_inc(ctx_in, 16)
            for k in range(2):
                pool.wait_ge(mod_stored[k], 16 + 16 * 12)
            pool.dma_start(mod_back[0:2 * NMOD * DT], mod_scr.rearrange("c (m p) -> (c m) p", p=P)).then_inc(mod_in, 16)
            for k, b in enumerate(LEVELS):
                step(pool.memset(block_of, 1.0))
                grid = block_of.rearrange("p (g j) -> p g j", j=b)
                step(select(grid, ALU.is_ge, 0.0, 0, [[-b, P // b], [0, b]], 1))
                step(select(grid, ALU.is_ge, 0.0, b - 1, [[b, P // b], [0, b]], -1))
                pool.tensor_copy(same[:, k, :], block_of).then_inc(same_ready, 1)
                pool.wait_ge(same_ready, k + 1)
            pool.wait_ge(x1_ready, 2)
            pool.memset(ml_v[:, :, :, P:P + 1], 1.0).then_inc(ones_ready, 1)
            pool.wait_ge(g16_ready, 1)
            for k in range(4):
                row = (row_g, row_f)[k % 2]
                pool.dma_start(row[0:MH, k // 2, :], sq[k * MH:(k + 1) * MH].rearrange("p a n -> p (a n)")[:, 0:S])\
                  .then_inc(rows_in, 16)
            pool.wait_ge(rows_ready, 1)
            for d in range(2):
                pool.dma_start(m_scr[d], row_f[0:MH, d, C:S]).then_inc(max_out, 16)
            pool.wait_ge(max_out, 32)
            with pool.Fori(0, MH) as i:
                pool.wait_ge(sums_kept, i + 2)
                for u, m in enumerate(LEVELS):
                    full(pool, unit_tiles(u - 2)[0] if u >= 2 else unit_tiles(CONTEXT - u)[1] - 16, 16 * i)

                    def split(x):
                        return x.rearrange("p (a b t m) -> p a b t m", a=TT, t=2, m=m)

                    def upto(d, inclusive):
                        v = sums_v[:, ds(i, 1), d, CT:ST, inclusive:inclusive + P]
                        return v.rearrange("p o a (b t m) -> p (o a) b t m", t=2, m=m)

                    k_, q_ = split(ek[:, u % 2]), split(eq[:, u % 2])
                    half = [P, TT, P // (2 * m), m]
                    mid_f, mid_b = (upto(d, 0)[:, :, :, 1, 0:1].to_broadcast(half) for d in range(2))
                    pool.tensor_tensor(k_[:, :, :, 1], upto(1, 0)[:, :, :, 1], mid_b, ALU.subtract)
                    pool.tensor_tensor(k_[:, :, :, 0], mid_f, upto(0, 1)[:, :, :, 0], ALU.subtract)
                    pool.tensor_tensor(q_[:, :, :, 0], mid_b, upto(1, 0)[:, :, :, 0], ALU.subtract)
                    pool.tensor_tensor(q_[:, :, :, 1], upto(0, 1)[:, :, :, 1], mid_f, ALU.subtract)\
                        .then_inc(diff_ready, 1)
            pool.wait_ge(hg_done, MH)
            for d, sign_ in enumerate((1, -1)):
                step(pool.memset(causal[:, d], 1.0))
                step(select(causal[:, d], ALU.is_ge, 0.0, 0, [[sign_, P]], -sign_))
            pool.wait_ge(qk_ready, 2)
            with pool.Fori(0, MH) as i:
                pool.tensor_copy(keys.unsqueeze(1), kc2[:, ds(i, 1), :]).then_inc(keys_ready, 1)
                pool.wait_ge(gap_ready, 2 * ST * (i + 1))
                for d in range(2):
                    pool.dma_start(cummax[:, d, :], m_scr[d, ds(i, 1), :].partition_broadcast(P)).then_inc(max_in, 16)
                for n in range(2 * TT):
                    b, d = divmod(n, 2)
                    if d == 0:
                        pool.wait_ge(p_ready, ST * i + CT + b + 1)
                    else:
                        copied(pool, T0["ml"] + CT + b, 2 * i)
                    w = weight[:, d, CT + b, b * P:(b + 1) * P]
                    pool.tensor_tensor(w, w, causal[:, d], ALU.mult).then_inc(p_masked, 1)
            def low(n, q, more=0):
                pool.wait_ge(hi_ready, q + 1 + more)
                pool.tensor_tensor(w_lo[:, n % SLOTS, :], ring[:, n % SLOTS, :], value(w_hi[:, n % SLOTS, :]), ALU.subtract)\
                    .then_inc(split_ready, 1)

            for k in range(2):
                low(C0["up2_0"] + k, SPLITS1 + k)
            for h, width2 in enumerate(F2_HALF):
                n, q = C0[f"up2_{h}"], SPLIT0[f"up2_{h}"]
                done = h * F2_HALF[0]

                def gate(i, j):
                    pool.wait_ge(silu2_ready, done + 2 * i + j + 1)
                    pool.tensor_tensor(gated[:, j], conv[:, 2 * j], conv[:, 2 * j + 1], ALU.mult).then_inc(gated_ready, 1)

                def gated_low(i, j):
                    pool.wait_ge(gated_hi_ready, done + 2 * i + j + 1)
                    pool.tensor_tensor(act_lo[:, ds(2 * i + j, 1), :], gated[:, j].unsqueeze(1),
                                       value(act_hi[:, ds(2 * i + j, 1), :]), ALU.subtract).then_inc(act2_ready, 1)

                def round_(i, first):
                    low(n + 2, q + 2, 2 * i)
                    if not first:
                        gated_low(i - 1, 0)
                        gate(i - 1, 1)
                    low(n + 3, q + 3, 2 * i)
                    if not first:
                        gated_low(i - 1, 1)
                    gate(i, 0)

                last = width2 // 2 - 1
                with pool.Fori(0, 1) as i:
                    round_(i, True)
                with pool.Fori(1, last + 1) as i:
                    round_(i, False)
                with pool.Fori(last, last + 1) as i:
                    gated_low(i, 0)
                    gate(i, 1)
                    gated_low(i, 1)
                n, q = C0[f"down2_{h}"], SPLIT0[f"down2_{h}"]
                if h == 0:
                    with pool.Fori(0, 2) as i:
                        for k in range(2, 6):
                            low(n + k, q + k, 4 * i)
                else:
                    for k in range(2, 8):
                        low(n + k, q + k)

        @block.tensor
        def _(pe):
            def claim(t, more=0):
                if t >= BANKS:
                    pe.wait_ge(acc_out[t % BANKS], t // BANKS + more)

            def arrived(n, more=0):
                pe.wait_ge(loaded[n % SLOTS], 32 * (n // SLOTS + 1) + 32 * more)

            def slot(n, k=DT):
                return ring[:, n % SLOTS, :].rearrange("p (k n) -> p k n", k=k)

            def flip(out, in_, rows=P):
                return pe.matmul(out, in_, ident[0:rows, 0:rows], is_transpose=True)

            def mean_square(ready, used, n):
                for k in range(DT):
                    pe.wait_ge(sq_ready, ready + k + 1)
                    pe.matmul(stat[:, 0:n], mean_d[:], sq[:, k % 2, 0:n], start=k == 0, stop=k == DT - 1)\
                      .then_inc(sq_used, 1)

            def linear(t, n, src, tiles=2, kt=DT, i=0, tile_rounds=0, slot_rounds=0, wait=None):
                arrived(n, i * slot_rounds)
                w = slot(n, kt)
                for m in range(tiles):
                    claim(t + m, i * tile_rounds)
                    for k in range(kt):
                        if wait is not None and m == 0:
                            pe.wait_ge(h_ready, wait + k + 1)
                        ins = pe.matmul(acc[(t + m) % BANKS][:], w[:, k, m * P:(m + 1) * P], src[:, k, :],
                                        start=k == 0, stop=k == kt - 1)
                        if m == 0 and k == 0 and n:
                            ins.then_inc(chunk_used, 1)
                    ins.then_inc(acc_full, 1)

            pe.wait_ge(consts, CONSTS)
            pe.wait_ge(params, 16 * len(param_loads))
            v = acc[0]
            flip(v[:, 0:P], vrows[:, 0, :])
            flip(v[:, VEC0:VEC1], vrows[0:VEC1 - VEC0, 1, :], VEC1 - VEC0)
            for k in range(3):
                ins = flip(v[:, VEC1 + 32 * k:VEC1 + 32 * (k + 1)], vrows[0:32, 2 + k, :], 32)
            ins.then_inc(acc_full, 1)
            for m in range(4):
                ins = flip(acc[1][:, 99 * m:99 * (m + 1)], frows[0:99, m, :], 99)
            ins.then_inc(acc_full, 1)
            for k in range(2):
                for m in range(UT):
                    ins = flip(acc[2 + k][:, m * P:(m + 1) * P], cn[:, k, m, :])
                ins.then_inc(acc_full, 1)
            pe.wait_ge(x_in, 16 * TT)
            for c in range(DT):
                t = T0["x"] + c
                claim(t)
                for m in range(TT):
                    ins = flip(acc[t % BANKS][:, m * P:(m + 1) * P], x_tok[:, m, c * P:(c + 1) * P])
                ins.then_inc(acc_full, 1)
            mean_square(0, 0, T)
            def projections(name, chunks, start):
                for n in range(chunks):
                    linear(T0[name] + 2 * n, C0[name] + n, hT, wait=start if n == 0 else None)

            projections("u", 2, 0)
            projections("q", 2, None)
            pe.wait_ge(ca_ready, 1)
            for m in range(8):
                t = T0["kernel"] + m
                claim(t)
                for g in range(4):
                    ins = pe.matmul(acc[t % BANKS][0:GROUP, g * P:(g + 1) * P], ubar[:, 4 * m + g, :],
                                    ca[:, 4 * m + g, 0:STEP, :], start=True, stop=True)
                ins.then_inc(acc_full, 1)
            pe.wait_ge(pows_ready, 1)
            for m in range(8):
                t = T0["bt"] + m
                claim(t)
                for g in range(4):
                    ins = flip(acc[t % BANKS][:, g * P:(g + 1) * P],
                               pows[:, 4 * m + g].rearrange("p s c -> p (s c)"))
                ins.then_inc(acc_full, 1)
            projections("kv", 3, None)
            t = T0["gates"]
            claim(t)
            pe.wait_ge(w_small, 16 * len(small_loads))
            for m in range(TT):
                for k in range(DT):
                    ins = pe.matmul(acc[t % BANKS][:, 24 * m:24 * (m + 1)], hT[:, k, m * P:(m + 1) * P],
                                    w_gate[:, k, :], start=k == 0, stop=k == DT - 1)
            ins.then_inc(acc_full, 1)
            for m in range(2):
                copied(pe, T0["bt"] + 6 + m)
            pe.wait_ge(u_in, 16 * STEP)
            for m in range(4):
                t = T0["state"] + m
                claim(t)
                for g in range(8):
                    if g % 4 == 0:
                        copied(pe, T0["bt"] + 2 * m + g // 4)
                    ins = pe.matmul(acc[t % BANKS][:, g * CHUNKS:(g + 1) * CHUNKS], bt[:, 8 * m + g, :],
                                    uch[:, 8 * m + g, :], start=True, stop=True)
                ins.then_inc(acc_full, 1)
            pe.wait_ge(silu_ready, 2)

            def modulation(g):
                with pe.Fori(0, 4) as i:
                    for k in range(2):
                        n = C0[f"mod{g}"] + k
                        arrived(n, i)
                        w = slot(n)
                        pe.wait_ge(mod_out, 2 * i + 8 * g + k + 1)
                        for kt in range(DT):
                            ins = pe.matmul(mod_banks[k][0:2, 0:2 * P], silu_c[:, kt, :], w[:, kt, :],
                                            start=kt == 0, stop=kt == DT - 1)
                            if kt == 0:
                                ins.then_inc(chunk_used, 1)
                        ins.then_inc(mod_full, 1)

            modulation(0)
            for kind in range(2):
                n = C0["cmp"] + kind
                arrived(n)
                pe.wait_ge(blocks_ready, 8 * kind + 8)
                for k in range(CMP_BLOCK // 2):
                    ins = pe.matmul(banks[(6, 4)[kind]][:, 0:KVG * NCMP], slot(n, 2 * DT)[:, k, :],
                                    block_cols(kind)[:, k].rearrange("p g n -> p (g n)"),
                                    start=k == 0, stop=k == CMP_BLOCK // 2 - 1)
                    if k == 0:
                        ins.then_inc(chunk_used, 1)
                ins.then_inc(hid_full, 1)
            for m in range(2):
                t = T0["v_tok"] + m
                claim(t)
                copied(pe, T0["kv"] + 3 + 2 * m)
                for b in range(TT):
                    ins = flip(acc[t % BANKS][:, b * P:(b + 1) * P], kvT[:, 3 + 2 * m, b * P:(b + 1) * P])
                ins.then_inc(acc_full, 1)
            modulation(1)
            for m in range(6):
                t = T0["qk_norm"] + m
                claim(t)
                pe.wait_ge(sq_ready, DT + m + 1)
                pe.matmul(acc[t % BANKS][:], mean_hd[:], sq[:, m % 2, :], start=True, stop=True).then_inc(acc_full, 1)
            pe.wait_ge(hid_ready, 2)
            pe.matmul(stat[:, 64:64 + KVG * NCMP], wk2[:].rearrange("p a n -> p (a n)"), hid[:, 0, 0:KVG * NCMP],
                      start=True, stop=True).then_inc(kc_full, 1)
            for g in range(KVG):
                ins = pe.matmul(banks[6][0:NCMP, g * HD:(g + 1) * HD], hid[:, 1, g * NCMP:(g + 1) * NCMP],
                                wv2[:], start=True, stop=True)
            ins.then_inc(vc_full, 1)
            pe.wait_ge(kc_sq, 1)
            pe.matmul(stat[:, 128:128 + KVG * NCMP], mean_hd[:], knorm[:, 0:KVG * NCMP],
                      start=True, stop=True).then_inc(kc_mean, 1)
            modulation(2)
            pe.wait_ge(toep_in, 16 * STEP)
            pe.wait_ge(xprev_ready, 1)
            for m in range(4):
                t = T0["y"] + m
                claim(t)
                for g in range(8):
                    o = acc[t % BANKS][:, g * CHUNKS:(g + 1) * CHUNKS]
                    pe.matmul(o, toep[:, 8 * m + g, :], uch[:, 8 * m + g, :], start=True, stop=False)
                    ins = pe.matmul(o, ca[:, 8 * m + g, 1:, :].rearrange("p s c -> p (s c)"), xprev[:, 8 * m + g, :],
                                    start=False, stop=True)
                ins.then_inc(acc_full, 1)
            pe.wait_ge(vc_ready, 1)
            for t in range(T0["y"], T0["y"] + 4):
                copied(pe, t)
            copied(pe, T0["v_tok"])
            copied(pe, T0["v_tok"] + 1)
            QUERIES = HPG * TT
            with pe.Fori(0, KVG) as gi:
                def scores(n):
                    hg, tt = divmod(n, TT)
                    half = slice(hg % 2 * HD, (hg % 2 + 1) * HD)
                    q = qn[half, hg // 2, tt * P:(tt + 1) * P]
                    if tt == 0 and hg % 2 == 0:
                        pe.wait_ge(qn_ready, 5 * gi + hg // 2 + 4)
                    if n:
                        pe.wait_ge(score_ready, gi * QUERIES + n)
                    pe.matmul(stat[:, 0:NCMP], q, kcg[half],
                              start=True, stop=True)
                    for m in range(2):
                        ins = pe.matmul(banks[m][:, 0:(tt + 1) * P], q,
                                        kkg[half, m, 0:(tt + 1) * P],
                                        start=True, stop=True)
                    ins.then_inc(score_full, 1)

                scores(0)
                for n in range(QUERIES):
                    tt = n % TT
                    if n + 1 < QUERIES:
                        scores(n + 1)
                    pe.wait_ge(prob_ready, gi * QUERIES + n + 1)
                    for m in range(2):
                        for b in range(tt + 1):
                            flip(banks[5 + m][:, b * P:(b + 1) * P], prob[:, n % 2, m, b * P:(b + 1) * P])
                    pe.wait_ge(cprob_ready, gi * QUERIES + n + 1)
                    flip(banks[3][0:NCMP, 0:P], cprob[:, n % 2, :]).then_inc(pt_full, 1)
                    pe.wait_ge(pt_out, gi * QUERIES + n + 1)
                    pe.wait_ge(cpt_out, gi * QUERIES + n + 1)
                    if n >= 2:
                        pe.wait_ge(o_ready, gi * QUERIES + n - 1)
                    o = banks[(2, 7)[n % 2]][:, 0:3 * HD]
                    for m in range(2):
                        for b in range(tt + 1):
                            pe.matmul(o[:, (m + 1) * HD:(m + 2) * HD], probT[:, n % 2, m, b * P:(b + 1) * P],
                                      v_tok[:, m, b, ds(gi * HD, HD)], start=b == 0, stop=b == tt)
                    pe.matmul(o[:, 0:HD], cprobT[0:NCMP, n % 2, :], vc[0:NCMP, ds(gi, 1), :].rearrange("p a n -> p (a n)"),
                              start=True, stop=True).then_inc(o_full, 1)
                pe.wait_ge(o_ready, gi * QUERIES + QUERIES)
            for c in range(4):
                t = T0["o_nsa"] + c
                claim(t)
                for m in range(TT):
                    ins = flip(acc[t % BANKS][:, m * P:(m + 1) * P], o_tok[:, m, c * P:(c + 1) * P])
                ins.then_inc(acc_full, 1)
            pe.wait_ge(gelu_done, UT)
            linear(T0["glu"], C0["glu"], gelu_y, tiles=UT, kt=UT)
            pe.wait_ge(yssm_ready, UT)
            for c in range(4):
                copied(pe, T0["o_nsa"] + c)
            def product(out, w, x, n, more, q, start, stop, ready=None):
                for k, cols in w:
                    if ready:
                        pe.wait_ge(ready[0], ready[1] + k + 1)
                    for m, (u, v) in enumerate(((w_hi, x[0]), (w_hi, x[1]), (w_lo, x[0]))):
                        ins = pe.matmul(out, u[:, n % SLOTS, cols], v[:, k, :],
                                        start=start and k == w[0][0] and m == 0, stop=stop and k == w[-1][0] and m == 2)
                        if q and k == w[0][0] and m == 0:
                            ins.then_inc(split_used, 1)
                return ins

            pe.wait_ge(mix_ready, 1)
            with pe.Fori(0, DT) as i:
                for m in range(2):
                    n = C0["merge"] + m
                    pe.wait_ge(split_ready, m + 1 + 2 * i)
                    ys = ((ssm_hi, ssm_lo), (nsa_hi, nsa_lo))[m]
                    for j, (at, kt, x) in enumerate(((0, DT, (mix_hi, mix_lo)), (DT, 4, ys))):
                        t = T0["merge"] + 2 * m + j
                        claim(t, i)
                        if j == 1:
                            pe.wait_ge(mix_ready, 1 + UT)
                        w = [(k, slice((at + k) * P, (at + k + 1) * P)) for k in range(kt)]
                        product(acc[t % BANKS][:], w, x, n, i, j == 0, True, True).then_inc(acc_full, 1)

            def wide(name, x, rounds, ready=None):
                n, q, t = C0[name], SPLIT0[name], T0[name]
                with pe.Fori(0, rounds) as i:
                    for c in range(2):
                        pe.wait_ge(split_ready, q + c + 1 + 2 * i)
                        for m in range(2):
                            b = t + 2 * c + m
                            claim(b, i)
                            w = [(k, slice((2 * k + m) * P, (2 * k + m + 1) * P)) for k in range(DT)]
                            product(acc[b % BANKS][:], w, x, n + c, i, m == 0, True, True, ready if c + m == 0 else None)\
                                .then_inc(acc_full, 1)

            wide("out1", (merged_hi, merged_lo), 2, (merged_parts, 0))
            mean_square(DT + 6, DT, T)
            def looped(name, src, rounds):
                with pe.Fori(0, rounds) as i:
                    for k in range(2):
                        linear(T0[name] + 2 * k, C0[name] + k, src, i=i, tile_rounds=1, slot_rounds=1)

            for h in range(2):
                wide(f"up1_{h}", (hT_hi, h_lo), 4, (h_ready, DT))
                n, q, t = C0[f"down1_{h}"], SPLIT0[f"down1_{h}"], T0[f"down1_{h}"]
                pe.wait_ge(act_ready, 2 + (h + 1) * FT // 2)
                with pe.Fori(0, 2) as i:
                    for c in range(4):
                        pe.wait_ge(split_ready, q + c + 1 + 4 * i)
                        for m in range(2):
                            b = t + c // 2 * 2 + m
                            if c % 2 == 0:
                                claim(b, i)
                            w = [(k + c % 2 * DT, slice((2 * k + m) * P, (2 * k + m + 1) * P)) for k in range(DT)]
                            ins = product(acc[b % BANKS][:], w, (act_hi, act_lo), n + c, i, m == 0, c % 2 == 0, c % 2 == 1)
                            if c % 2:
                                ins.then_inc(acc_full, 1)
            pe.wait_ge(mod_in, 16)
            flip(mod_banks[0][:, 0:2 * NMOD * DT], mod_back[0:2 * NMOD * DT], 2 * NMOD * DT).then_inc(mod_flipped, 1)
            pe.wait_ge(ctx_in, 16)
            for c in range(4):
                t = T0["ctx"] + c
                claim(t)
                for k in range(2):
                    for m in range(CT):
                        ins = flip(acc[t % BANKS][:, k * C + m * P:k * C + (m + 1) * P],
                                   ctx_tok[:, m, (2 * c + k) * P:(2 * c + k + 1) * P])
                ins.then_inc(acc_full, 1)
            norms = DT + 6 + DT
            mean_square(norms, 2 * DT, C)
            pe.wait_ge(rstd_ready, 3)
            mean_square(norms + DT, 3 * DT, T)
            pe.wait_ge(h_ready, 4 * DT)
            for m, src in enumerate((hT, hcT)):
                t, n = T0["gate_rows"] + m, (T, C)[m]
                claim(t)
                for k in range(DT):
                    ins = pe.matmul(acc[t % BANKS][0:4 * MH, 0:n], w_mgate[:, k, :], src[:, k, 0:n],
                                    start=k == 0, stop=k == DT - 1)
                ins.then_inc(acc_full, 1)
            for m in range(2):
                n = C0["v2"] + 2 * m
                arrived(n)
                for b in range(ST):
                    t = T0["v2"] + ST * m + b
                    claim(t)
                    for k in range(DT):
                        if (b, k) == (0, DT // 2):
                            arrived(n + 1)
                        src = hcT[:, k, b * P:(b + 1) * P] if b < CT else hT[:, k, (b - CT) * P:(b - CT + 1) * P]
                        w = ring[:, (n + k // 4) % SLOTS, :].rearrange("p (k n) -> p k n", k=DT // 2)[:, k % 4, :]
                        ins = pe.matmul(acc[t % BANKS][:], src, w, start=k == 0, stop=k == DT - 1)
                        if (b, k) in ((0, 0), (ST - 1, DT // 2)):
                            ins.then_inc(chunk_used, 1)
                    ins.then_inc(acc_full, 1)
            t = T0["gate_cols"]
            claim(t)
            pe.wait_ge(rows_ready, 1)
            for d in range(2):
                for b in range(ST):
                    at = (d * ST + b) * MH
                    flip(acc[t % BANKS][:, at:at + MH], row_g[0:MH, d, b * P:(b + 1) * P], MH)
                for b in range(TT):
                    at = (2 * ST + d * TT + b) * MH
                    ins = flip(acc[t % BANKS][:, at:at + MH], row_b[0:MH, d, C + b * P:C + (b + 1) * P], MH)
            ins.then_inc(acc_full, 1)

            with pe.Fori(0, MH) as i:
                t = T0["hg_in"]
                for c in range(2):
                    n = C0["hg_in"] + c
                    arrived(n, i)
                    w = ring[:, n % SLOTS, :].rearrange("p (m k n) -> p m k n", m=2, k=DT)
                    for m in range(2):
                        b = t + 2 * c + m
                        claim(b, i)
                        for k in range(DT):
                            ins = pe.matmul(acc[b % BANKS][:], w[:, m, k, :], hT[:, k, :], start=k == 0, stop=k == DT - 1)
                            if m == 0 and k == 0:
                                ins.then_inc(chunk_used, 1)
                        ins.then_inc(acc_full, 1)
                        if m != c:
                            if c == 0:
                                pe.wait_ge(z_ready, i + 1)
                            for k in range(DT):
                                ins = pe.matmul(banks[5][:, c * C:(c + 1) * C], w[:, m, k, :], hcT[:, k, :],
                                                start=k == 0, stop=k == DT - 1)
                            ins.then_inc(z_ctx, 1)
            for b in range(ST):
                copied(pe, T0["v2"] + b)
            with pe.Fori(0, MH) as i:
                def ml_project(m):
                    c, src, b = min(m, 1), (hT, hT, hcT)[m], ml_tile(m)
                    n = C0["ml_in"] + c
                    if m < 2:
                        arrived(n, i)
                    w = ring[:, n % SLOTS, 0:DT * P].rearrange("p (k n) -> p k n", k=DT)
                    claim(b, 4 * i)
                    cols = C if m == 2 else T
                    for k in range(DT):
                        ins = pe.matmul(acc[b % BANKS][:, 0:cols], w[:, k, :], src[:, k, :],
                                        start=k == 0, stop=k == DT - 1)
                        if m < 2 and k == 0:
                            ins.then_inc(chunk_used, 1)
                    ins.then_inc(acc_full, 1)

                for u in range(UNITS):
                    tiles = unit_tiles(u)
                    for b in tiles:
                        claim(b, 4 * i)
                    pe.wait_ge(kq_ready, UNITS * i + u + 1)
                    o = [acc[b % BANKS] for b in tiles]
                    k_, q_ = ek[:, u % 2, :], eq[:, u % 2, :]
                    for s in range(TT):
                        ks = k_[:, s * P:(s + 1) * P]
                        if u <= PAIRS:
                            other = s if u < PAIRS else s ^ 1
                            ins = pe.matmul(o[0][:, s * P:(s + 1) * P], ks, q_[:, other * P:(other + 1) * P],
                                            start=True, stop=True)
                        elif u == HALVES:
                            other = C if s < 2 else 0
                            ins = pe.matmul(o[s // 2][:, s % 2 * C:(s % 2 + 1) * C], ks, q_[:, other:other + C],
                                            start=True, stop=True)
                            if s % 2:
                                ins.then_inc(acc_full, 1)
                        else:
                            c, d = divmod(s, 2)
                            ins = pe.matmul(o[c][:], k_[:, d * C + c * P:d * C + (c + 1) * P], (q_, eq_b[:])[d],
                                            start=d == 0, stop=d == 1)
                            if d:
                                ins.then_inc(acc_full, 1)
                    if u <= PAIRS:
                        ins.then_inc(acc_full, 1)
                    for m in range(3):
                        if ML_AFTER[m] == u:
                            ml_project(m)
                for b in range(16 - BANKS, 16):
                    copied(pe, T0["hg"] + b, 4 * i)
                for b in range(TT):
                    for s in range(ST):
                        if s < CT:
                            w = a_ctx[:, s, b * P:(b + 1) * P]
                        elif s - CT == b:
                            w = a_own[:, b, :]
                        elif s - CT == b ^ 1:
                            w = a_pair[:, s - CT, :]
                        else:
                            w = a_half[:, s - CT, b % 2 * P:(b % 2 + 1) * P]
                        ins = pe.matmul(banks[4][:, b * P:(b + 1) * P], w,
                                        hg_v[:, s, ds(i * P, P)], start=s == 0, stop=s == ST - 1)
                ins.then_inc(hg_o, 1)
                pe.wait_ge(hg_y, i + 1)
                for b in range(TT):
                    ins = flip(banks[6][:, b * P:(b + 1) * P], y_tok[:, b, :])
                ins.then_inc(hg_flipped, 1)
            pe.wait_ge(hg_done, MH)
            for b in range(ST):
                copied(pe, T0["v2"] + ST + b)
            pe.wait_ge(ones_ready, 1)
            pe.wait_ge(qk_ready, 2)
            with pe.Fori(0, MH) as i:
                t = T0["ml"]
                pe.wait_ge(keys_ready, i + 1)
                for s in range(ST):
                    b = t + s
                    claim(b, 2 * i)
                    pe.matmul(acc[b % BANKS][:], keys[:, s * P:(s + 1) * P], qc[:, ds(i, 1), :].rearrange("p o n -> p (o n)"),
                              start=True, stop=True).then_inc(acc_full, 1)
                pe.wait_ge(p_ready, ST * (i + 1))
                for s in range(ST - BANKS, ST):
                    copied(pe, t + s, 2 * i)
                pe.wait_ge(p_masked, 2 * TT * (i + 1))
                for b in range(TT):
                    for d in range(2):
                        srcs = [s for s in range(ST) if s < CT or (s - CT <= b if d == 0 else s - CT >= b)]
                        for s in srcs:
                            ins = pe.matmul(banks[4 + b][:, d * (P + 1):(d + 1) * (P + 1)],
                                            weight[:, d, s, b * P:(b + 1) * P],
                                            ml_v[:, s, ds(i, 1), :].rearrange("p o n -> p (o n)"),
                                            start=s == srcs[0], stop=s == srcs[-1])
                    ins.then_inc(ml_o, 1)
                claim(t + 6, 2 * i)
                for c in range(2):
                    n = C0["ml_o"] + c
                    arrived(n, i)
                    w = ring[:, n % SLOTS, 0:DT // 2 * P].rearrange("p (k n) -> p k n", n=P)
                    for k in range(DT // 2):
                        ins = pe.matmul(acc[(t + 6) % BANKS][:], w[:, k, :], hT[:, c * DT // 2 + k, :],
                                        start=c == 0 and k == 0, stop=c == 1 and k == DT // 2 - 1)
                        if k == 0:
                            ins.then_inc(chunk_used, 1)
                ins.then_inc(acc_full, 1)
                claim(t + 7, 2 * i)
                pe.wait_ge(ml_y, i + 1)
                for b in range(TT):
                    ins = flip(acc[(t + 7) % BANKS][:, b * P:(b + 1) * P], h_tok[:, b, :])
                ins.then_inc(acc_full, 1)
            for b in range(MH * 8 - 4, MH * 8):
                copied(pe, T0["ml"] + b)
            looped("out2", y_all, 2)
            mean_square(norms + 2 * DT, 4 * DT, T)
            for h, width2 in enumerate(F2_HALF):
                n, q, t = C0[f"up2_{h}"], SPLIT0[f"up2_{h}"], T0[f"up2_{h}"]
                with pe.Fori(0, width2 // 2) as i:
                    for c in range(2):
                        pe.wait_ge(split_ready, q + c + 1 + 2 * i)
                        for m in range(2):
                            b = t + 2 * c + m
                            claim(b, i)
                            w = [(k, slice((m * DT + k) * P, (m * DT + k + 1) * P)) for k in range(DT)]
                            product(acc[b % BANKS][:], w, (hT_hi, h_lo), n + c, i, m == 0, True, True,
                                    (h_ready, 4 * DT) if c + m == 0 else None).then_inc(acc_full, 1)
                n, q, t = C0[f"down2_{h}"], SPLIT0[f"down2_{h}"], T0[f"down2_{h}"]
                w = [(k, slice(k * P, (k + 1) * P)) for k in range(width2)]
                early, late = w[:-2], w[-2:]

                def down(c, i, rows, counts):
                    ins = product(acc[(t + c) % BANKS][:], rows, (act_hi, act_lo), n + c, i, counts,
                                  rows[0] == w[0], rows[-1] == w[-1])
                    if rows[-1] == w[-1]:
                        ins.then_inc(acc_full, 1)

                def chunk(c, i):
                    pe.wait_ge(split_ready, q + c + 1 + 4 * i)
                    claim(t + c, i)

                with pe.Fori(0, 1) as i:
                    pe.wait_ge(act2_ready, h * F2_HALF[0] + len(early))
                    for c in range(2):
                        chunk(c, i)
                        down(c, i, early, c == 0)
                    pe.wait_ge(act2_ready, h * F2_HALF[0] + width2)
                    for c in range(2):
                        down(c, i, late, c == 1)
                    for c in range(2, 4):
                        chunk(c, i)
                        down(c, i, w, True)
                with pe.Fori(1, 2) as i:
                    for c in range(4):
                        chunk(c, i)
                        down(c, i, w, True)
            mean_square(norms + 3 * DT, 5 * DT, T)
            pe.wait_ge(out_ready, DT)
            for t in range(TT):
                for k in range(2):
                    b = T0["final"] + 2 * t + k
                    claim(b)
                    for c in range(4):
                        ins = flip(acc[b % BANKS][:, c * P:(c + 1) * P], hT[:, 4 * k + c, t * P:(t + 1) * P])
                    ins.then_inc(acc_full, 1)

        @block.scalar
        def _(sc):
            step = Steps(sc, act_step)

            def squares(src, n, used):
                for k in range(DT):
                    if used + k >= 2:
                        sc.wait_ge(sq_used, used + k - 1)
                    sc.activation(sq[:, k % 2, 0:n], src[:, k, 0:n], ACT.Square).then_inc(sq_ready, 1)

            def inverse_root(dst, src):
                step(sc.activation(dst, src, ACT.Ln, bias=eps[0:dst.shape[0]]))
                return sc.activation(dst, dst, ACT.Exp, scale=-0.5)

            for dst, src in param_loads:
                sc.dma_start(dst, src).then_inc(params, 16)
            for dst, src in small_loads:
                sc.dma_start(dst, src).then_inc(w_small, 16)
            sc.wait_ge(consts, CONSTS)
            full(sc, 0)
            out_of(0, sc.copy(vec[:], acc[0][:, 0:VEC_COLS]))
            full(sc, 1)
            out_of(1, sc.copy(ffn_taps[:], acc[1][:, 0:TAPS * 2 * F2T]))
            full(sc, 2)
            out_of(2, sc.mul(cu.rearrange("p g c -> p (g c)"), acc[2][:], sign[:]))
            full(sc, 3)
            out_of(3, sc.mul(cv.rearrange("p g c -> p (g c)"), acc[3][:], -1.0))
            sc.wait_ge(params, 16 * len(param_loads))
            sc.activation(s5[:, DT_], s5[:, LOG_DT], ACT.Exp).then_inc(s5_exp, 1)
            for c in range(DT):
                t = T0["x"] + c
                full(sc, t)
                out_of(t, sc.copy(xT[:, c, :], acc[t % BANKS][:]))
            for c in range(BANKS):
                copied(sc, T0["x"] + DT - BANKS + c)
            squares(xT, T, 0)
            sc.wait_ge(sq_used, DT)
            inverse_root(rstd[:], stat[:]).then_inc(rstd_ready, 1)
            sc.wait_ge(s5_small, 1)
            sc.activation(s5[:, MAG], s5[:, AR_DT], ACT.Exp).then_inc(s5_exp, 1)
            sc.activation(s5[:, MAG_STEP], s5[:, AR_DT], ACT.Exp, scale=float(STEP)).then_inc(s5_exp, 1)
            sc.wait_ge(s5_angle, 1)
            sc.activation(s5[:, SIN_H], s5[:, ANGLE], ACT.Sin, scale=0.5).then_inc(s5_sin, 1)
            sc.activation(s5[:, SIN], s5[:, ANGLE], ACT.Sin).then_inc(s5_sin, 1)
            copied(sc, 0)
            for k, name in enumerate(("c_2", "c_ctx_2")):
                sc.activation(silu_c[:, :, k], vec[:, VEC[name]:VEC[name] + DT], ACT.Silu).then_inc(silu_ready, 1)
            for m in range(UT):
                t = T0["u"] + m
                full(sc, t)
                out_of(t, sc.copy(u_st[:, m], acc[t % BANKS][:].rearrange("p (j s) -> p s j", s=STEP)))
            for m in range(4):
                t = T0["q"] + m
                full(sc, t)
                out_of(t, sc.copy(qT[:, m, :], acc[t % BANKS][:]))
            sc.wait_ge(s5_bbar, 2)
            for m in range(8):
                t = T0["kernel"] + m
                full(sc, t)
                out_of(t, sc.copy(kern[0:GROUP, 4 * m:4 * (m + 1)].rearrange("p g n -> p (g n)"), acc[t % BANKS][0:GROUP, :]))
            for m in range(6):
                t = T0["kv"] + m
                full(sc, t)
                out_of(t, sc.copy(kvT[:, m, :], acc[t % BANKS][:]))
            t = T0["gates"]
            full(sc, t)
            out_of(t, sc.activation(gsig.rearrange("p t n -> p (t n)"), acc[t % BANKS][:, 0:TT * 3 * HEADS], ACT.Sigmoid))
            for m in range(4):
                t = T0["state"] + m
                full(sc, t)
                out_of(t, sc.copy(e1[:, 8 * m:8 * (m + 1)].rearrange("p g j -> p (g j)"), acc[t % BANKS][:]))
            free(sc, mod_out, 2)
            for k in range(2):
                free(sc, mod_stored[k], 16)

            def modulation(g):
                with sc.Fori(0, 4) as i:
                    for k in range(2):
                        n = 8 * g + k
                        sc.wait_ge(mod_full, 2 * i + n + 1)
                        sc.wait_ge(mod_stored[k], 16 * i + 64 * g + 16)
                        sc.copy(mod_rows[:, k], mod_banks[k][0:2, 0:2 * P]).then_inc(mod_out, 1)
                        sc.wait_ge(mod_out, 2 * i + n + 3)
                        sc.dma_start(mod_scr[:, ds(i * (4 * P) + n * (2 * P), 2 * P)], mod_rows[:, k]).then_inc(mod_stored[k], 16)

            modulation(0)
            for kind in range(2):
                sc.wait_ge(hid_full, kind + 1)
                sc.activation(hid[:, kind, 0:KVG * NCMP], banks[(6, 4)[kind]][:, 0:KVG * NCMP], ACT.Gelu_apprx_tanh)\
                  .then_inc(hid_ready, 1)
            for m in range(2):
                t = T0["v_tok"] + m
                full(sc, t)
                out_of(t, sc.copy(v_tok[:, m].rearrange("p b n -> p (b n)"), acc[t % BANKS][:]))
            modulation(1)
            for m in range(4):
                copied(sc, T0["q"] + m)
            for m in range(2, 6):
                copied(sc, T0["kv"] + m)

            def qk_root(m):
                t = T0["qk_norm"] + m
                full(sc, t)
                if m >= 2:
                    sc.wait_ge(qk_rstd, m - 1)
                step(sc.activation(root[:, m % 2, :], acc[t % BANKS][:], ACT.Ln, bias=eps[:]))
                sc.activation(root[:, m % 2, :], root[:, m % 2, :], ACT.Exp, scale=-0.5).then_inc(qk_sq, 1)

            sc.wait_ge(sq_used, DT)
            for m in range(6):
                src = qT[:, m, :] if m < 4 else kvT[:, 2 * (m - 3), :]
                if m >= 2:
                    full(sc, T0["qk_norm"] + m - 2)
                sc.activation(sq[:, m % 2, :], src, ACT.Square).then_inc(sq_ready, 1)
                if m >= 1:
                    qk_root(m - 1)
            qk_root(5)
            n = KVG * NCMP
            sc.wait_ge(kc_full, 1)
            sc.activation(knorm[:, 0:n], stat[:, 64:64 + n], ACT.Square).then_inc(kc_sq, 1)
            sc.wait_ge(vc_full, 1)
            sc.copy(vc[0:NCMP].rearrange("p g n -> p (g n)"), banks[6][0:NCMP, 0:P]).then_inc(vc_ready, 1)
            sc.wait_ge(kc_mean, 1)
            inverse_root(knorm[:, 0:n], stat[:, 128:128 + n]).then_inc(kc_sq, 1)
            modulation(2)
            sc.wait_ge(xprev_ready, 1)
            for m in range(4):
                t = T0["y"] + m
                full(sc, t)
                out_of(t, sc.copy(ych[:, 8 * m:8 * (m + 1)].rearrange("p g j -> p (g j)"), acc[t % BANKS][:]))
            QUERIES = HPG * TT
            with sc.Fori(0, KVG) as gi:
                def exps(n):
                    w = (n % TT + 1) * P
                    st = stats[:, n % 2]
                    sc.wait_ge(score_ready, gi * QUERIES + n + 1)
                    if n >= 2:
                        sc.wait_ge(pt_full, gi * QUERIES + n - 1)
                    sc.activation(cprob[:, n % 2, :], cscore[:, n % 2, :], ACT.Exp, bias=st[:, 3:4], accum_out=st[:, 6:7])
                    for m in range(2):
                        ins = sc.activation(prob[:, n % 2, m, 0:w], score[:, n % 2, m, 0:w], ACT.Exp,
                                            bias=st[:, 4 + m:5 + m], accum_out=st[:, 7 + m:8 + m])
                    ins.then_inc(prob_ready, 1)

                exps(0)
                for n in range(QUERIES):
                    w = (n % TT + 1) * P
                    if n + 1 < QUERIES:
                        exps(n + 1)
                    sc.wait_ge(pt_full, gi * QUERIES + n + 1)
                    if n >= 2:
                        sc.wait_ge(o_full, gi * QUERIES + n - 1)
                    sc.copy(cprobT[0:NCMP, n % 2, :], banks[3][0:NCMP, 0:P])
                    sc.copy(probT[:, n % 2, 1, 0:w], banks[6][:, 0:w]).then_inc(pt_out, 1)
                sc.wait_ge(o_full, gi * QUERIES + QUERIES)
            for k in range(2):
                sc.wait_ge(mod_stored[k], 16 + 16 * 12)
            for m in range(UT):
                sc.wait_ge(y_sum, m + 1)
                sc.activation(gelu_y[:, m, :].rearrange("p (j s) -> p s j", s=STEP), yT[:, m], ACT.Gelu_apprx_tanh)\
                  .then_inc(gelu_done, 1)
            sc.copy(mix_hi[:], hT[:]).then_inc(mix_hi_ready, 1)
            for c in range(4):
                t = T0["o_nsa"] + c
                full(sc, t)
                sc.copy(nsa_hi[:, c, :], acc[t % BANKS][:]).then_inc(nsa_hi_ready, 1)
            sc.wait_ge(gelu_done, UT)
            for m in range(UT):
                t = T0["glu"] + m
                full(sc, t)
                out_of(t, sc.activation(yT[:, m].rearrange("p s j -> p (s j)"), acc[t % BANKS][:], ACT.Sigmoid,
                                        bias=vcol("ssm_b_glu", m)))
            def high(n, q, more=0, slots=0, free=False):
                sc.wait_ge(loaded[n % SLOTS], 32 * (n // SLOTS + 1) + 32 * slots)
                if not free:
                    sc.wait_ge(split_used, q + more)
                sc.copy(w_hi[:, n % SLOTS, :], ring[:, n % SLOTS, :]).then_inc(hi_ready, 1)

            n = C0["merge"]
            high(n, 0, free=True)
            for m in range(UT):
                sc.wait_ge(yssm_ready, m + 1)
                sc.copy(ssm_hi[:, m, :], y_ssm[:, m, :]).then_inc(mix_hi_ready, 1)
            with sc.Fori(0, DT) as i:
                for m in range(2):
                    high(n + 1 + m, 1 + m, 2 * i, i)
                    t = T0["merge"] + 2 * m
                    full(sc, t, 4 * i)
                    sc.wait_ge(merged_ready, i + 1)
                    out_of(t, sc.activation(sig[:, m, :], acc[t % BANKS][:], ACT.Sigmoid))
            sc.wait_ge(merged_ready, DT + 1)
            for c in range(DT):
                sc.copy(merged_hi[:, c, :], merged[:, c, :]).then_inc(merged_hi_ready, 1)
            for k in range(1, 4):
                high(C0["out1"] + k, SPLIT0["out1"] + k)
            high(C0["up1_0"], SPLIT0["up1_0"])
            sc.wait_ge(x1_ready, 1)
            squares(xT, T, DT)
            sc.wait_ge(sq_used, 2 * DT)
            inverse_root(rstd[:], stat[:]).then_inc(rstd_ready, 1)
            for c in range(DT):
                sc.wait_ge(h_new_ready, c + 1)
                sc.copy(hT_hi[:, c, :], h_new[:, c, :]).then_inc(h_hi_ready, 1)
            high(C0["up1_0"] + 1, SPLIT0["up1_0"] + 1, free=True)
            for h in range(2):
                n, q, t = C0[f"up1_{h}"], SPLIT0[f"up1_{h}"], T0[f"up1_{h}"]
                with sc.Fori(0, 4) as i:
                    for k in range(4):
                        full(sc, t + k, 4 * i)
                        sc.wait_ge(act_ready, 4 * i + FT // 2 * h + k + 1)
                        out_of(t + k, sc.activation(relu[:, k % 2, :], acc[(t + k) % BANKS][:], ACT.Relu))
                        copied(sc, t + k, i)
                        sc.activation(act_hi[:, ds(4 * i + k, 1), :], relu[:, k % 2, :].unsqueeze(1), ACT.Square)\
                          .then_inc(act_hi_ready, 1)
                        if k % 2:
                            high(n + 2 + k // 2, q + 2 + k // 2, 2 * i, i, free=True)
                n, q = C0[f"down1_{h}"], SPLIT0[f"down1_{h}"]
                if h == 0:
                    with sc.Fori(0, 2) as i:
                        for k in range(2, 6):
                            high(n + k, q + k, 4 * i, 2 * i)
                else:
                    for k in range(2, 8):
                        high(n + k, q + k)
            sc.wait_ge(lb_logit, 1)
            sc.activation(lb[:, 0], lb[:, 2], ACT.Sigmoid, scale=-1.0).then_inc(lb_sig, 1)
            sc.activation(lb[:, 1], lb[:, 2], ACT.Sigmoid).then_inc(lb_sig, 1)
            for c in range(4):
                t = T0["ctx"] + c
                full(sc, t)
                out_of(t, sc.copy(xcT[:, 2 * c:2 * c + 2].rearrange("p k n -> p (k n)"), acc[t % BANKS][:]))
            for c in range(4):
                copied(sc, T0["ctx"] + c)
            squares(xcT, C, 2 * DT)
            sc.wait_ge(sq_used, 3 * DT)
            inverse_root(root[:, 0, 0:C], stat[:, 0:C]).then_inc(rstd_ready, 1)
            sc.wait_ge(x1_ready, 2)
            squares(xT, T, 3 * DT)
            sc.wait_ge(sq_used, 4 * DT)
            inverse_root(rstd[:], stat[:]).then_inc(rstd_ready, 1)

            def shifted(dst, shift, col, scaled):
                for c in range(DT):
                    sc.wait_ge(h_scaled, scaled + c + 1)
                    sc.activation(dst[:, c, :], dst[:, c, :], ACT.Identity, bias=mod[:, shift * DT + c, col:col + 1])\
                      .then_inc(h_ready, 1)

            sc.wait_ge(mod_ready, 1)
            shifted(hcT, 0, 1, 0)
            shifted(hT, 0, 0, DT)
            for m in range(2):
                t, n = T0["gate_rows"] + m, (T, C)[m]
                full(sc, t)
                g16 = sq[0:4 * MH].rearrange("p a n -> p (a n)")[:, C * (1 - m):C * (1 - m) + n]
                out_of(t, sc.activation(g16, acc[t % BANKS][0:4 * MH, 0:n], ACT.Identity, bias=mgate_b[:]))
            for m in range(2):
                copied(sc, T0["gate_rows"] + m)
            free(sc, g16_ready)
            sc.wait_ge(neg_ready, 1)
            step(sc.activation(row_b[0:MH], row_b[0:MH], ACT.Exp))
            sc.activation(row_b[0:MH], row_b[0:MH], ACT.Ln, bias=1.0).then_inc(ln_ready, 1)
            for m in range(2):
                for b in range(ST):
                    t = T0["v2"] + ST * m + b
                    full(sc, t)
                    if m == 0:
                        out_of(t, sc.copy(hg_v[:, b, :], acc[t % BANKS][:]))
                    else:
                        out_of(t, sc.copy(ml_v[:, b, :, 0:P], acc[t % BANKS][:].rearrange("p (h n) -> p h n", n=P)))
            t, n = T0["gate_cols"], 2 * ST * MH
            full(sc, t)
            sc.copy(gcol.rearrange("p d b h -> p (d b h)"), acc[t % BANKS][:, 0:n]).then_inc(cols_ready, 1)
            out_of(t, sc.activation(floor.rearrange("p d b h -> p (d b h)"), acc[t % BANKS][:, n:n + 2 * TT * MH],
                                    ACT.Exp, scale=-1.0))
            sc.wait_ge(max_out, 32)
            copied(sc, t)
            free(sc, z_ready)
            free(sc, sums_kept)
            with sc.Fori(0, MH) as i:
                t = T0["hg_in"]

                def bank(k):
                    return acc[(t + k) % BANKS][:]

                full(sc, t, 4 * i)
                out_of(t, sc.activation(hg_q[:, ds(i, 1), :], bank(0).unsqueeze(1), ACT.Silu))
                for d in range(2):
                    full(sc, t + 1 + d, 4 * i)
                    sc.activation(logf[:, d, CT:, 1:], bank(1 + d).rearrange("p (b n) -> p b n", n=P), ACT.Sigmoid)
                    out_of(t + 1 + d, sc.activation(hg_k[:, ds(i, 1), d, C:], bank(1 + d).unsqueeze(1), ACT.Sigmoid,
                                                    scale=-1.0))
                sc.wait_ge(z_ctx, 2 * i + 2)
                z = banks[5][:].rearrange("p (d n) -> p d n", d=2)
                for d in range(2):
                    sc.activation(logf[:, d, 0:CT, 1:], z[:, d].rearrange("p (b n) -> p b n", n=P), ACT.Sigmoid)
                for d in range(2):
                    ins = sc.activation(hg_k[:, ds(i, 1), d, 0:C], z[:, d].unsqueeze(1), ACT.Sigmoid, scale=-1.0)
                ins.then_inc(z_ready, 1)
                full(sc, t + 3, 4 * i)
                out_of(t + 3, sc.activation(hg_g[:, ds(i, 1), :], bank(3).unsqueeze(1), ACT.Silu))
                for d in range(2):
                    sc.wait_ge(f_ready, 2 * i + d + 1)
                    sc.activation(logf[:, d, :, 1:], logf[:, d, :, 1:], ACT.Ln).then_inc(logf_ready, 1)
                sc.wait_ge(sums_ready, i + 1)
                sc.copy(sums[:, ds(i, 1), :], sums1.unsqueeze(1)).then_inc(sums_kept, 1)
            sc.wait_ge(sums_kept, MH + 1)
            with sc.Fori(0, MH) as i:
                t = T0["hg"]

                def upto(d, b, inclusive, n=1, by=1):
                    return sums_v[:, ds(i, 1), d, b:b + (n - 1) * by + 1:by, inclusive:inclusive + P]\
                        .rearrange("p o a n -> p (o a) n")

                def total(d, b):
                    return sums_v[:, ds(i, 1), d, b, P:P + 1].rearrange("p o n -> p (o n)")

                def over(k):
                    return sums[:, ds(i, 1), k:k + 1].rearrange("p o n -> p (o n)")

                def decay(dst, x, bias=None, sign=1):
                    dst = dst.rearrange("p (a n) -> p a n", n=P) if len(dst.shape) == 2 else dst
                    if bias is None:
                        return sc.activation(dst, x, ACT.Exp, scale=float(sign))
                    return sc.activation(dst, x, ACT.Exp, scale=float(sign), bias=bias)

                def exps(u):
                    k_, q_ = ek[:, u % 2, :], eq[:, u % 2, :]
                    ks, qs = ([x[:, s * P:(s + 1) * P] for s in range(TT)] for x in (k_, q_))
                    if u < DIAG:
                        sc.wait_ge(diff_ready, DIAG * i + u + 1)
                        sc.activation(k_, k_, ACT.Exp)
                        sc.activation(q_, q_, ACT.Exp).then_inc(exp_ready, 1)
                        return
                    full(sc, unit_tiles(u - 2)[-1], 16 * i)
                    if u == PAIRS:
                        for s in (0, 2):
                            decay(ks[s], upto(0, CT + s, 1), total(0, CT + s), -1)
                            decay(qs[s], upto(1, CT + s, 0), total(1, CT + s), -1)
                        odd = [x.rearrange("p (a t n) -> p a t n", t=2, n=P)[:, :, 1] for x in (k_, q_)]
                        decay(odd[0], upto(1, CT + 1, 0, 2, 2))
                        ins = decay(odd[1], upto(0, CT + 1, 1, 2, 2))
                    elif u == HALVES:
                        decay(ks[0], upto(0, CT, 1), over(PRE_F + 1), -1)
                        decay(ks[1], upto(0, CT + 1, 1), total(0, CT + 1), -1)
                        decay(ks[2], upto(1, CT + 2, 0))
                        decay(ks[3], upto(1, CT + 3, 0), total(1, CT + 2))
                        decay(qs[0], upto(1, CT, 0), over(PRE_B + 1), -1)
                        decay(qs[1], upto(1, CT + 1, 0), total(1, CT + 1), -1)
                        decay(qs[2], upto(0, CT + 2, 1))
                        ins = decay(qs[3], upto(0, CT + 3, 1), total(0, CT + 2))
                    else:
                        decay(ks[0], upto(0, 0, 1), over(CTX_F + 1), -1)
                        decay(ks[1], upto(0, 1, 1), total(0, 1), -1)
                        decay(ks[2], upto(1, 0, 0))
                        decay(ks[3], upto(1, 1, 0), total(1, 0))
                        for s in range(TT):
                            decay(qs[s], upto(0, CT + s, 1), over(PRE_F + s - 1) if s else None)
                            ins = decay(eq_b[:, s * P:(s + 1) * P], upto(1, CT + s, 0), over(SUF_B + s), -1)
                    ins.then_inc(exp_ready, 1)

                exps(0)
                exps(1)
                for u in range(2, DIAG):
                    exps(u)
                    for m in range(3):
                        if ML_AFTER[m] == u - 1:
                            b = ml_tile(m)
                            full(sc, b, 16 * i)
                            dst = (ml_q[:, ds(i, 1), :], ml_k[:, ds(i, 1), C:], ml_k[:, ds(i, 1), 0:C])[m]
                            out_of(b, sc.copy(dst, acc[b % BANKS][:, 0:(T, T, C)[m]].unsqueeze(1)))
                exps(PAIRS)
                exps(HALVES)

                def weights(b, dst):
                    full(sc, b, 16 * i)
                    out_of(b, sc.copy(dst.rearrange("p s n -> p (s n)") if len(dst.shape) == 3 else dst, acc[b % BANKS][:]))

                weights(unit_tiles(PAIRS)[0], a_pair)
                exps(CONTEXT)
                for k in range(2):
                    weights(unit_tiles(HALVES)[k], a_half[:, 2 * k:2 * k + 2])
                for k in range(2):
                    weights(unit_tiles(CONTEXT)[k], a_ctx[:, k])
                step.enter(i, TT + 1)
                sc.wait_ge(hg_o, i + 1)
                for b in range(TT):
                    last = step.mark(sc.activation(squared[:, b, :], banks[4][:, b * P:(b + 1) * P], ACT.Square,
                                                   accum_out=stat2[:, 0, b:b + 1]))
                step.wait(last)
                step(sc.activation(stat2[:, 1, 0:TT], stat2[:, 0, 0:TT], ACT.Ln, scale=1.0 / P, bias=eps[:]))
                sc.activation(stat2[:, 2, 0:TT], stat2[:, 1, 0:TT], ACT.Exp, scale=-0.5).then_inc(hg_rstd, 1)
                step.leave(MH)
            sc.wait_ge(qk_conv, 3 * MH)
            for x in (qc, kc2):
                sc.activation(x, x, ACT.Silu).then_inc(qk_ready, 1)
            with sc.Fori(0, MH) as i:
                t = T0["ml"]
                for n in range(2 * ST):
                    s, d = divmod(n, 2)
                    sc.wait_ge(gap_ready, 2 * ST * i + 2 * ST + n + 1)
                    w = targets(weight, d, s)
                    sc.activation(w, w, ACT.Exp, scale=-1.0).then_inc(w_ready, 1)
                step.enter(i, TT + 1)
                for b in range(TT):
                    sc.wait_ge(ml_h, TT * i + b + 1)
                    last = step.mark(sc.activation(squared[:, b, :], h_tok[:, b, :], ACT.Square,
                                                   accum_out=stat2[:, 0, TT + b:TT + b + 1]))
                step.wait(last)
                step(sc.activation(stat2[:, 1, TT:], stat2[:, 0, TT:], ACT.Ln, scale=1.0 / P, bias=eps[:]))
                sc.activation(stat2[:, 2, TT:], stat2[:, 1, TT:], ACT.Exp, scale=-0.5).then_inc(ml_rstd, 1)
                full(sc, t + 6, 8 * i)
                copied(sc, t - 1, 2 * i)
                out_of(t + 6, sc.activation(o_sig, acc[(t + 6) % BANKS][:], ACT.Sigmoid))
                step.leave(MH)
            full(sc, T0["out2"])
            high(C0["up2_0"], SPLITS1, free=True)
            sc.wait_ge(x1_ready, 3)
            squares(xT, T, 4 * DT)
            sc.wait_ge(sq_used, 5 * DT)
            inverse_root(rstd[:], stat[:]).then_inc(rstd_ready, 1)
            high(C0["up2_0"] + 1, SPLITS1 + 1, free=True)
            for c in range(DT):
                sc.wait_ge(h_scaled, 2 * DT + c + 1)
                step(sc.activation(h_new[:, c, :], h_new[:, c, :], ACT.Identity, bias=mod[:, 3 * DT + c, 0:1]))
                sc.copy(hT_hi[:, c, :], h_new[:, c, :]).then_inc(h_hi_ready, 1)
            for h, width2 in enumerate(F2_HALF):
                n, q, t = C0[f"up2_{h}"], SPLIT0[f"up2_{h}"], T0[f"up2_{h}"]
                done = h * F2_HALF[0]

                def copies(i, j, later):
                    for k in (2 * j, 2 * j + 1):
                        b = t + k
                        full(sc, b, 4 * i)
                        sc.wait_ge(conv_ready, 2 * done + 4 * i + k + 1)
                        sc.copy(raw[:, k], acc[b % BANKS][:])
                        if later:
                            sc.wait_ge(gated_ready, done + 2 * i + j - 1)
                        centre = TAPS // 2 * 2 * F2T + k % 2 * F2T + j + done
                        out_of(b, sc.mul(conv[:, k], acc[b % BANKS][:], ffn_taps[:, ds(i * 2 + centre, 1)]))

                def silu(i, j):
                    sc.wait_ge(conv_ready, 4 + 2 * done + 4 * i + 2 * j + 2)
                    sc.activation(conv[:, 2 * j], conv[:, 2 * j], ACT.Silu).then_inc(silu2_ready, 1)

                def gated_high(i, j):
                    sc.wait_ge(gated_ready, done + 2 * i + j + 1)
                    sc.copy(act_hi[:, ds(2 * i + j, 1), :], gated[:, j].unsqueeze(1)).then_inc(gated_hi_ready, 1)

                def round_(i, first):
                    copies(i, 0, h or not first)
                    high(n + 2, q + 2, 2 * i, i, free=True)
                    if not first:
                        gated_high(i - 1, 0)
                        silu(i - 1, 1)
                    copies(i, 1, h or not first)
                    high(n + 3, q + 3, 2 * i, i, free=True)
                    if not first:
                        gated_high(i - 1, 1)
                    silu(i, 0)

                last = width2 // 2 - 1
                with sc.Fori(0, 1) as i:
                    round_(i, True)
                with sc.Fori(1, last + 1) as i:
                    round_(i, False)
                with sc.Fori(last, last + 1) as i:
                    gated_high(i, 0)
                    silu(i, 1)
                    gated_high(i, 1)
                n, q = C0[f"down2_{h}"], SPLIT0[f"down2_{h}"]
                if h == 0:
                    with sc.Fori(0, 2) as i:
                        for k in range(2, 6):
                            high(n + k, q + k, 4 * i, 2 * i)
                else:
                    for k in range(2, 8):
                        high(n + k, q + k)
            sc.wait_ge(x1_ready, 4)
            squares(xT, T, 5 * DT)
            sc.wait_ge(sq_used, 6 * DT)
            inverse_root(rstd[:], stat[:]).then_inc(rstd_ready, 1)
            for t in range(TT):
                for k in range(2):
                    b = T0["final"] + 2 * t + k
                    full(sc, b)
                    out_of(b, sc.copy(out_tok[:, t, k * 4 * P:(k + 1) * 4 * P], acc[b % BANKS][:]))

        @block.vector
        def _(ve):
            step = Steps(ve, dve_step)

            def product(out, x, y):
                return ve.tensor_tensor(out, x, y, ALU.mult)

            def complex_product(oc, os, xc, xs, yc, ys, n):
                t = [ptmp[:, k // 2, k % 2 * 256:k % 2 * 256 + n * GROUPS].rearrange("p (k g) -> p k g", g=GROUPS)
                     for k in range(4)]
                for o, x, y in zip(t, (xc, xs, xc, xs), (yc, ys, ys, yc)):
                    last = step.mark(product(o, x, y))
                step.wait(last)
                step.mark(ve.tensor_tensor(oc, t[0], t[1], ALU.subtract))
                step(ve.tensor_tensor(os, t[2], t[3], ALU.add))

            def newton(y, mean, t):
                step(product(t, y, y))
                last = ve.scalar_tensor_tensor(t, mean, EPS, t, ALU.add, ALU.mult)
                step(last)
                step(ve.tensor_scalar(t, t, -0.5, 1.5, ALU.mult, ALU.add))
                step(product(y, y, t))

            step.mark(ve.memset(sign[:], 1.0))
            step.mark(ve.memset(nsign[:], -1.0))
            step(ve.memset(mean_hd[:], 0.0))
            ve.memset(sign[HD:P], -1.0).then_inc(consts, 1)
            ve.memset(nsign[HD:P], 1.0).then_inc(consts, 1)
            for h in range(2):
                ve.memset(mean_hd[h * HD:(h + 1) * HD, h * HD:(h + 1) * HD], 1.0 / HD).then_inc(consts, 1)
            ve.memset(zero[:], 0.0).then_inc(consts, 1)
            ve.wait_ge(consts, CONSTS)
            step.mark(ve.tensor_scalar(cmask[:], cdist[:], FAR / 2, None, ALU.is_lt))
            copied(ve, 0)
            ar, ai = (vec[:, VEC[n]:VEC[n] + GROUPS] for n in ("a_re", "a_im"))
            ve.wait_ge(s5_exp, 1)
            product(s5[:, AR_DT], ar, s5[:, DT_]).then_inc(s5_small, 1)
            step.mark(ve.tensor_scalar(g_q[:], vcol("q_norm_g"), HD ** -0.5, None, ALU.mult))
            step(product(s5[:, ANGLE], ai, s5[:, DT_]))
            step(ve.tensor_scalar(s5[:, TURNS], s5[:, ANGLE], 1.0 / TWO_PI, ROUND, ALU.mult, ALU.add))
            step(ve.tensor_scalar(s5[:, TURNS], s5[:, TURNS], -ROUND, None, ALU.add))
            for part in (TURN_A, TURN_B, TURN_C):
                step(ve.scalar_tensor_tensor(s5[:, ANGLE], s5[:, TURNS], -part, s5[:, ANGLE], ALU.mult, ALU.add))
            ve.tensor_scalar(s5[:, ANGLE], s5[:, ANGLE], -3.1415925, 3.1415925, ALU.max, ALU.min).then_inc(s5_angle, 1)
            def norm(gain, start):
                ve.wait_ge(rstd_ready, start + 1)
                for c in range(DT):
                    ve.scalar_tensor_tensor(hT[:, c, :], xT[:, c, :], vcol(gain, c), rstd[:], ALU.mult, ALU.mult)\
                      .then_inc(h_ready, 1)

            norm("norm1_g", 0)
            ve.wait_ge(s5_sin, 2)
            ve.wait_ge(s5_exp, 3)
            step(product(s5[:, COS], s5[:, SIN_H], s5[:, SIN_H]))
            step(ve.tensor_scalar(s5[:, COS], s5[:, COS], -2.0, 1.0, ALU.mult, ALU.add))
            re, im = s5[:, PR:PR + STEP + 1], s5[:, PI:PI + STEP + 1]
            step.mark(ve.memset(re[:, 0], 1.0))
            step.mark(ve.memset(im[:, 0], 0.0))
            step.mark(product(re[:, 1], s5[:, MAG], s5[:, COS]))
            step(product(im[:, 1], s5[:, MAG], s5[:, SIN]))
            m = 1
            while m < STEP:
                shape = [P, m, GROUPS]
                complex_product(re[:, m + 1:2 * m + 1], im[:, m + 1:2 * m + 1], re[:, 1:m + 1], im[:, 1:m + 1],
                                re[:, m:m + 1].to_broadcast(shape), im[:, m:m + 1].to_broadcast(shape), m)
                m *= 2
            xc, xs = s5[:, COS:COS + 1], s5[:, SIN:SIN + 1]
            for n in range(3):
                oc, os = ((s5[:, E1C:E1C + 1], s5[:, E1S:E1S + 1]), (s5[:, COS:COS + 1], s5[:, SIN:SIN + 1]),
                          (s5[:, E8C:E8C + 1], s5[:, E8S:E8S + 1]))[n]
                complex_product(oc, os, xc, xs, xc, xs, 1)
                xc, xs = oc, os
            step.mark(product(s5[:, DEN], ar, ar))
            step(product(s5[:, TMP], ai, ai))
            step(ve.tensor_tensor(s5[:, DEN], s5[:, DEN], s5[:, TMP], ALU.add))
            step.mark(ve.reciprocal(s5[:, DEN], s5[:, DEN]))
            step(ve.tensor_scalar(s5[:, NR], re[:, 1], -1.0, None, ALU.add))
            step.mark(product(s5[:, _1], s5[:, NR], ar))
            step.mark(product(s5[:, _2], im[:, 1], ai))
            step.mark(product(s5[:, _3], im[:, 1], ar))
            step(product(s5[:, _4], s5[:, NR], ai))
            step.mark(ve.tensor_tensor(s5[:, FR], s5[:, _1], s5[:, _2], ALU.add))
            step(ve.tensor_tensor(s5[:, FI], s5[:, _3], s5[:, _4], ALU.subtract))
            step.mark(product(s5[:, FR], s5[:, FR], s5[:, DEN]))
            step(product(s5[:, FI], s5[:, FI], s5[:, DEN]))
            bu_, bv_, ub, vb = (x.rearrange("p g c -> p (g c)") for x in (bu, bv, ubar, vbar))
            step(ve.tensor_scalar(bv_, bv_, nsign[:], None, ALU.mult))
            fr, fi = (s5[:, k].unsqueeze(2).to_broadcast([P, GROUPS, GROUP]) for k in (FR, FI))
            t0, t1 = (ptmp[:, k].rearrange("p (g c) -> p g c", c=GROUP) for k in range(2))
            step.mark(product(t0, bu, fr))
            step(product(t1, bv, fi))
            ve.tensor_tensor(ubar, t0, t1, ALU.add).then_inc(s5_bbar, 1)
            ve.wait_ge(s5_bbar, 1)
            step.mark(product(t0, bv, fr))
            step(product(t1, bu, fi))
            ve.tensor_tensor(vbar, t0, t1, ALU.subtract).then_inc(s5_bbar, 1)
            def flat(x):
                return x.rearrange("p g j -> p (g j)")

            def cols(k):
                return s5[:, k].unsqueeze(2).to_broadcast([P, GROUPS, GROUP])

            def twist(out, re, im, x, y):
                t0, t1 = (twist_tmp[:, k].rearrange("p (g c) -> p g c", c=GROUP) for k in range(2))
                step.mark(product(t0, cols(re), x))
                step(product(t1, cols(im), y))
                return ve.tensor_tensor(out, t0, t1, ALU.add)

            copied(ve, T0["params"] + 3)
            copied(ve, T0["params"] + 2)
            for k in range(STEP):
                step(twist(ca[:, :, k, :], PR + k, PI + k, cu, cv))
            twist(ca[:, :, STEP, :], PR + STEP, PI + STEP, cu, cv).then_inc(ca_ready, 1)
            ve.wait_ge(ca_ready, 1)
            step.mark(ve.memset(rot_c[:, :, 0:1], 1.0))
            step.mark(ve.memset(rot_s[:, :, 0:1], 0.0))
            step.mark(ve.tensor_copy(rot_c[:, :, 1:2], s5[:, E8C].unsqueeze(2)))
            step(ve.tensor_copy(rot_s[:, :, 1:2], s5[:, E8S].unsqueeze(2)))
            m = 2
            while m < CHUNKS:
                half_c, half_s = rot_c[:, :, m // 2:m // 2 + 1], rot_s[:, :, m // 2:m // 2 + 1]
                wc, ws, t0, t1 = (s5[:, TMP + k].unsqueeze(2) for k in range(4))
                step.mark(ve.tensor_tensor(t0, half_c, half_c, ALU.mult))
                step.mark(ve.tensor_tensor(t1, half_s, half_s, ALU.mult))
                step(ve.tensor_tensor(ws, half_c, half_s, ALU.mult))
                step.mark(ve.tensor_tensor(wc, t0, t1, ALU.subtract))
                step(ve.tensor_tensor(ws, ws, ws, ALU.add))
                t0, t1 = (twist_tmp[:, k, 0:GROUPS * min(m, 16)].rearrange("p (g j) -> p g j", g=GROUPS) for k in range(2))
                for b in range(0, m, 16):
                    w = min(16, m)
                    shape = [P, GROUPS, w]
                    oc, os, ic, is_ = rot_c[:, :, m + b:m + b + w], rot_s[:, :, m + b:m + b + w], rot_c[:, :, b:b + w], rot_s[:, :, b:b + w]
                    step.mark(ve.tensor_tensor(t0, ic, wc.to_broadcast(shape), ALU.mult))
                    step(ve.tensor_tensor(t1, is_, ws.to_broadcast(shape), ALU.mult))
                    step(ve.tensor_tensor(oc, t0, t1, ALU.subtract))
                    step.mark(ve.tensor_tensor(t0, ic, ws.to_broadcast(shape), ALU.mult))
                    step(ve.tensor_tensor(t1, is_, wc.to_broadcast(shape), ALU.mult))
                    step(ve.tensor_tensor(os, t0, t1, ALU.add))
                m *= 2
            ve.tensor_scalar(flat(rot_s), flat(rot_s), sign[:], None, ALU.mult).then_inc(rot_ready, 1)

            for m in range(8):
                t = T0["bt"] + m
                full(ve, t)
                out_of(t, ve.tensor_copy(bt[:, 4 * m:4 * (m + 1)].rearrange("p g n -> p (g n)"), acc[t % BANKS][:]))
            for kind in range(2):
                ve.wait_ge(kv_in, 64)
                copied(ve, T0["kv"] + kind)
                for h in range(2):
                    half = slice(h * HD, (h + 1) * HD)
                    for g in range(KVG):
                        src = (kvT[:, kind] if g == h else kv_swapped[:, kind]).rearrange("p (j r) -> p j r", r=CMP_STRIDE)
                        for c in range(2):
                            at = VEC["pe"] + CMP_STRIDE * kind + 8 * c
                            ve.tensor_tensor(block_cols(kind)[half, 8 * c:8 * c + 8, g],
                                             src[half, c:c + NCMP, h::2].rearrange("p j k -> p k j"),
                                             vec[half, at:at + 8].unsqueeze(2).to_broadcast([HD, 8, NCMP]), ALU.add)\
                              .then_inc(blocks_ready, 1)
            for t in range(4):
                copied(ve, T0["state"] + t)
            ve.wait_ge(rot_ready, 1)
            step.mark(product(flat(z1), flat(e1), flat(rot_c)))
            ve.wait_ge(e_swapped, 32)
            step(product(flat(zs), flat(e2), flat(rot_s)))
            step(ve.tensor_tensor(flat(z1), flat(z1), flat(zs), ALU.add))
            for g in range(GROUPS):
                ins = ve.tensor_tensor_scan(zs[:, g, :], s5[:, MAG_STEP, g:g + 1].to_broadcast([P, CHUNKS]), z1[:, g, :],
                                            0.0, ALU.mult, ALU.add)
                if g < GROUPS - 1:
                    step.mark(ins)
            ins.then_inc(z_scanned, 1)
            ve.wait_ge(z_scanned, 1)
            n = CHUNKS - 1
            step.mark(ve.memset(xprev[:, :, 0:1], 0.0))
            step(product(xprev[:, :, 1:], zs[:, :, 0:n], rot_c[:, :, 0:n]))
            ve.wait_ge(z_swapped, 32)
            step(product(z1[:, :, 0:n], z2[:, :, 0:n], rot_s[:, :, 0:n]))
            ve.tensor_tensor(xprev[:, :, 1:], xprev[:, :, 1:], z1[:, :, 0:n], ALU.subtract).then_inc(xprev_ready, 1)
            for m in range(6):
                t = T0["qk_norm"] + m
                ve.wait_ge(qk_sq, m + 1)
                y, tmp = root[:, m % 2, :], rstd[:]
                step(product(tmp, y, y))
                step.mark(ve.scalar_tensor_tensor(tmp, acc[t % BANKS][:], EPS, tmp, ALU.add, ALU.mult))
                step.wait(step.base + step.n)
                out_of(t, ve.tensor_scalar(tmp, tmp, -0.5, 1.5, ALU.mult, ALU.add))
                copied(ve, t)
                step(product(y, y, tmp))
                if m < 4:
                    ve.scalar_tensor_tensor(qT[:, m, :], qT[:, m, :], g_q[:], y, ALU.mult, ALU.mult).then_inc(qk_rstd, 1)
                else:
                    for h in range(KVG):
                        half = slice(h * HD, (h + 1) * HD)
                        ins = ve.scalar_tensor_tensor(kk[half, m - 4, h, :], kvT[half, 2 * (m - 3), :],
                                                      vcol("k_norm_g", m - 3)[half], y[half], ALU.mult, ALU.mult)
                        ins.then_inc(k_normed, 1)
            n = KVG * NCMP
            ve.wait_ge(kc_sq, 2)
            newton(knorm[:, 0:n], stat[:, 128:128 + n], rstd[:, 0:n])
            ve.scalar_tensor_tensor(kc, stat[:, 64:64 + n], vcol("k_norm_g", 0), knorm[:, 0:n], ALU.mult, ALU.mult)\
              .then_inc(kc_ready, 1)
            QUERIES = HPG * TT
            ve.wait_ge(qk_rstd, 4)
            ve.wait_ge(kc_ready, 1)
            ve.wait_ge(k_normed, 4)
            ve.wait_ge(k_dup, 64)
            full(ve, T0["y"] + 3)
            with ve.Fori(0, KVG) as gi:
                step.enter(gi, ATT_STEPS)
                ve.tensor_copy(kcg, kc[:, ds(gi * NCMP, NCMP)]).then_inc(qn_ready, 1)
                for k in range(2):
                    ve.tensor_copy(kkg[:, k, :], kk[:, k, ds(gi, 1), :].rearrange("p a n -> p (a n)")).then_inc(qn_ready, 1)
                for k in range(2):
                    ve.tensor_copy(qn[:, k, :], qT[:, ds(2 * gi + k, 1), :].rearrange("p a n -> p (a n)")).then_inc(qn_ready, 1)

                def maxima(n):
                    hg, tt = divmod(n, TT)
                    w, st = (tt + 1) * P, stats[:, n % 2]
                    if tt == 0:
                        slope = negslope[:, ds(HPG * gi + hg, 1)]
                        step.mark(ve.tensor_scalar(bias[:, hg % 2, :], dist[:], slope, None, ALU.mult))
                        step(ve.tensor_scalar(cbias[:, hg % 2].rearrange("p t n -> p (t n)"),
                                              cdist[:].rearrange("p t n -> p (t n)"), slope, None, ALU.mult))
                    ve.wait_ge(score_full, gi * QUERIES + n + 1)
                    if n >= 2:
                        ve.wait_ge(prob_ready, gi * QUERIES + n - 1)
                    step.mark(ve.memset(tick[:, 0:1], 0.0))
                    step.mark(ve.tensor_tensor_reduce(cscore[:, n % 2, :], stat[:, 0:NCMP],
                                                      cbias[:, hg % 2, tt, :], 1.0, -3e38, ALU.add, ALU.max, st[:, 0:1]))
                    for m in range(2):
                        last = step.mark(ve.tensor_tensor_reduce(
                            score[:, n % 2, m, 0:w], banks[m][:, 0:w], bias[:, hg % 2, T - w:T],
                            1.0, -3e38, ALU.add, ALU.max, st[:, 1 + m:2 + m]))
                    step.wait(last)
                    ve.tensor_scalar(st[:, 3:6], st[:, 0:3], -1.0, None, ALU.mult).then_inc(score_ready, 1)

                def weights(n):
                    hg, tt = divmod(n, TT)
                    st = stats[:, n % 2]
                    ve.wait_ge(prob_ready, gi * QUERIES + n + 1)
                    product(cprob[:, n % 2, :], cprob[:, n % 2, :], cmask[:, tt, :]).then_inc(cprob_ready, 1)
                    step(ve.reciprocal(st[:, 9:12], st[:, 6:9]))
                    return step.mark(product(st[:, 12:15], st[:, 9:12], gsig[:, tt, ds(HPG * gi + hg, 3, HEADS)]))

                def combine(n, weighed):
                    hg, tt = divmod(n, TT)
                    st = stats[:, n % 2]
                    o = o_tok[:, tt, ds(gi * HPG * HD + hg * HD, HD)]
                    p = banks[(2, 7)[n % 2]]
                    ve.wait_ge(o_full, gi * QUERIES + n + 1)
                    step.wait(weighed)
                    step(ve.tensor_scalar(o, p[:, 0:HD], st[:, 12:13], None, ALU.mult))
                    step(ve.scalar_tensor_tensor(o, p[:, HD:2 * HD], st[:, 13:14], o, ALU.mult, ALU.add))
                    ve.scalar_tensor_tensor(o, p[:, 2 * HD:3 * HD], st[:, 14:15], o, ALU.mult, ALU.add).then_inc(o_ready, 1)

                maxima(0)
                weighed = None
                for n in range(QUERIES):
                    if n >= 1:
                        before = weighed
                    weighed = weights(n)
                    if n >= 1:
                        combine(n - 1, before)
                    if n + 1 < QUERIES:
                        maxima(n + 1)
                    w = (n % TT + 1) * P
                    ve.wait_ge(pt_full, gi * QUERIES + n + 1)
                    ve.tensor_copy(probT[:, n % 2, 0, 0:w], banks[5][:, 0:w]).then_inc(cpt_out, 1)
                combine(QUERIES - 1, weighed)
                step.leave(KVG)
            ve.wait_ge(y_in, 32)
            for m in range(UT):
                y = yT[:, m].rearrange("p s j -> p (s j)")
                ve.scalar_tensor_tensor(y, y_us[:, m].rearrange("p s j -> p (s j)"), vcol("ssm_d", m), y, ALU.mult, ALU.add)\
                  .then_inc(y_sum, 1)
            ve.wait_ge(mix_hi_ready, 1)
            ve.tensor_tensor(mix_lo[:], hT[:], value(mix_hi[:]), ALU.subtract).then_inc(mix_ready, 1)
            for c in range(4):
                t = T0["o_nsa"] + c
                ve.wait_ge(nsa_hi_ready, c + 1)
                out_of(t, ve.tensor_tensor(nsa_lo[:, c, :], acc[t % BANKS][:], value(nsa_hi[:, c, :]), ALU.subtract))
            for m in range(UT):
                copied(ve, T0["glu"] + m)
                product(y_ssm[:, m, :], gelu_y[:, m, :], yT[:, m].rearrange("p s j -> p (s j)")).then_inc(yssm_ready, 1)
            def low(n, q, more=0):
                ve.wait_ge(hi_ready, q + 1 + more)
                ve.tensor_tensor(w_lo[:, n % SLOTS, :], ring[:, n % SLOTS, :], value(w_hi[:, n % SLOTS, :]), ALU.subtract)\
                  .then_inc(split_ready, 1)

            free(ve, chunk_used)
            low(C0["merge"], 0)
            for m in range(UT):
                ve.wait_ge(mix_hi_ready, m + 2)
                ve.tensor_tensor(ssm_lo[:, m, :], y_ssm[:, m, :], value(ssm_hi[:, m, :]), ALU.subtract).then_inc(mix_ready, 1)

            free(ve, merged_ready)
            n = C0["merge"]
            with ve.Fori(0, DT) as i:
                for m in range(2):
                    low(n + 1 + m, 1 + m, 2 * i)
                    t = T0["merge"] + 2 * m + 1
                    copied(ve, t - 1, i)
                    full(ve, t, 4 * i)
                    ve.wait_ge(merged_ready, i + 1)
                    out_of(t, product(prod[:, m, :], sig[:, m, :], acc[t % BANKS][:]))
                for m in range(2):
                    copied(ve, T0["merge"] + 2 * m + 1, i)
                ve.tensor_tensor(merged[:, ds(i, 1), :], prod[:, 0:1, :], prod[:, 1:2, :], ALU.add)\
                  .then_inc(merged_ready, 1)
            for c in range(DT):
                ve.wait_ge(merged_hi_ready, c + 1)
                ve.tensor_tensor(merged_lo[:, c, :], merged[:, c, :], value(merged_hi[:, c, :]), ALU.subtract)\
                  .then_inc(merged_parts, 1)
            for k in range(1, 3):
                low(C0["out1"] + k, SPLIT0["out1"] + k)

            def residual(name, rounds, gain=None, first=0):
                with ve.Fori(first, rounds) as i:
                    for k in range(4):
                        t = T0[name] + k
                        full(ve, t, 4 * i)
                        x = xT[:, ds(4 * i + k, 1), :].rearrange("p a n -> p (a n)")
                        if gain is None:
                            out_of(t, ve.tensor_tensor(x, acc[t % BANKS][:], x, ALU.add))
                        else:
                            out_of(t, ve.scalar_tensor_tensor(x, acc[t % BANKS][:], mod[:, ds(gain * DT + k + 4 * i, 1), 0],
                                                              x, ALU.mult, ALU.add))

            def residual_done(name):
                for k in range(BANKS):
                    copied(ve, T0[name] + DT - BANKS + k)
                ve.memset(tick[:, 1:2], 0.0).then_inc(x1_ready, 1)

            residual("out1", 1)
            low(C0["out1"] + 3, SPLIT0["out1"] + 3)
            residual("out1", 2, first=1)
            residual_done("out1")
            low(C0["up1_0"], SPLIT0["up1_0"])
            ve.wait_ge(rstd_ready, 2)
            for c in range(DT + 1):
                if c < DT:
                    ve.scalar_tensor_tensor(h_new[:, c, :], xT[:, c, :], vcol("norm2_g", c), rstd[:], ALU.mult, ALU.mult)\
                      .then_inc(h_new_ready, 1)
                if c:
                    ve.wait_ge(h_hi_ready, c)
                    ve.tensor_tensor(h_lo[:, c - 1, :], h_new[:, c - 1, :], value(hT_hi[:, c - 1, :]), ALU.subtract)\
                      .then_inc(h_ready, 1)
            low(C0["up1_0"] + 1, SPLIT0["up1_0"] + 1)
            free(ve, act_ready, 2)
            for h in range(2):
                n, q, t = C0[f"up1_{h}"], SPLIT0[f"up1_{h}"], T0[f"up1_{h}"]
                with ve.Fori(0, 4) as i:
                    step.enter(i, 4)
                    for k in range(4):
                        copied(ve, t + k, i)
                        step(product(relu2[:, k % 2, :], relu[:, k % 2, :], relu[:, k % 2, :]))
                        ve.wait_ge(act_hi_ready, FT // 2 * h + 4 * i + k + 1)
                        ve.tensor_tensor(act_lo[:, ds(4 * i + k, 1), :], relu2[:, k % 2, :].unsqueeze(1),
                                         value(act_hi[:, ds(4 * i + k, 1), :]), ALU.subtract).then_inc(act_ready, 1)
                        if k % 2:
                            low(n + 2 + k // 2, q + 2 + k // 2, 2 * i)
                    step.leave(4)
                n, q, t = C0[f"down1_{h}"], SPLIT0[f"down1_{h}"], T0[f"down1_{h}"]

                def round_(i, splits):
                    for m in range(2):
                        for k in range(2 * m, 2 * m + 2):
                            if k + 2 < splits:
                                low(n + 2 + k, q + 2 + k, 4 * i)
                        for k in range(2 * m, 2 * m + 2):
                            full(ve, t + k, 4 * i)
                            x = xT[:, ds(4 * i + k, 1), :]
                            out_of(t + k, ve.tensor_tensor(x, acc[(t + k) % BANKS][:].unsqueeze(1), x, ALU.add))

                if h == 0:
                    with ve.Fori(0, 2) as i:
                        round_(i, 8)
                else:
                    with ve.Fori(0, 1) as i:
                        round_(i, 8)
                    with ve.Fori(1, 2) as i:
                        round_(i, 4)
                if h == 0:
                    for k in range(BANKS):
                        copied(ve, t + DT - BANKS + k)
            residual_done("down1_1")
            logits = vec[:, VEC["hgrn_lb_logits_2"]:VEC["hgrn_lb_logits_2"] + 4 * MH]\
                .rearrange("p (d l h) -> p d l h", d=2, l=2)
            ve.tensor_tensor(lb[:, 2], logits[:, :, 1], logits[:, :, 0], ALU.subtract).then_inc(lb_logit, 1)
            ve.wait_ge(lb_sig, 2)
            ve.tensor_scalar(lb[:, 0], lb[:, 0], TINY, None, ALU.max).then_inc(lb_ready, 1)
            ve.wait_ge(mod_flipped, 1)
            b = vec[:, VEC["b_mod_2"]:VEC["b_mod_2"] + NMOD * DT].unsqueeze(2).to_broadcast([P, NMOD * DT, 2])
            ve.tensor_tensor(mod[:], mod_banks[0][:, 0:2 * NMOD * DT].rearrange("p (c m) -> p m c", c=2), b, ALU.add)\
              .then_inc(mod_ready, 1)
            ve.wait_ge(mod_ready, 1)
            for k, (name, scale, col) in enumerate((("norm1_w_2", 1, 0), ("norm1_w_2", 1, 1), ("norm2_w_2", 4, 0))):
                last = step.mark(ve.scalar_tensor_tensor(amod[:, k], mod[:, scale * DT:(scale + 1) * DT, col], 1.0,
                                                         vec[:, VEC[name]:VEC[name] + DT], ALU.add, ALU.mult))
            step.wait(last)

            def scaled(dst, src, gain, r):
                for c in range(DT):
                    ve.scalar_tensor_tensor(dst[:, c, :], src[:, c, :], amod[:, gain, c:c + 1], r, ALU.mult, ALU.mult)\
                      .then_inc(h_scaled, 1)

            ve.wait_ge(rstd_ready, 3)
            scaled(hcT, xcT, 1, root[:, 0, 0:C])
            ve.wait_ge(rstd_ready, 4)
            scaled(hT, xT, 0, rstd[:])
            f, g, b = (x[0:MH] for x in (row_f, row_g, row_b))
            ve.wait_ge(rows_in, 64)
            ve.scalar_tensor_tensor(b, f, -1.0, f, ALU.mult, ALU.min).then_inc(neg_ready, 1)
            ve.wait_ge(ln_ready, 1)
            step(ve.scalar_tensor_tensor(f, f, 0.0, b, ALU.min, ALU.subtract))

            def scan(out, x, initial, op):
                n = x.shape[-1]
                if op == ALU.add:
                    return ve.tensor_tensor_scan(out, x, zero[0:x.shape[0]].to_broadcast([x.shape[0], n]), initial,
                                                 ALU.add, ALU.add)
                return ve.tensor_tensor_scan(out, x, x, initial, op, op)

            def both_ways(out, x, op):
                step.mark(scan(out[:, 0], x[:, 0], 0.0, op))
                step(scan(out[:, 1, 0:C][:, ::-1], x[:, 1, 0:C][:, ::-1], 0.0, op))
                step(scan(out[:, 1, C:][:, ::-1], x[:, 1, C:][:, ::-1], out[:, 1, 0:1], op))

            both_ways(b, f, ALU.add)
            step(ve.tensor_tensor(g, g, b, ALU.subtract))
            both_ways(f, g, ALU.max)
            ve.tensor_tensor(b, b, f, ALU.add).then_inc(rows_ready, 1)
            ve.wait_ge(max_out, 32)
            copied(ve, T0["gate_cols"])
            step(ve.memset(sums1, 0.0))
            s1 = sums1[:, 0:2 * SEGS].rearrange("p (d a n) -> p d a n", d=2, a=ST)
            ve.wait_ge(lb_ready, 1)
            with ve.Fori(0, MH) as i:
                step.enter(i, 2 + 2 * ST + 3)
                ve.wait_ge(z_ready, i + 2)
                for d in range(2):
                    x = logf[:, d, :, 1:]
                    ve.tensor_scalar(x, x, lb[:, 1, d, ds(i, 1)], lb[:, 0, d, ds(i, 1)], ALU.mult, ALU.add).then_inc(f_ready, 1)
                for d in range(2):
                    x = hg_k[:, ds(i, 1), d, :]
                    step.mark(ve.tensor_scalar(x, x, lb[:, 1, d, ds(i, 1)], None, ALU.mult))
                ve.wait_ge(sums_kept, i + 1)
                ve.wait_ge(logf_ready, 2 * i + 2)
                for d in range(2):
                    for b in range(ST):
                        last = step.mark(scan(s1[:, d, b, 1:], logf[:, d, b, 1:], 0.0, ALU.add))
                step.wait(last)
                tot = [s1[:, d, CT:, P] for d in range(2)]
                step.mark(scan(sums1[:, PRE_F:PRE_F + TT], tot[0], 0.0, ALU.add))
                step.mark(scan(sums1[:, SUF_B:SUF_B + TT][:, ::-1], tot[1][:, ::-1], 0.0, ALU.add))
                step.mark(scan(sums1[:, PRE_B:PRE_B + 2], tot[1][:, 0:2], 0.0, ALU.add))
                scan(sums1[:, CTX_F:CTX_F + CT], s1[:, 0, 0:CT, P], 0.0, ALU.add).then_inc(sums_ready, 1)
                step.leave(MH)
            def convolve(chains, done):
                rounds = []
                for chain, (out, src, rows_, col, first) in enumerate(chains):
                    taps = [4] + [k for k in range(TAPS) if k != 4 and (rows_ > 1 or k // 3 == 1)]
                    for n, k in enumerate(taps[1 - first:]):
                        dy, dx = k // 3 - 1, k % 3 - 1
                        w = out.shape[-1] // rows_
                        o, x = (v.rearrange("p (y x) -> p y x", x=w) for v in (out, src))
                        ys, xs = slice(max(0, -dy), rows_ - max(0, dy)), slice(max(0, -dx), w - max(0, dx))
                        yt, xt = (slice(v.start + e, v.stop + e) for v, e in ((ys, dy), (xs, dx)))
                        rounds += [[]] if n >= len(rounds) else []
                        rounds[n].append((chain, o[:, ys, xs], x[:, yt, xt], col(k), k == 4, k == taps[-1]))
                before = {}
                for ops in rounds:
                    for chain, o, x, c, alone, final in ops:
                        if chain in before:
                            step.wait(before[chain])
                        if alone:
                            ins = ve.tensor_scalar(o, x, c, None, ALU.mult)
                        else:
                            ins = ve.scalar_tensor_tensor(o, x, c, o, ALU.mult, ALU.add)
                        if final:
                            ins.then_inc(done, 1)
                        else:
                            before[chain] = step.mark(ins)

            ve.wait_ge(same_ready, len(LEVELS))
            ve.wait_ge(sums_kept, MH + 1)
            step.wait(step.base + step.n)
            with ve.Fori(0, MH) as i:
                step.enter(i, 2 * (TAPS - 1) + 2)
                def k_of(d, at=C):
                    n = T if at else C
                    return hg_k[:, ds(i, 1), d, at:at + n].rearrange("p o n -> p (o n)")

                q = hg_q[:, ds(i, 1), :].rearrange("p o n -> p (o n)")

                def decayed(u):
                    k_, q_ = ek[:, u % 2, :], eq[:, u % 2, :]
                    if u == DIAG:
                        full(ve, unit_tiles(u - 2)[0], 16 * i)
                        ve.tensor_tensor(k_, k_of(0), k_of(1), ALU.add)
                        ve.tensor_scalar(q_, q, P ** -0.5, None, ALU.mult).then_inc(kq_ready, 1)
                        return
                    ve.wait_ge(exp_ready, (UNITS - 1) * i + u + (u < DIAG))
                    if u < HALVES:
                        m = LEVELS[u] if u < DIAG else P

                        def halves(x):
                            return x.rearrange("p (b t m) -> p b t m", t=2, m=m)

                        for h in range(2):
                            product(halves(k_)[:, :, h], halves(k_)[:, :, h], halves(k_of(h))[:, :, h])
                    elif u == HALVES:
                        for h in range(2):
                            half = slice(h * C, (h + 1) * C)
                            product(k_[:, half], k_[:, half], k_of(h)[:, half])
                    else:
                        for d in range(2):
                            half = slice(d * C, (d + 1) * C)
                            product(k_[:, half], k_[:, half], k_of(d, 0))
                        ve.scalar_tensor_tensor(eq_b[:], eq_b[:], P ** -0.5, q, ALU.mult, ALU.mult)
                    ve.scalar_tensor_tensor(q_, q_, P ** -0.5, q, ALU.mult, ALU.mult).then_inc(kq_ready, 1)

                def assemble(u):
                    b = unit_tiles(u)[0]
                    full(ve, b, 16 * i)
                    own = acc[b % BANKS][:].rearrange("p (s n) -> p s n", n=P)
                    if u == 0:
                        out_of(b, ve.tensor_copy(a_own, own))
                        return
                    copied(ve, unit_tiles(u - 1)[0], 4 * i)
                    ve.memset(tick[:, 0:1], 0.0)
                    mask = same[:, u - 1, :].unsqueeze(1).to_broadcast([P, TT, P])
                    out_of(b, ve.copy_predicated(a_own, mask, own))

                for u in range(UNITS):
                    decayed(u)
                    if 1 <= u <= DIAG + 1:
                        assemble(u - 1)
                def of(x):
                    return x[:, ds(i, 1), :].rearrange("p o n -> p (o n)")

                for m in range(3):
                    copied(ve, ml_tile(m), 4 * i)

                ve.wait_ge(kq_ready, UNITS * (i + 1))

                def chain(out, src, rows_, head):
                    return (out, src.rearrange("p o n -> p (o n)"), rows_,
                            lambda k: vec[:, ds(i + VEC["mlstm_conv_w_2"] + k * DT + head, 1)], 1)

                convolve([chain(of(qc), ml_q[:, ds(i, 1), :], ROWS, 0), chain(of(kc2)[:, C:], ml_k[:, ds(i, 1), C:], ROWS, MH),
                          chain(of(kc2)[:, 0:C], ml_k[:, ds(i, 1), 0:C], 1, MH)], qk_conv)
                ve.wait_ge(hg_rstd, i + 1)
                for b in range(TT):
                    ins = ve.tensor_scalar(y_tok[:, b, :], banks[4][:, b * P:(b + 1) * P], stat2[:, 2, b:b + 1], None, ALU.mult)
                ins.then_inc(hg_y, 1)
                ve.wait_ge(hg_flipped, i + 1)
                g = hg_g[:, ds(i, 1), :]
                ve.scalar_tensor_tensor(g, banks[6][:].unsqueeze(1), vec[:, ds(i + VEC["hgrn_norm_w_2"], 1)], g,
                                        ALU.mult, ALU.mult).then_inc(hg_done, 1)
                step.leave(MH)

            free(ve, gap_ready, 2 * ST)
            ve.wait_ge(hg_done, MH)
            ve.wait_ge(cols_ready, 1)
            copied(ve, T0["gate_cols"])
            with ve.Fori(0, MH) as i:
                step.enter(i, 2 * TT + 3)
                t = T0["ml"]
                ve.wait_ge(max_in, 32 * (i + 1))
                for n in range(2 * ST):
                    s, d = divmod(n, 2)
                    x = targets(cummax.unsqueeze(2).to_broadcast([P, 2, ST, T]), d, s)
                    ve.tensor_scalar(targets(weight, d, s), x, gcol[:, d, s, ds(i, 1)], 0.0, ALU.subtract, ALU.max)\
                      .then_inc(gap_ready, 1)
                for n in range(2 * ST):
                    s, d = divmod(n, 2)
                    w, b = targets(weight, d, s), t + s
                    full(ve, b, 8 * i)
                    ve.wait_ge(w_ready, 2 * ST * i + n + 1)
                    x = acc[b % BANKS][:].unsqueeze(1).unsqueeze(1).to_broadcast([P, 2, ST, T])
                    ins = ve.scalar_tensor_tensor(w, targets(x, d, s), P ** -0.5, w, ALU.mult, ALU.mult)
                    if d:
                        out_of(b, ins)
                    else:
                        ins.then_inc(p_ready, 1)
                den = stat2[:, 3].rearrange("p (d b) -> p d b", d=2)
                for b in range(TT):
                    ve.wait_ge(ml_o, TT * i + b + 1)
                    x = banks[4 + b][:, P:2 * P + 2:P + 1]
                    last = step.mark(ve.tensor_copy(den[:, :, b], x))
                step.wait(last)
                step(ve.scalar_tensor_tensor(den, den, -1.0, den, ALU.mult, ALU.max))
                step(ve.tensor_tensor(den, den, floor[:, :, :, ds(i, 1)].rearrange("p d b o -> p d (b o)"), ALU.max))
                step(ve.reciprocal(stat2[:, 3], stat2[:, 3]))
                for b in range(TT):
                    last = step.mark(ve.tensor_scalar(h_tok[:, b, :], banks[4 + b][:, 0:P], den[:, 0, b:b + 1], None, ALU.mult))
                step.wait(last)
                for b in range(TT):
                    ve.scalar_tensor_tensor(h_tok[:, b, :], banks[4 + b][:, P + 1:2 * P + 1], den[:, 1, b:b + 1],
                                            h_tok[:, b, :], ALU.mult, ALU.add).then_inc(ml_h, 1)
                ve.wait_ge(ml_rstd, i + 1)
                for b in range(TT):
                    ins = ve.tensor_scalar(h_tok[:, b, :], h_tok[:, b, :], stat2[:, 2, TT + b:TT + b + 1], None, ALU.mult)
                ins.then_inc(ml_y, 1)
                full(ve, t + 7, 8 * i)
                copied(ve, t + 6, 2 * i)
                out_of(t + 7, ve.scalar_tensor_tensor(ml_q[:, ds(i, 1), :], acc[(t + 7) % BANKS][:].unsqueeze(1),
                                                      vec[:, ds(i + VEC["mlstm_norm_w_2"], 1)], o_sig.unsqueeze(1),
                                                      ALU.mult, ALU.mult))
                step.leave(MH)
            residual("out2", 2, 2)
            residual_done("out2")
            free(ve, chunk_used)
            ve.wait_ge(rstd_ready, 5)
            for c in range(DT + 2):
                if c < DT:
                    ve.scalar_tensor_tensor(h_new[:, c, :], xT[:, c, :], amod[:, 2, c:c + 1], rstd[:], ALU.mult, ALU.mult)\
                      .then_inc(h_scaled, 1)
                if c >= 2:
                    ve.wait_ge(h_hi_ready, DT + c - 1)
                    ve.tensor_tensor(h_lo[:, c - 2, :], h_new[:, c - 2, :], value(hT_hi[:, c - 2, :]), ALU.subtract)\
                      .then_inc(h_ready, 1)
            free(ve, conv_ready, 4)
            for h, width2 in enumerate(F2_HALF):
                t = T0[f"up2_{h}"]
                with ve.Fori(0, width2 // 2) as i:
                    step.enter(i, 4 * (TAPS - 2))
                    for j in range(2):
                        for m in range(2):
                            copied(ve, t + 2 * j + m, i)
                        at = [m * F2T + h * F2_HALF[0] + j for m in range(2)]
                        convolve([(conv[:, 2 * j + m], raw[:, 2 * j + m], ROWS,
                                   lambda k, m=m: ffn_taps[:, ds(i * 2 + k * 2 * F2T + at[m], 1)], 0) for m in range(2)],
                                 conv_ready)
                    step.leave(width2 // 2)
                residual(f"down2_{h}", 2, 5)
                if h == 0:
                    for k in range(BANKS):
                        copied(ve, T0["down2_0"] + DT - BANKS + k)
            residual_done("down2_1")
            ve.wait_ge(rstd_ready, 6)
            for c in range(DT):
                ve.scalar_tensor_tensor(hT[:, c, :], xT[:, c, :], vcol("final_norm_w_2", c), rstd[:], ALU.mult, ALU.mult)\
                  .then_inc(out_ready, 1)


_INS = ['x', 'norm1_g', 'w_in', 'ssm_a_re', 'ssm_a_im', 'ssm_log_dt', 'ssm_b_re', 'ssm_b_im', 'ssm_c_re', 'ssm_c_im',
        'ssm_d', 'ssm_w_glu', 'ssm_b_glu', 'cmp_pe_k', 'cmp_pe_v', 'cmp_wk1', 'cmp_wk2', 'cmp_wv1', 'cmp_wv2',
        'q_norm_g', 'k_norm_g', 'w_proj_ssm', 'w_proj_nsa', 'w_out', 'norm2_g', 'w_up', 'w_down', 'c_2', 'ctx_2',
        'c_ctx_2', 'w_mod_2', 'b_mod_2', 'norm1_w_2', 'w_in_2', 'mlstm_gate_b_2', 'mlstm_conv_w_2',
        'mlstm_norm_w_2', 'hgrn_lb_logits_2', 'hgrn_norm_w_2', 'w_out_2', 'norm2_w_2', 'w_up_2', 'ffn_conv_w_2',
        'w_down_2', 'final_norm_w_2']


def kernel(**inputs):
    import numpy as _np
    import concourse.bacc as _bacc
    from concourse import mybir as _mybir
    from concourse.bass_utils import run_bass_kernel_spmd as _run

    nc = _bacc.Bacc("TRN2", target_bir_lowering=False, num_devices=1)
    arrays, args = {}, {}
    for name in _INS:
        arr = _np.ascontiguousarray(inputs[name])
        arrays["in_" + name] = arr
        args[name] = nc.dram_tensor("in_" + name, arr.shape, _mybir.dt.from_np(arr.dtype), kind="ExternalInput").ap()
    out = nc.dram_tensor("out_x", (1, T, D), _mybir.dt.float32, kind="ExternalOutput").ap()
    two_block_program(nc, args, out)
    r = _run(nc, [arrays], core_ids=[0])
    return r.results[0]["out_x"]
```
